# Optimizing a Trainium2 kernel written in Bass

```python
import jax, jax.numpy as jnp
from jax import lax
import numpy as np
import math

D_MODEL = 1024
BATCH = 1
SEQ = 256
DEPTH = 1

CHUNK = 64
HEAD_DIM = 64
N_HEADS_A = 8
N_HEADS_B = 8
D_A = N_HEADS_A * HEAD_DIM
D_B = N_HEADS_B * HEAD_DIM
D_MIX = D_A + D_B
N_LEFT_CHUNKS = 8
BAND_CHUNKS = N_LEFT_CHUNKS + 1
REL_CLIP = 128
Q_BLOCK = 128
D_FF = 2816
CONV_WIDTH = 3
LN_EPS = 1e-5
DEEPNORM_ALPHA = (2.0 * DEPTH) ** 0.25
DEEPNORM_BETA = (8.0 * DEPTH) ** -0.25
PROJ_COLS = 3 * D_A + N_HEADS_A + 3 * D_B
SPLITS = (D_A, 2 * D_A, 3 * D_A, 3 * D_A + N_HEADS_A,
          3 * D_A + N_HEADS_A + D_B, 3 * D_A + N_HEADS_A + 2 * D_B)


def layer_norm(x, g, b):
    xf = x.astype(jnp.float32)
    mu = jnp.mean(xf, axis=-1, keepdims=True)
    var = jnp.mean(jnp.square(xf - mu), axis=-1, keepdims=True)
    y = (xf - mu) * lax.rsqrt(var + LN_EPS)
    return (y * g.astype(jnp.float32) + b.astype(jnp.float32)).astype(x.dtype)

def split_heads(t, n_heads):
    b, s, _ = t.shape
    return t.reshape(b, s, n_heads, HEAD_DIM).transpose(0, 2, 1, 3)

def forgetting_attention(q, k, v, log_f):
    b, h, s, d = q.shape
    n_blk = s // Q_BLOCK
    cum = jnp.cumsum(log_f.astype(jnp.float32), axis=-1)
    q_blocks = q.reshape(b, h, n_blk, Q_BLOCK, d).transpose(2, 0, 1, 3, 4)
    c_blocks = cum.reshape(b, h, n_blk, Q_BLOCK).transpose(2, 0, 1, 3)
    starts = jnp.arange(n_blk, dtype=jnp.int32) * Q_BLOCK
    k_pos = jnp.arange(s, dtype=jnp.int32)
    scale = d ** -0.5

    def one_block(args):
        qb, cb, start = args
        logits = jnp.einsum('bhqd,bhkd->bhqk', qb, k).astype(jnp.float32) * scale
        logits = logits + cb[..., :, None] - cum[..., None, :]
        q_pos = start + jnp.arange(Q_BLOCK, dtype=jnp.int32)
        causal = k_pos[None, :] <= q_pos[:, None]
        logits = jnp.where(causal, logits, -jnp.inf)
        p = jax.nn.softmax(logits, axis=-1)
        return jnp.einsum('bhqk,bhkd->bhqd', p.astype(v.dtype), v)

    out = lax.map(one_block, (q_blocks, c_blocks, starts))
    return out.transpose(1, 2, 0, 3, 4).reshape(b, h, s, d)

def chunked_band_attention(q, k, v, rel_bias):
    b, h, s, d = q.shape
    n_c = s // CHUNK
    band = BAND_CHUNKS * CHUNK
    qc = q.reshape(b, h, n_c, CHUNK, d)
    pad = ((0, 0), (0, 0), (N_LEFT_CHUNKS, 0), (0, 0), (0, 0))
    kp = jnp.pad(k.reshape(b, h, n_c, CHUNK, d), pad)
    vp = jnp.pad(v.reshape(b, h, n_c, CHUNK, d), pad)
    band_idx = np.arange(n_c)[:, None] + np.arange(BAND_CHUNKS)[None, :]
    k_band = kp[:, :, band_idx].reshape(b, h, n_c, band, d)
    v_band = vp[:, :, band_idx].reshape(b, h, n_c, band, d)
    dist = (N_LEFT_CHUNKS * CHUNK + np.arange(CHUNK)[:, None]) - np.arange(band)[None, :]
    rel_idx = np.clip(dist, -REL_CLIP, REL_CLIP) + REL_CLIP
    bias = rel_bias.astype(jnp.float32)[:, rel_idx]
    valid = (np.arange(n_c)[:, None] + np.arange(band)[None, :] // CHUNK) >= N_LEFT_CHUNKS
    logits = jnp.einsum('bhcqd,bhckd->bhcqk', qc, k_band).astype(jnp.float32) * (d ** -0.5)
    logits = logits + bias[None, :, None, :, :]
    logits = jnp.where(valid[None, None, :, None, :], logits, -jnp.inf)
    p = jax.nn.softmax(logits, axis=-1)
    out = jnp.einsum('bhcqk,bhckd->bhcqd', p.astype(v.dtype), v_band)
    return out.reshape(b, h, s, d)

def token_mixer(x, w_in, b_forget, rel_bias, w_out):
    b, s, _ = x.shape
    proj = x @ w_in
    q_a, k_a, v_a, f_a, q_b, k_b, v_b = jnp.split(proj, SPLITS, axis=-1)
    log_f = jax.nn.log_sigmoid((f_a + b_forget).astype(jnp.float32)).transpose(0, 2, 1)
    y_a = forgetting_attention(split_heads(q_a, N_HEADS_A), split_heads(k_a, N_HEADS_A),
                               split_heads(v_a, N_HEADS_A), log_f)
    y_b = chunked_band_attention(split_heads(q_b, N_HEADS_B), split_heads(k_b, N_HEADS_B),
                                 split_heads(v_b, N_HEADS_B), rel_bias)
    y = jnp.concatenate([y_a, y_b], axis=1)
    y = y.transpose(0, 2, 1, 3).reshape(b, s, D_MIX)
    return y @ w_out

def conv_ffn(x, w_up, conv_w, conv_b, w_down):
    s = x.shape[1]
    u = x @ w_up
    u_pad = jnp.pad(u, ((0, 0), (CONV_WIDTH - 1, 0), (0, 0)))
    u = sum(u_pad[:, j:j + s, :] * conv_w[j] for j in range(CONV_WIDTH)) + conv_b
    value, gate = jnp.split(u, 2, axis=-1)
    return (value * jax.nn.gelu(gate)) @ w_down

def first_inputs(seed: int = 0) -> dict:
    key = jax.random.key(seed)
    ks = jax.random.split(key, 16)
    f32 = jnp.float32
    x = jax.random.normal(ks[0], (BATCH, SEQ, D_MODEL), f32)
    col_scale = np.ones((PROJ_COLS,), np.float32)
    col_scale[2 * D_A:3 * D_A] = DEEPNORM_BETA
    col_scale[SPLITS[5]:] = DEEPNORM_BETA
    w_in = jax.random.normal(ks[1], (DEPTH, D_MODEL, PROJ_COLS), f32) * (D_MODEL ** -0.5) * jnp.asarray(col_scale)
    b_forget = jax.random.uniform(ks[2], (DEPTH, N_HEADS_A), f32, 2.0, 5.0)
    rel_bias = jax.random.normal(ks[3], (DEPTH, N_HEADS_B, 2 * REL_CLIP + 1), f32) * 0.5
    w_out = jax.random.normal(ks[4], (DEPTH, D_MIX, D_MODEL), f32) * (D_MIX ** -0.5) * DEEPNORM_BETA
    ln1_g = 1.0 + 0.05 * jax.random.normal(ks[5], (DEPTH, D_MODEL), f32)
    ln1_b = 0.02 * jax.random.normal(ks[6], (DEPTH, D_MODEL), f32)
    w_up = jax.random.normal(ks[7], (DEPTH, D_MODEL, 2 * D_FF), f32) * (D_MODEL ** -0.5)
    conv_w = jax.random.normal(ks[8], (DEPTH, CONV_WIDTH, 2 * D_FF), f32) * (CONV_WIDTH ** -0.5)
    conv_b = 0.02 * jax.random.normal(ks[9], (DEPTH, 2 * D_FF), f32)
    w_down = jax.random.normal(ks[10], (DEPTH, D_FF, D_MODEL), f32) * (D_FF ** -0.5) * DEEPNORM_BETA
    ln2_g = 1.0 + 0.05 * jax.random.normal(ks[11], (DEPTH, D_MODEL), f32)
    ln2_b = 0.02 * jax.random.normal(ks[12], (DEPTH, D_MODEL), f32)
    return {"x": x, "w_in": w_in, "b_forget": b_forget, "rel_bias": rel_bias, "w_out": w_out,
            "ln1_g": ln1_g, "ln1_b": ln1_b, "w_up": w_up, "conv_w": conv_w, "conv_b": conv_b,
            "w_down": w_down, "ln2_g": ln2_g, "ln2_b": ln2_b}

def first_block(x, w_in, b_forget, rel_bias, w_out, ln1_g, ln1_b, w_up, conv_w, conv_b,
              w_down, ln2_g, ln2_b):
    for l in range(DEPTH):
        mix = token_mixer(x, w_in[l], b_forget[l], rel_bias[l], w_out[l])
        x = layer_norm(DEEPNORM_ALPHA * x + mix, ln1_g[l], ln1_b[l])
        ffn = conv_ffn(x, w_up[l], conv_w[l], conv_b[l], w_down[l])
        x = layer_norm(DEEPNORM_ALPHA * x + ffn, ln2_g[l], ln2_b[l])
    return x


DEPTH_2 = 2

RET_HEADS = 4
RET_DK = 256
RET_DV = 512
RET_CHUNK = 128
MLA_HEADS = 8
MLA_NOPE = 128
MLA_ROPE = 64
MLA_V = 128
MLA_Q_RANK = 256
MLA_KV_RANK = 256
ATTN_Q_BLOCK = 128
MOBA_HEADS = 16
MOBA_DH = D_MODEL // MOBA_HEADS
MOBA_BLOCK = 256
MOBA_TOPK = 3
MOBA_Q_CHUNK = 32

ROPE_THETA = 10000.0
RMS_EPS = 1e-6
NEG = -1e30
DN_ALPHA = (2.0 * DEPTH_2) ** 0.25
DN_BETA = (8.0 * DEPTH_2) ** -0.25
N_EVEN = (DEPTH_2 + 1) // 2
N_ODD = DEPTH_2 // 2

RET_W = RET_HEADS * RET_DV
MLA_W = MLA_HEADS * MLA_V
MOBA_W = MOBA_HEADS * MOBA_DH
EVEN_SPLITS = (RET_HEADS * RET_DK, RET_HEADS * RET_DK, RET_W, RET_W,
               MLA_Q_RANK, MLA_KV_RANK, MLA_ROPE, MLA_W)
EVEN_IN = sum(EVEN_SPLITS)
ODD_SPLITS = (MOBA_W, MOBA_W, MOBA_W, MOBA_W)
ODD_IN = sum(ODD_SPLITS)


def _split(h, sizes):
    offs = np.cumsum(sizes)[:-1].tolist()
    return jnp.split(h, offs, axis=-1)

def _heads(t, n):
    B, S, W = t.shape
    return t.reshape(B, S, n, W // n).transpose(0, 2, 1, 3)

def _merge(t):
    B, H, S, d = t.shape
    return t.transpose(0, 2, 1, 3).reshape(B, S, H * d)

def layer_norm_2(x, g, b):
    xf = x.astype(jnp.float32)
    mu = jnp.mean(xf, -1, keepdims=True)
    xc = xf - mu
    var = jnp.mean(xc * xc, -1, keepdims=True)
    return (xc * lax.rsqrt(var + LN_EPS) * g + b).astype(x.dtype)

def rms_norm(x, g):
    xf = x.astype(jnp.float32)
    return (xf * lax.rsqrt(jnp.mean(xf * xf, -1, keepdims=True) + RMS_EPS) * g).astype(x.dtype)

def rope(x, pos):
    d = x.shape[-1]
    inv = 1.0 / (ROPE_THETA ** (jnp.arange(0, d, 2, dtype=jnp.float32) / d))
    ang = pos.astype(jnp.float32)[:, None, :, None] * inv
    cos, sin = jnp.cos(ang), jnp.sin(ang)
    x1, x2 = x[..., : d // 2], x[..., d // 2:]
    return jnp.concatenate([x1 * cos - x2 * sin, x1 * sin + x2 * cos], -1).astype(x.dtype)

def retnet_rotate(x, pos):
    d = x.shape[-1]
    inv = 1.0 / (ROPE_THETA ** jnp.linspace(0.0, 1.0, d // 2, dtype=jnp.float32))
    ang = pos.astype(jnp.float32)[:, None, :, None] * inv
    cos, sin = jnp.cos(ang), jnp.sin(ang)
    x1, x2 = x[..., 0::2], x[..., 1::2]
    out = jnp.stack([x1 * cos - x2 * sin, x2 * cos + x1 * sin], -1)
    return out.reshape(x.shape).astype(x.dtype)

def retention_chunkwise(q, k, v):
    B, H, S, dk = q.shape
    dv = v.shape[-1]
    C = RET_CHUNK
    n = S // C
    q = q.astype(jnp.float32)
    k = k.astype(jnp.float32) * (dk ** -0.5)
    v = v.astype(jnp.float32)
    log_g = jnp.log(1.0 - 2.0 ** (-5.0 - jnp.arange(H, dtype=jnp.float32)))
    qc = q.reshape(B, H, n, C, dk)
    kc = k.reshape(B, H, n, C, dk)
    vc = v.reshape(B, H, n, C, dv)
    idx = jnp.arange(C, dtype=jnp.float32)
    rel = idx[:, None] - idx[None, :]
    decay = jnp.where(rel >= 0, jnp.exp(log_g[:, None, None] * jnp.maximum(rel, 0.0)), 0.0)
    inner = jnp.einsum('bhncd,bhnkd->bhnck', qc, kc) * decay[None, :, None]
    o_inner = jnp.einsum('bhnck,bhnkv->bhncv', inner, vc)
    zeta = jnp.exp(log_g[:, None] * (C - 1.0 - idx))
    kv_chunk = jnp.einsum('bhnkd,bhnkv->bhndv', kc * zeta[None, :, None, :, None], vc)
    g_chunk = jnp.exp(log_g * C)[None, :, None, None]

    def step(R, kv):
        return R * g_chunk + kv, R

    _, r_prev = lax.scan(step, jnp.zeros((B, H, dk, dv), jnp.float32), jnp.moveaxis(kv_chunk, 2, 0))
    r_prev = jnp.moveaxis(r_prev, 0, 2)
    xi = jnp.exp(log_g[:, None] * (idx + 1.0))
    o_cross = jnp.einsum('bhncd,bhndv->bhncv', qc, r_prev) * xi[None, :, None, :, None]
    return (o_inner + o_cross).reshape(B, H, S, dv)

def head_group_norm(o):
    of = o.astype(jnp.float32)
    mu = jnp.mean(of, -1, keepdims=True)
    oc = of - mu
    var = jnp.mean(oc * oc, -1, keepdims=True)
    return oc * lax.rsqrt(var + LN_EPS)

def causal_attention(q, k, v, scale):
    B, H, S, d = q.shape
    dv = v.shape[-1]
    nq = S // ATTN_Q_BLOCK
    qb = q.reshape(B, H, nq, ATTN_Q_BLOCK, d).transpose(2, 0, 1, 3, 4)
    kpos = jnp.arange(S)

    def one(args):
        qi, i = args
        s = jnp.einsum('bhqd,bhkd->bhqk', qi, k).astype(jnp.float32) * scale
        qpos = i * ATTN_Q_BLOCK + jnp.arange(ATTN_Q_BLOCK)
        s = jnp.where(kpos[None, :] <= qpos[:, None], s, NEG)
        p = jax.nn.softmax(s, axis=-1).astype(v.dtype)
        return jnp.einsum('bhqk,bhkd->bhqd', p, v)

    out = lax.map(one, (qb, jnp.arange(nq)))
    return out.transpose(1, 2, 0, 3, 4).reshape(B, H, S, dv)

def moba_attention(q, k, v):
    B, H, S, dh = q.shape
    L = MOBA_BLOCK
    nb = -(-S // L)
    pad = nb * L - S
    kp = jnp.pad(k, ((0, 0), (0, 0), (0, pad), (0, 0)))
    vp = jnp.pad(v, ((0, 0), (0, 0), (0, pad), (0, 0)))
    kb = kp.reshape(B, H, nb, L, dh)
    vb = vp.reshape(B, H, nb, L, dh)
    kmean = jnp.mean(kb.astype(jnp.float32), axis=3)
    qblk = jnp.arange(S) // L
    gate = jnp.einsum('bhsd,bhnd->bhsn', q.astype(jnp.float32), kmean)
    past = jnp.arange(nb)[None, :] < qblk[:, None]
    gate = jnp.where(past, gate, NEG)
    k_sel = min(MOBA_TOPK, nb)
    _, sel = lax.top_k(gate, k_sel)
    valid = jnp.arange(k_sel)[None, :] < qblk[:, None]
    scale = dh ** -0.5
    Qc = MOBA_Q_CHUNK
    nc = S // Qc
    qch = jnp.moveaxis(q.reshape(B, H, nc, Qc, dh), 2, 0)
    selch = jnp.moveaxis(sel.reshape(B, H, nc, Qc, k_sel), 2, 0)
    validch = valid.reshape(nc, Qc, k_sel)
    bi = jnp.arange(B)[:, None, None, None]
    hi = jnp.arange(H)[None, :, None, None]

    def one(args):
        qi, si, vi, c = args
        q0 = c * Qc
        qpos = q0 + jnp.arange(Qc)
        own = q0 // L
        kg = kb[bi, hi, si]
        vg = vb[bi, hi, si]
        s_g = jnp.einsum('bhqd,bhqnld->bhqnl', qi, kg).astype(jnp.float32) * scale
        s_g = jnp.where(vi[None, None, :, :, None], s_g, NEG)
        ko = lax.dynamic_slice_in_dim(kp, own * L, L, axis=2)
        vo = lax.dynamic_slice_in_dim(vp, own * L, L, axis=2)
        s_o = jnp.einsum('bhqd,bhld->bhql', qi, ko).astype(jnp.float32) * scale
        kpos = own * L + jnp.arange(L)
        s_o = jnp.where(kpos[None, :] <= qpos[:, None], s_o, NEG)
        s = jnp.concatenate([s_g.reshape(B, H, Qc, k_sel * L), s_o], axis=-1)
        p = jax.nn.softmax(s, axis=-1).astype(v.dtype)
        p_g = p[..., : k_sel * L].reshape(B, H, Qc, k_sel, L)
        p_o = p[..., k_sel * L:]
        return (jnp.einsum('bhqnl,bhqnld->bhqd', p_g, vg)
                + jnp.einsum('bhql,bhld->bhqd', p_o, vo))

    out = lax.map(one, (qch, selch, validch, jnp.arange(nc)))
    return jnp.moveaxis(out, 0, 2).reshape(B, H, S, dh)

def retention_mla_layer(x, pos, w_in, q_norm_g, w_uq, kv_norm_g, w_ukv, w_out):
    B, S, _ = x.shape
    h = x @ w_in
    rq, rk, rv, rg, mq, mkv, mkr, mg = _split(h, EVEN_SPLITS)
    q_r = retnet_rotate(_heads(rq, RET_HEADS), pos)
    k_r = retnet_rotate(_heads(rk, RET_HEADS), pos)
    o_r = head_group_norm(retention_chunkwise(q_r, k_r, _heads(rv, RET_HEADS)))
    ret_out = (_merge(o_r) * jax.nn.silu(rg.astype(jnp.float32))).astype(x.dtype)
    q_m = (rms_norm(mq, q_norm_g) @ w_uq).reshape(B, S, MLA_HEADS, MLA_NOPE + MLA_ROPE).transpose(0, 2, 1, 3)
    q_nope, q_pe = q_m[..., :MLA_NOPE], rope(q_m[..., MLA_NOPE:], pos)
    kv = (rms_norm(mkv, kv_norm_g) @ w_ukv).reshape(B, S, MLA_HEADS, MLA_NOPE + MLA_V).transpose(0, 2, 1, 3)
    k_nope, v_m = kv[..., :MLA_NOPE], kv[..., MLA_NOPE:]
    k_pe = rope(mkr[:, None], pos)
    q_full = jnp.concatenate([q_nope, q_pe], -1)
    k_full = jnp.concatenate([k_nope, jnp.broadcast_to(k_pe, (B, MLA_HEADS, S, MLA_ROPE))], -1)
    o_m = causal_attention(q_full, k_full, v_m, (MLA_NOPE + MLA_ROPE) ** -0.5)
    mla_out = (_merge(o_m) * jax.nn.silu(mg)).astype(x.dtype)
    return jnp.concatenate([ret_out, mla_out], axis=-1) @ w_out

def moba_layer(x, pos, w_in, w_out):
    h = x @ w_in
    q, k, v, g = _split(h, ODD_SPLITS)
    q = rope(_heads(q, MOBA_HEADS), pos)
    k = rope(_heads(k, MOBA_HEADS), pos)
    o = moba_attention(q, k, _heads(v, MOBA_HEADS))
    return (_merge(o) * jax.nn.silu(g)) @ w_out

def second_inputs(seed: int = 0) -> dict:
    key = jax.random.key(seed)
    ks = jax.random.split(key, 16)
    f32 = jnp.float32
    nrm = lambda k, shape, fan_in, gain=1.0: jax.random.normal(k, shape, f32) * (gain * fan_in ** -0.5)
    x = jax.random.normal(ks[0], (BATCH, SEQ, D_MODEL), f32)
    offs = jax.random.randint(ks[1], (BATCH, 1), 0, 1024, dtype=jnp.int32)
    positions = (offs + jnp.arange(SEQ, dtype=jnp.int32)[None, :]).astype(jnp.int32)
    return {
        "x": x,
        "positions": positions,
        "w_in_even": nrm(ks[2], (N_EVEN, D_MODEL, EVEN_IN), D_MODEL),
        "q_norm_even": 1.0 + 0.02 * jax.random.normal(ks[3], (N_EVEN, MLA_Q_RANK), f32),
        "w_uq_even": nrm(ks[4], (N_EVEN, MLA_Q_RANK, MLA_HEADS * (MLA_NOPE + MLA_ROPE)), MLA_Q_RANK),
        "kv_norm_even": 1.0 + 0.02 * jax.random.normal(ks[5], (N_EVEN, MLA_KV_RANK), f32),
        "w_ukv_even": nrm(ks[6], (N_EVEN, MLA_KV_RANK, MLA_HEADS * (MLA_NOPE + MLA_V)), MLA_KV_RANK),
        "w_out_even": nrm(ks[7], (N_EVEN, RET_W + MLA_W, D_MODEL), RET_W + MLA_W, DN_BETA),
        "w_in_odd": nrm(ks[8], (N_ODD, D_MODEL, ODD_IN), D_MODEL),
        "w_out_odd": nrm(ks[9], (N_ODD, MOBA_W, D_MODEL), MOBA_W, DN_BETA),
        "ln_g": 1.0 + 0.02 * jax.random.normal(ks[10], (DEPTH_2, D_MODEL), f32),
        "ln_b": 0.02 * jax.random.normal(ks[11], (DEPTH_2, D_MODEL), f32),
    }

def second_block(x, positions, w_in_even, q_norm_even, w_uq_even, kv_norm_even, w_ukv_even,
              w_out_even, w_in_odd, w_out_odd, ln_g, ln_b):
    for i in range(DEPTH_2):
        j = i // 2
        if i % 2 == 0:
            y = retention_mla_layer(x, positions, w_in_even[j], q_norm_even[j], w_uq_even[j],
                                    kv_norm_even[j], w_ukv_even[j], w_out_even[j])
        else:
            y = moba_layer(x, positions, w_in_odd[j], w_out_odd[j])
        x = layer_norm_2(DN_ALPHA * x + y, ln_g[i], ln_b[i])
    return x


def setup_inputs(seed=0):
    out = dict(first_inputs(seed))
    for name, value in second_inputs(seed + 1).items():
        if name != "x":
            out[name + "_2"] = value
    return out


def reference(
    x, w_in, b_forget, rel_bias, w_out, ln1_g, ln1_b, w_up, conv_w, conv_b, w_down, ln2_g,
    ln2_b, positions_2, w_in_even_2, q_norm_even_2, w_uq_even_2, kv_norm_even_2, w_ukv_even_2,
    w_out_even_2, w_in_odd_2, w_out_odd_2, ln_g_2, ln_b_2,
):
    x = first_block(
        x, w_in, b_forget, rel_bias, w_out, ln1_g, ln1_b, w_up, conv_w, conv_b, w_down, ln2_g,
        ln2_b,
    )
    return second_block(
        x, positions_2, w_in_even_2, q_norm_even_2, w_uq_even_2, kv_norm_even_2, w_ukv_even_2,
        w_out_even_2, w_in_odd_2, w_out_odd_2, ln_g_2, ln_b_2,
    )


_drawn_inputs = setup_inputs


def setup_inputs(seed=0):
    import zlib

    import numpy as np

    out = dict(_drawn_inputs(seed))
    spreads = {}
    factors = {'rel_bias': 3.554,
     'conv_b': 6.068,
     'ln2_b': 2.72,
     'q_norm_even_2': 8.0,
     'w_uq_even_2': 2.99,
     'kv_norm_even_2': 8.0}
    for name, (base, spread) in spreads.items():
        noise = np.random.default_rng([zlib.crc32(name.encode()), seed]).standard_normal(out[name].shape)
        drawn = base * np.exp(spread * noise) if base else spread * noise
        out[name] = __import__('jax').numpy.asarray(drawn.astype(out[name].dtype))
    for name, factor in factors.items():
        out[name] = (out[name] * factor).astype(out[name].dtype)
    return out
```

```python
from contextlib import ExitStack

import numpy as np

import concourse.bass as bass
from concourse import mybir

ALU = mybir.AluOpType
ACT = mybir.ActivationFunctionType
AX_X = mybir.AxisListType.X
F32 = mybir.dt.float32
F32R = mybir.dt.float32r
I32 = mybir.dt.int32

P = 128
S = 256
NT = S // P
D = 1024
KT = D // P
DFF = 2816
FT = DFF // P
UNIT = 2048
RING = 3
RAW = 2
NEG = -1e30
LN_EPS = 1e-5
RMS_EPS = 1e-6
ALPHA1 = 2.0 ** 0.25
ALPHA2 = 4.0 ** 0.25
HD = 64
SCALE_64 = HD ** -0.5
SCALE_MLA = 192 ** -0.5
MAGIC = 12582912.0
TWO_PI = 6.283185307179586
PI_HALF = 1.5707963267948966
PI_SAFE = 3.1415925
C1 = 6.28125
C2 = float(np.float32(0.0019350051879882812))
C3 = TWO_PI - C1 - C2

QA, KA, VA, FA, QB, KB, VB = 0, 512, 1024, 1536, 1544, 2056, 2568
RQ, RK, RV, RG, MQ, MKV, MKR, MG = 0, 1024, 2048, 4096, 6144, 6400, 6656, 6720


def chunks():
    out = []

    def add(name, kind, n_units, src, tiles, who, evac, pick, **kw):
        out.append(dict(name=name, kind=kind, n=n_units, src=src, tiles=tiles, who=who, evac=evac, pick=pick, **kw))

    k8 = list(range(KT))

    def cols(c0, n):
        return list(range(c0, c0 + n))

    def feat(name, c0, s, half):
        add(f"{name}{half}", "F", 1, "X", k8, "act", ("copy_feat", name[0], s, half),
            ("w_in", None, cols(c0 + 256 * half, 256)))

    feat("kA", KA, 0, 0)
    feat("qA", QA, 0, 0)
    add("f", "small", 0, "X", k8, "dve", ("forget",), None)
    add("vA", "A", 2, "X", k8, "act", ("copy_tok", 0), ("w_in", None, cols(VA, 512)))
    feat("kA", KA, 0, 1)
    feat("qA", QA, 0, 1)
    feat("kB", KB, 1, 0)
    feat("qB", QB, 1, 0)
    add("vB", "A", 2, "X", k8, "act", ("copy_tok", 1), ("w_in", None, cols(VB, 512)))
    feat("kB", KB, 1, 1)
    feat("qB", QB, 1, 1)
    add("out1", "B", 4, "S", k8, "dve", ("norm", 0), ("w_out", k8, None))
    for j in range(FT):
        add(f"up{j}", "F", 1, "X", k8, "dve", ("conv", j),
            ("w_up", None, cols(P * j, P) + cols(DFF + P * j, P)))
    add("down", "B", FT // 2, "S", list(range(FT)), "dve", ("norm", 1), ("w_down", list(range(FT)), None))

    even_perm = list(range(0, 256, 2)) + list(range(1, 256, 2))
    add("mqkv", "A", 2, "X", k8, "dve", ("rms",), ("w_in_even", None, cols(MQ, 512)))

    def mla(half):
        add(f"mg{half}", "A", 2, "X", k8, "dve", ("gate", 0), ("w_in_even", None, cols(MG + 512 * half, 512)),
            after_job=16 + 4 * half)
        if half == 0:
            add("mkr", "small", 0, "X", k8, "dve", ("rope_kpe",), None)
        heads = range(4 * half, 4 * half + 4)
        add(f"mlaq{half}", "Q1", 1, "S", [20, 21], "dve", ("mla_q", half),
            ("w_uq_even", [0, 1], [c for h in heads for c in cols(192 * h, 128)]
             + [c for h in heads for c in cols(192 * h + 128, 64)]), after_job=16 + 4 * half)
        add(f"mlakv{half}", "Q2", 1, "S", [22, 23], "act", ("mla_kv", half),
            ("w_ukv_even", [0, 1], [c for h in heads for c in cols(256 * h, 128)]
             + [c for h in heads for c in cols(256 * h + 128, 128)]), after_job=16 + 4 * half)

    def ret_qk(pair):
        for name, c0 in (("k", RK), ("q", RQ)):
            add(f"r{name}{pair}", "A", 2, "X", k8, "dve", ("rope", name, 1 - pair, 256),
                ("w_in_even", None, [c0 + 256 * h + c for h in (2 * pair, 2 * pair + 1) for c in even_perm]),
                after_job=24 * pair)

    def ret_vg(r):
        s = 1 - r % 2
        add(f"rv{r}", "A", 2, "X", k8, "act", ("copy_tok", s), ("w_in_even", None, cols(RV + 512 * r, 512)),
            after_ret=max(r - 1, 0), after_job=24 if r == 1 else 0)
        add(f"rg{r}", "A", 2, "X", k8, "dve", ("gate", s), ("w_in_even", None, cols(RG + 512 * r, 512)),
            after_ret=max(r - 1, 0), after_job=24 if r == 1 else 0)

    mla(0)
    ret_qk(0)
    mla(1)
    for r in (0, 1):
        ret_vg(r)
    ret_qk(1)
    for r in (2, 3):
        ret_vg(r)
    add("out2", "B", 12, "S", list(range(24)), "dve", ("norm", 2), ("w_out_even", list(range(16, 24)) + list(range(16)), None))

    for half in (0, 1):
        s = 1 - half
        for name, c0 in (("k", 1024), ("q", 0)):
            add(f"m{name}{half}", "A", 2, "X", k8, "dve", ("rope", name, s, 64), ("w_in_odd", None, cols(c0 + 512 * half, 512)),
                after_ret=4)
        add(f"mv{half}", "A", 2, "X", k8, "act", ("copy_tok", s), ("w_in_odd", None, cols(2048 + 512 * half, 512)),
            after_ret=4)
        add(f"mgt{half}", "A", 2, "X", k8, "dve", ("gate", s), ("w_in_odd", None, cols(3072 + 512 * half, 512)),
            after_ret=4)
    add("out3", "B", 4, "S", k8, "dve", ("norm", 3), ("w_out_odd", k8, None))

    width = dict(F=1, small=1, A=2, B=4, Q1=4, Q2=4)
    at, held, n_act, n_dve, u = 0, [None] * 4, 0, 0, 0
    for c, ch in enumerate(out):
        w = width[ch["kind"]]
        at = (at + w - 1) // w * w % 4
        ch["bank"], ch["before"] = at, sorted({held[b] for b in range(at, at + w)} - {None})
        for b in range(at, at + w):
            held[b] = c
        at = (at + w) % 4
        ch["u0"] = u
        u += ch["n"]
        if ch["who"] == "act":
            n_act += 1
        else:
            n_dve += 1
        ch["count"] = n_act if ch["who"] == "act" else n_dve
    return out


CH = chunks()
BY = {ch["name"]: i for i, ch in enumerate(CH)}
UNITS = [(c, i) for c, ch in enumerate(CH) for i in range(ch["n"])]
NU = len(UNITS)


def unit_size(u):
    return 2 * 768 if CH[UNITS[u][0]]["kind"] == "Q1" else UNIT


JOBS = []
for h in range(8):
    JOBS.append(dict(kind="fox", s=0, h=h, needs=["vA", "f", f"kA{h // 4}", f"qA{h // 4}"]))
for h in range(8):
    JOBS.append(dict(kind="band", s=1, h=h, needs=["vB", f"kB{h // 4}", f"qB{h // 4}"]))
for h in range(8):
    JOBS.append(dict(kind="mla", s=0, h=h % 4, needs=[f"mlaq{h // 4}", f"mlakv{h // 4}", f"mg{h // 4}"]))
for h in range(16):
    JOBS.append(dict(kind="moba", s=1 - h // 8, h=h % 8, needs=[f"m{x}{h // 8}" for x in ("k", "q", "v", "gt")]))
for j, job in enumerate(JOBS):
    job["dv"] = 128 if job["kind"] == "mla" else 64

TJ = []


def new_t(src, dst, split, bank, needs, tiles=1):
    TJ.append(dict(src=src, dst=dst, split=split, bank=bank, needs=needs, tiles=tiles))
    return len(TJ) - 1


def plan():
    order, given, pending, deferred = [], set(), [], []
    state = dict(split=0, wait=0)

    def emit(step, *gives):
        order.append(step)
        given.update(gives)

    def background(rate):
        n = 0
        while pending and n < rate and pending[0][0] <= given:
            _, steps, gives = pending.pop(0)
            for st in steps:
                emit(st)
            given.update(gives)
            n += 1

    def require(names):
        while not names <= given:
            if deferred and not pending[0][0] <= given:
                flush_turns()
            need, steps, gives = pending.pop(0)
            assert need <= given, (names - given, need - given)
            for st in steps:
                emit(st)
            given.update(gives)

    def split_to(u):
        while state["split"] < min(u, NU):
            emit(("split", state["split"]))
            state["split"] += 1

    def flush_turns():
        while deferred:
            name = deferred.pop()
            rope_turns(name)
            given.add(name)
            state["wait"] = 0

    def evacuate(c):
        name, kind = CH[c]["name"], CH[c]["evac"][0]
        if kind in ("rope", "rope_kpe", "mla_q", "rms"):
            flush_turns()
        emit(("evac", c))
        if kind in ("rope", "rope_kpe", "mla_q"):
            deferred.append(name)
            state["wait"] = 2
        else:
            given.add(name)

    def run(name, rate, needs=lambda i, half: set()):
        c = BY[name]
        ch = CH[c]
        if ch["kind"] == "small":
            emit(("mm_small", c))
            evacuate(c)
        for i in range(ch["n"]):
            u = ch["u0"] + i
            for half in (0, 1):
                require(needs(i, half))
                emit(("mm", u, half))
                if half == 0:
                    split_to(u + RING)
                if deferred:
                    state["wait"] -= 1
                    if state["wait"] == 0:
                        flush_turns()
                if i == ch["n"] - 1 and half == 1:
                    evacuate(c)
                background(rate)

    def rope_turns(name):
        kind = CH[BY[name]]["evac"]
        if kind[0] == "rope":
            tiles, dst = 4, ("attn", kind[1], kind[2])
        elif kind[0] == "mla_q":
            tiles, dst = 2, ("qpe",)
        else:
            tiles, dst = 1, ("kpe",)
        for i in range(0, tiles, 2):
            emit(("turn", new_t(("rot", i), dst + (i,), False, 3, BY[name], min(2, tiles))))

    def attention(jobs):
        n = len(jobs)
        for i in range(n + 3):
            steps, need, gives = [], set(), set()
            if i >= 3:
                j = jobs[i - 3]
                job = JOBS[j]
                per = P // job["dv"]
                if (j + 1) % per == 0:
                    tile = (j % 16 if job["kind"] in ("fox", "band") else j - 16 if job["kind"] == "mla" else j - 24) // per
                    steps.append(("turn", new_t(("y", j), ("S", tile), True, 3, j)))
                    gives.add(f"{'L1' if j < 16 else 'L2' if j < 24 else 'L3'}y{tile}")
            if i < n:
                need = set(JOBS[jobs[i]]["needs"])
                steps += [("scores", jobs[i]), ("soft", jobs[i])]
            if 1 <= i <= n:
                steps += [("pt", jobs[i - 1])]
            if 2 <= i <= n + 1:
                steps += [("pv", jobs[i - 2])]
            pending.append((need, steps, gives))

    def retention(r):
        s = set([f"rk{r // 2}", f"rq{r // 2}"])
        pending.append((s, [("ret_s", r)], set()))
        pending.append((s | {f"rv{r}", f"rg{r}"}, [("ret_o", r)], set()))
        for i in (0, 2):
            t = new_t(("ry", r, i), ("S", 8 + 4 * r + i), True, 3, r, 2)
            pending.append((set(), [("turn", t)], {f"L2y{8 + 4 * r + i}", f"L2y{9 + 4 * r + i}"}))

    def turn_x(base):
        if base:
            for t in range(NT):
                emit(("norm_rest", base - 1, t))
        for t in range(NT):
            for q in range(2):
                emit(("turn", new_t(("x", t, q), ("X", t, q), True, 2 * t + q, base)))

    emit(("load", "start"))
    turn_x(0)
    split_to(1)
    emit(("small_split",))
    split_to(RING)

    for name in ("kA0", "qA0", "f"):
        run(name, 0)
    emit(("cum",))
    run("vA", 0)
    attention(range(0, 8))
    for name in ("kA1", "qA1", "kB0", "qB0"):
        run(name, 1)
    run("vB", 1)
    attention(range(8, 16))
    for name in ("kB1", "qB1"):
        run(name, 1)
    run("out1", 1, lambda i, half: {f"L1y{2 * i + half}"})
    emit(("load", "ln", 0))
    turn_x(1)
    for j in range(FT + 2):
        if j < FT:
            run(f"up{j}", 0)
        if 1 <= j <= FT:
            emit(("gelu", j - 1))
        if j >= 2:
            emit(("h_split", j - 2))
    emit(("load", "ln", 1))
    emit(("tables",))
    run("down", 0)
    turn_x(2)

    emit(("load", "even"))
    run("mqkv", 0)
    run("mg0", 0)
    for i in (0, 2):
        emit(("turn", new_t(("mn", i), ("S", 20 + i), True, 3, 0, 2)))
    for name in ("mkr", "mlaq0", "mlakv0"):
        run(name, 0)
    attention(range(16, 20))
    for name in ("rk0", "rq0"):
        run(name, 2)
    for name in ("mg1",):
        require({"L2y3"})
        run(name, 0)
    for name in ("mlaq1", "mlakv1"):
        run(name, 0)
    attention(range(20, 24))
    retention(0)
    run("rv0", 2)
    run("rg0", 2)
    retention(1)
    require({"L2y7"})
    for name in ("rv1", "rg1"):
        run(name, 1)
    for name in ("rk1", "rq1"):
        run(name, 2)
    retention(2)
    require({"L2y15"})
    for name in ("rv2", "rg2"):
        run(name, 1)
    retention(3)
    run("rv3", 1)
    require({"L2y19"})
    run("rg3", 1)
    run("out2", 1, lambda i, half: {f"L2y{2 * i + half}"})
    emit(("load", "ln", 2))
    turn_x(3)

    for name in ("mk0", "mq0", "mv0", "mgt0"):
        run(name, 0)
    attention(range(24, 32))
    for name in ("mk1", "mq1", "mv1", "mgt1"):
        run(name, 1)
    attention(range(32, 40))
    run("out3", 1, lambda i, half: {f"L3y{2 * i + half}"})
    emit(("load", "ln", 3))
    emit(("norm_rest", 3, 0))
    emit(("norm_rest", 3, 1))
    emit(("store",))
    assert not pending, pending
    return order


ORDER = plan()
assert [s[1] for s in ORDER if s[0] == "evac"] == list(range(len(CH)))
RANK = {n: i for i, n in enumerate(s[1] for s in ORDER if s[0] == "turn")}
SPLITS = [s[1] for s in ORDER if s[0] == "turn" and TJ[s[1]]["split"]]
SPLIT_RANK = {n: i for i, n in enumerate(SPLITS)}
BANKS = dict(scores=lambda n: [n % 2], pt=lambda n: [2], pv=lambda n: [3], turn=lambda n: [TJ[n]["bank"]],
             cum=lambda n: [0], ret_s=lambda n: [0], ret_o=lambda n: [1, 2])
BANK_BEFORE = {}
_last = {}
for _s in ORDER:
    if _s[0] in BANKS:
        _banks = BANKS[_s[0]](_s[-1])
        BANK_BEFORE[_s] = sorted({_last[b] for b in _banks if b in _last})
        _last.update({b: _s for b in _banks})
FILLED = {}
_seen = {}
for _s in ORDER:
    if _s[0] == "turn":
        d = TJ[_s[1]]["dst"]
        if d[0] == "S":
            for _i in range(TJ[_s[1]]["tiles"]):
                _seen[("S", d[1] + _i)] = _s[1]
        elif d[0] == "X":
            _seen[("X", 0)] = _s[1]
        else:
            _seen[d[:3] if d[0] == "attn" else d[:1]] = _s[1]
    elif _s[0] in ("mm", "mm_small", "scores", "ret_s"):
        FILLED[_s] = dict(_seen)
Y_TURN = {TJ[n]["src"][1]: n for n in RANK if TJ[n]["src"][0] == "y"}
_tiles = sorted(Y_TURN)
Y_SLOT = {j: i % 2 for i, j in enumerate(_tiles)}
Y_BEFORE = {}
for _i, _j in enumerate(_tiles):
    for _k in range(_j - P // JOBS[_j]["dv"] + 1, _j + 1):
        Y_SLOT[_k] = _i % 2
        if _i >= 2:
            Y_BEFORE[_k] = Y_TURN[_tiles[_i - 2]]
ROT_READ, _r = {}, None
for _s in ORDER:
    if _s[0] == "turn" and TJ[_s[1]]["src"][0] in ("rot", "mn"):
        _r = _s[1]
    elif _s[0] == "evac":
        ROT_READ[_s[1]] = _r
RET_TURN = {r: max((n for n in RANK if TJ[n]["src"][:2] == ("ry", r)), key=RANK.get) for r in range(4)}

CONST = {}
_at = 0
for _name, _n in (("ident", P), ("causal", 3 * P), ("band", P), ("tri", 2 * P), ("pick0", 1), ("pick1", 1),
                  ("inv64", 32), ("inv256", 128)):
    CONST[_name] = (_at, _at + _n)
    _at += _n
NCONST = _at


def constants():
    c = np.zeros((P, NCONST), np.float32)

    def put(name, a):
        c[:, CONST[name][0]:CONST[name][1]] = a

    q, k = np.arange(P)[:, None], np.arange(P)[None, :]
    tri = np.where(k <= q, 0.0, NEG).astype(np.float32)
    put("ident", np.eye(P, dtype=np.float32))
    put("causal", np.concatenate([tri, np.zeros((P, P), np.float32), tri], 1))
    put("band", np.where(k // 64 <= q // 64, 0.0, NEG).astype(np.float32))
    put("tri", np.concatenate([(q <= k).astype(np.float32), np.ones((P, P), np.float32)], 1))
    put("pick0", (q % 32 == 0).astype(np.float32))
    put("pick1", (q % 32 == 1).astype(np.float32))
    put("inv64", (1.0 / (np.float32(10000.0) ** (np.arange(0, 64, 2, dtype=np.float32) / np.float32(64)))).astype(np.float32)[None, :])
    put("inv256", (1.0 / (np.float32(10000.0) ** np.linspace(0, 1, 128, dtype=np.float32))).astype(np.float32)[None, :])
    return c


def decay_table():
    g = 1.0 - 2.0 ** (-5.0 - np.arange(4, dtype=np.float64))
    d = np.arange(S)[None, :] - np.arange(P)[:, None]
    t = np.where(d[None] >= 0, g[:, None, None] ** np.maximum(d, 0)[None], 0.0) / 16.0
    return np.ascontiguousarray(t.transpose(1, 0, 2)).astype(np.float32)


def build(nc, t):
    with ExitStack() as ctx:
        def sb(name, shape, dt=F32):
            return ctx.enter_context(nc.sbuf_tensor(name, shape, dt))

        def sem(name):
            return ctx.enter_context(nc.semaphore(name))

        raw = sb("raw", [P, RAW, UNIT])
        w_hi = sb("w_hi", [P, RING, UNIT], F32R)
        w_lo = sb("w_lo", [P, RING, UNIT], F32R)
        X_hi = sb("X_hi", [P, KT, S], F32R)
        X_lo = sb("X_lo", [P, KT, S], F32R)
        S_hi = sb("S_hi", [P, 24, S], F32R)
        S_lo = sb("S_lo", [P, 24, S], F32R)
        res = sb("res", [P, NT, D])
        decay = sb("decay", [P, 4, S])
        ryb = sb("ryb", [P, NT, 512])
        cst = sb("cst", [P, NCONST])
        qT = [sb(f"qT{s}", [P, 4, S]) for s in (0, 1)]
        kT = [sb(f"kT{s}", [P, 4, S]) for s in (0, 1)]
        vv = [sb(f"v{s}", [P, NT, 512]) for s in (0, 1)]
        gate = sb("gate", [P, 2, NT, 512])
        qpeT = sb("qpeT", [P, 2, S])
        kpeT = sb("kpeT", [P, 1, S])
        rot = sb("rot", [P, NT, 512])
        rtmp = sb("rtmp", [P, NT, 512])
        pr = sb("pr", [P, 2, 3 * P])
        ptb = sb("ptb", [P, 2, 3 * P])
        yb = sb("yb", [P, 2, NT, P])
        small = sb("small", [P, 96])
        tab64 = sb("tab64", [P, 2, NT, 32])
        tab256 = sb("tab256", [P, 2, NT, 128])
        wsm_hi = sb("wsm_hi", [P, KT, 72], F32R)
        wsm_lo = sb("wsm_lo", [P, KT, 72], F32R)
        cvp = sb("cvp", [P, 4, 2, FT])
        posi = sb("posi", [P, NT], I32)
        cumA = rot[:, 0, :].rearrange("p (g s) -> p g s", g=2)
        cumB = rot[:, 1, :].rearrange("p (g s) -> p g s", g=2)

        acc = ctx.enter_context(nc.psum_tensor("acc", [P, 4, 512], F32))
        job = ctx.enter_context(nc.psum_tensor("job", [P, 4, 512], F32))

        lfx = vv[1][:, :, 0:256].rearrange("p t (g c) -> p t g c", g=2)
        lf = vv[1][:, :, 256:256 + 32].rearrange("p t (a h) -> p t a h", a=4)
        bias = gate[:, :, :, :].rearrange("p s t n -> p (s t n)").rearrange("p (h k) -> p h k", h=8)
        conv = [vv[b][:, 0, :].rearrange("p (i s) -> p i s", i=2) for b in (0, 1)]
        gel = [vv[b][:, 1, 0:256] for b in (0, 1)]
        hh = [vv[b][:, 1, 256:512] for b in (0, 1)]
        gb = gate[:, :, :, :].rearrange("p s t n -> p s (t n)")
        wsm = ryb[:, :, :].rearrange("p t n -> p (t n)")[:, 0:KT * 72].rearrange("p (k n) -> p k n", k=KT)
        rgain = pr[:, :, :].rearrange("p b n -> p (b n)")[:, 0:512]
        ang = qT[0][:, 0:2, 0:160]
        turns = qT[0][:, 2:4, 0:160]
        wrap = qT[1][:, 0:2, 0:160]
        sin_arg = kT[0][:, 0:2, 0:160]
        cos_arg = kT[0][:, 2:4, 0:160]
        posf = small[:, 90:92]
        bforget = small[:, 80:88]
        neg_max = small[:, 0:4].rearrange("p (b t) -> p b t", b=2)
        rsum = small[:, 4:8].rearrange("p (b t) -> p b t", b=2)
        rinv = small[:, 8:10]
        rdbl = small[:, 10:12]
        stats = small[:, 12:36].rearrange("p (t q s) -> p t q s", t=2, q=2)
        mv = small[:, 36:40].rearrange("p (t a) -> p t a", t=2)
        rstd_in = small[:, 40:44]
        rstd = small[:, 44:48]
        half_neg = small[:, 48:52]
        nmr = small[:, 52:54]
        ssq = small[:, 56:60]

        def const(name):
            a, b = CONST[name]
            return cst[:, a:b]

        ident = const("ident")

        landed = [sem(f"landed{i}") for i in range(RAW)]
        hi_done, lo_done, w_used = sem("hi_done"), sem("lo_done"), sem("w_used")
        small_ready, evac_act, evac_dve = sem("small_ready"), sem("evac_act"), sem("evac_dve")
        t_ready, t_hi, t_lo = sem("t_ready"), sem("t_hi"), sem("t_lo")
        sc_ready, max_done, exp_done = sem("sc_ready"), sem("max_done"), sem("exp_done")
        pt_ready, pt_copied, o_ready, y_done = sem("pt_ready"), sem("pt_copied"), sem("o_ready"), sem("y_done")
        const_in, x_in, bias_in, small_in = sem("const_in"), sem("x_in"), sem("bias_in"), sem("small_in")
        pos_in, bf_in, conv_in = sem("pos_in"), sem("bf_in"), sem("conv_in")
        ln_g_in, ln_b_in, even_in, rg_in = sem("ln_g_in"), sem("ln_b_in"), sem("even_in"), sem("rg_in")
        wsm_hi_done, wsm_lo_done = sem("wsm_hi_done"), sem("wsm_lo_done")
        ang_done, sin_done, tab_done = sem("ang_done"), sem("sin_done"), sem("tab_done")
        z_ready, ln_ready, cum_ready, cum_done = (sem("z_ready"), sem("ln_ready"),
                                                             sem("cum_ready"), sem("cum_done"))
        bias_ready = sem("bias_ready")
        tap_act, tap_dve, gelu_done, h_done, h_hi, h_lo = (sem("tap_act"), sem("tap_dve"), sem("gelu_done"),
                                                           sem("h_done"), sem("h_hi"), sem("h_lo"))
        stat_done, pow_done, x_norm, x_gain, x_ready = (sem("stat_done"), sem("pow_done"), sem("x_norm"),
                                                        sem("x_gain"), sem("x_ready"))
        pow_in = sem("pow_in")
        mn_ready = sem("mn_ready")
        sq_done = sem("sq_done")
        half_ready = sem("half_ready")
        th_done = sem("th_done")
        rot_prod, rot_ready = sem("rot_prod"), sem("rot_ready")
        rs_ready, rp_done, ro_ready, ry_done = sem("rs_ready"), sem("rp_done"), sem("ro_ready"), sem("ry_done")
        stored = sem("stored")
        qn_copied, nmr_ready = sem("qn_copied"), sem("nmr_ready")
        dve_chain, act_chain, pool_chain = sem("dve_chain"), sem("act_chain"), sem("pool_chain")

        block = ctx.enter_context(nc.Block())

        ROT = [c for c, ch in enumerate(CH) if ch["evac"][0] in ("rope", "rope_kpe", "mla_q")]
        GATE = [c for c, ch in enumerate(CH) if ch["evac"][0] == "gate"]
        POW = []
        for s_ in ORDER:
            if s_[0] == "evac" and CH[s_[1]]["evac"][0] == "norm":
                POW += [("norm", CH[s_[1]]["evac"][1], 0), ("norm", CH[s_[1]]["evac"][1], 1)]
            elif s_[0] == "evac" and CH[s_[1]]["evac"][0] == "rms":
                POW.append(("rms",))
            elif s_[0] == "ret_o":
                POW.append(("ret", s_[1]))

        def chunk_waits(eng, c):
            for b in CH[c]["before"]:
                eng.wait_ge(evac_act if CH[b]["who"] == "act" else evac_dve, CH[b]["count"])

        def wait_chunk_evac(eng, name):
            ch = CH[BY[name]]
            eng.wait_ge(evac_act if ch["who"] == "act" else evac_dve, ch["count"])

        def after_waits(eng, ch):
            if ch.get("after_job"):
                eng.wait_ge(y_done, ch["after_job"])
            if ch.get("after_ret"):
                eng.wait_ge(ry_done, ch["after_ret"])

        def place(n):
            return job[:, TJ[n]["bank"], :]

        def bank_free(eng, step):
            for before in BANK_BEFORE[step]:
                kind, n = before[0], before[-1]
                if kind == "scores":
                    eng.wait_ge(max_done, n + 1)
                elif kind == "pt":
                    eng.wait_ge(pt_copied, n + 1)
                elif kind == "pv":
                    eng.wait_ge(y_done, n + 1)
                elif kind == "cum":
                    eng.wait_ge(cum_done, 2)
                elif kind == "ret_s":
                    eng.wait_ge(rp_done, n + 1)
                elif kind == "ret_o":
                    eng.wait_ge(ry_done, n + 1)
                elif TJ[n]["split"]:
                    eng.wait_ge(t_lo, SPLIT_RANK[n] + 1)
                else:
                    eng.wait_ge(t_hi, RANK[n] + 1)

        @block.sync
        def _(sp):
            def load_unit(u):
                n = unit_size(u)
                if u >= RAW:
                    sp.wait_ge(lo_done, u - RAW + 1)
                sp.dma_start(raw[:, u % RAW, 0:n], t["w"][u, :, 0:n]).then_inc(landed[u % RAW], 16)

            for step in ORDER:
                if step == ("load", "start"):
                    sp.dma_start(cst[:], t["const"]).then_inc(const_in, 16)
                    sp.dma_start(res[:], t["x"].rearrange("b (t p) d -> p (b t) d", p=P)).then_inc(x_in, 16)
                    load_unit(0)
                    load_unit(1)
                    sp.dma_start(posi[:], t["positions_2"]).then_inc(pos_in, 16)
                    sp.dma_start(wsm[:], t["w_small"]).then_inc(small_in, 16)
                    sp.dma_start(bforget, t["b_forget"].partition_broadcast(P)).then_inc(bf_in, 16)
                    sp.dma_start(bias[:, :, :], t["bias"]).then_inc(bias_in, 16)
                    sp.dma_start(cvp[:], t["conv"]).then_inc(conv_in, 16)
                    sp.dma_start(decay[:], t["decay"]).then_inc(even_in, 16)
                elif step[0] == "split":
                    if step[1] + RAW < NU:
                        load_unit(step[1] + RAW)
                elif step == ("store",):
                    for i in range(NT):
                        sp.wait_ge(x_ready, 2 * 3 + i + 1)
                        sp.dma_start(t["out"][0, i * P:(i + 1) * P, :], res[:, i, :]).then_inc(stored, 16)
            sp.wait_ge(stored, 16 * NT)

        @block.tensor
        def _(pe):
            def three(out, a_hi, a_lo, b_hi, b_lo, start, stop):
                nc.tensor.matmul(out, a_hi, b_hi, start=start, stop=False)
                nc.tensor.matmul(out, a_hi, b_lo, start=False, stop=False)
                return nc.tensor.matmul(out, a_lo, b_hi, start=False, stop=stop)

            def wait_stationary(step, ch, tiles):
                seen = FILLED[step]
                keys = [("X", 0)] if ch["src"] == "X" else [("S", i) for i in tiles if ("S", i) in seen]
                if ch["name"] == "down":
                    pe.wait_ge(h_lo, max(tiles) + 1)
                else:
                    pe.wait_ge(t_lo, max(SPLIT_RANK[seen[k]] for k in keys) + 1)

            def mm(step):
                u, half = step[1], step[2]
                c, i = UNITS[u]
                ch = CH[c]
                hi, lo = (X_hi, X_lo) if ch["src"] == "X" else (S_hi, S_lo)
                wh, wl = w_hi[:, u % RING, :], w_lo[:, u % RING, :]
                kind, b0 = ch["kind"], ch["bank"]
                if i == 0 and half == 0:
                    chunk_waits(pe, c)
                if half == 0:
                    pe.wait_ge(lo_done, u + 1)
                last = None
                if kind == "F":
                    wait_stationary(step, ch, ch["tiles"])
                    for k in range(KT):
                        w = slice(k * 256 + half * P, k * 256 + half * P + P)
                        last = three(acc[:, b0, half * S:(half + 1) * S], wh[:, w], wl[:, w], hi[:, k, :], lo[:, k, :],
                                     k == 0, k == KT - 1)
                elif kind in ("A", "B"):
                    per, n, nb = (2, 512, 1) if kind == "A" else (1, D, 2)
                    first = (i * 2 + half) * per
                    tiles = ch["tiles"][first:first + per]
                    wait_stationary(step, ch, tiles)
                    for x, k in enumerate(tiles):
                        for tt in range(NT):
                            for nn in range(nb):
                                w0 = (half * per + x) * n + nn * 512
                                last = three(acc[:, b0 + tt * nb + nn, :], hi[:, k, tt * P:(tt + 1) * P],
                                             lo[:, k, tt * P:(tt + 1) * P], wh[:, w0:w0 + 512], wl[:, w0:w0 + 512],
                                             first + x == 0, first + x == len(ch["tiles"]) - 1)
                else:
                    wait_stationary(step, ch, ch["tiles"])
                    wide = 768 if kind == "Q1" else D
                    if half == 0:
                        for f in range(4):
                            for x, k in enumerate(ch["tiles"]):
                                w = slice(x * wide + f * P, x * wide + f * P + P)
                                last = three(acc[:, b0 + f // 2, (f % 2) * S:(f % 2 + 1) * S], wh[:, w], wl[:, w],
                                             hi[:, k, :], lo[:, k, :], x == 0, x == 1)
                    else:
                        n = wide - 512
                        for tt in range(NT):
                            for x, k in enumerate(ch["tiles"]):
                                w = slice(x * wide + 512, x * wide + 512 + n)
                                last = three(acc[:, b0 + 2 + tt, 0:n], hi[:, k, tt * P:(tt + 1) * P],
                                             lo[:, k, tt * P:(tt + 1) * P], wh[:, w], wl[:, w], x == 0, x == 1)
                if half == 1:
                    last.then_inc(w_used, 1)

            def mm_small(step):
                c = step[1]
                ch = CH[c]
                chunk_waits(pe, c)
                pe.wait_ge(wsm_lo_done, 1)
                wait_stationary(step, ch, ch["tiles"])
                a, n = (0, 8) if ch["name"] == "f" else (8, 64)
                for tt in range(NT):
                    for k in range(KT):
                        last = three(acc[:, ch["bank"], tt * 64:tt * 64 + n], X_hi[:, k, tt * P:(tt + 1) * P],
                                     X_lo[:, k, tt * P:(tt + 1) * P], wsm_hi[:, k, a:a + n], wsm_lo[:, k, a:a + n],
                                     k == 0, k == KT - 1)
                last.then_inc(small_ready, 1)

            def cum():
                wait_chunk_evac(pe, "f")
                bank_free(pe, ("cum",))
                tri = const("tri")
                for g in range(2):
                    nc.tensor.matmul(job[:, 0, g * S:(g + 1) * S], lfx[:, 0, g, :], tri, start=True, stop=False)
                    last = nc.tensor.matmul(job[:, 0, g * S + P:(g + 1) * S], lfx[:, 1, g, :], tri[:, 0:P],
                                            start=False, stop=True)
                last.then_inc(cum_ready, 1)

            def scores(step):
                j = step[1]
                jb = JOBS[j]
                s, h = jb["s"], jb["h"]
                for name in jb["needs"]:
                    if CH[BY[name]]["evac"][0] not in ("gate", "rope", "forget"):
                        wait_chunk_evac(pe, name)
                bank_free(pe, step)
                out = job[:, j % 2, :]
                blocks = [(out[:, 0:P], 0, P), (out[:, P:3 * P], 1, S)]
                seen = FILLED[step]
                if jb["kind"] in ("mla", "moba"):
                    keys = [("qpe",), ("kpe",)] if jb["kind"] == "mla" else [("attn", "q", s), ("attn", "k", s)]
                    pe.wait_ge(t_hi, max(RANK[seen[k]] for k in keys) + 1)
                for dst, tt, nk in blocks:
                    q = slice(tt * P, (tt + 1) * P)
                    if jb["kind"] == "mla":
                        lo_p = 64 * (h % 2)
                        nc.tensor.matmul(dst, qT[s][:, h, q], kT[s][:, h, 0:nk], start=True, stop=False)
                        last = nc.tensor.matmul(dst, qpeT[lo_p:lo_p + 64, h // 2, q], kpeT[lo_p:lo_p + 64, 0, 0:nk],
                                                start=False, stop=True)
                    else:
                        lo_p = 64 * (h % 2)
                        fox = jb["kind"] == "fox"
                        last = nc.tensor.matmul(dst, qT[s][lo_p:lo_p + 64, h // 2, q], kT[s][lo_p:lo_p + 64, h // 2, 0:nk],
                                                start=True, stop=not fox)
                        if fox:
                            pe.wait_ge(cum_done, 2)
                            r = 32 * (h % 4)
                            last = nc.tensor.matmul(dst, cumA[r:r + 2, h // 4, q], cumB[r:r + 2, h // 4, 0:nk],
                                                    start=False, stop=True)
                last.then_inc(sc_ready, 1)

            def pt(step):
                j = step[1]
                pe.wait_ge(exp_done, j + 1)
                bank_free(pe, step)
                for b in range(3):
                    last = nc.tensor.transpose(job[:, 2, b * P:(b + 1) * P], pr[:, j % 2, b * P:(b + 1) * P], ident)
                last.then_inc(pt_ready, 1)

            def pv(step):
                j = step[1]
                jb = JOBS[j]
                s, h, dv = jb["s"], jb["h"], jb["dv"]
                pe.wait_ge(pt_copied, j + 1)
                bank_free(pe, step)
                b = ptb[:, j % 2, :]
                v = slice(h * dv, (h + 1) * dv)
                nc.tensor.matmul(job[:, 3, 0:dv], b[:, 0:P], vv[s][:, 0, v], start=True, stop=True)
                nc.tensor.matmul(job[:, 3, P:P + dv], b[:, P:2 * P], vv[s][:, 0, v], start=True, stop=False)
                nc.tensor.matmul(job[:, 3, P:P + dv], b[:, 2 * P:3 * P], vv[s][:, 1, v], start=False, stop=True)\
                    .then_inc(o_ready, 1)

            def turn(step):
                n = step[1]
                tj = TJ[n]
                kind = tj["src"][0]
                bank_free(pe, step)
                out = place(n)
                if kind == "x":
                    _, tt, q = tj["src"]
                    if tj["needs"] == 0:
                        pe.wait_ge(x_in, 16)
                        pe.wait_ge(const_in, 16)
                    else:
                        pe.wait_ge(x_ready, 2 * (tj["needs"] - 1) + tt + 1)
                    for i in range(4):
                        k = 4 * q + i
                        last = nc.tensor.transpose(out[:, i * P:(i + 1) * P], res[:, tt, k * P:(k + 1) * P], ident)
                else:
                    for tt in range(NT):
                        if kind == "rot":
                            pe.wait_ge(rot_ready, NT * ROT.index(tj["needs"]) + tt + 1)
                            src = rot[:, tt, tj["src"][1] * P:]
                        elif kind == "mn":
                            pe.wait_ge(mn_ready, tt + 1)
                            src = rot[:, tt, tj["src"][1] * P:]
                        elif kind == "y":
                            pe.wait_ge(y_done, tj["src"][1] + 1)
                            src = yb[:, Y_SLOT[tj["src"][1]], tt, :]
                        else:
                            pe.wait_ge(ry_done, tj["src"][1] + 1)
                            src = ryb[:, tt, tj["src"][2] * P:]
                        for i in range(tj["tiles"]):
                            last = nc.tensor.transpose(out[:, i * S + tt * P:i * S + (tt + 1) * P],
                                                       src[:, i * P:(i + 1) * P], ident)
                last.then_inc(t_ready, 1)

            def ret_s(step):
                r = step[1]
                s = 1 - r // 2
                seen = FILLED[step]
                pe.wait_ge(t_hi, max(RANK[seen[("attn", "q", s)]], RANK[seen[("attn", "k", s)]]) + 1)
                bank_free(pe, step)
                b = 2 * (r % 2)
                for e in range(2):
                    nc.tensor.matmul(job[:, 0, 0:S], kT[s][:, b + e, 0:P], qT[s][:, b + e, :], start=e == 0, stop=e == 1)
                for e in range(2):
                    last = nc.tensor.matmul(job[:, 0, S:S + P], kT[s][:, b + e, P:S], qT[s][:, b + e, P:S],
                                            start=e == 0, stop=e == 1)
                last.then_inc(rs_ready, 1)

            def ret_o(step):
                r = step[1]
                s = 1 - r % 2
                wait_chunk_evac(pe, f"rv{r}")
                pe.wait_ge(rp_done, r + 1)
                bank_free(pe, step)
                b = ptb[:, r % 2, :]
                nc.tensor.matmul(job[:, 1, :], b[:, 0:P], vv[s][:, 0, :], start=True, stop=True)
                nc.tensor.matmul(job[:, 2, :], b[:, P:2 * P], vv[s][:, 0, :], start=True, stop=False)
                nc.tensor.matmul(job[:, 2, :], b[:, 2 * P:3 * P], vv[s][:, 1, :], start=False, stop=True)\
                    .then_inc(ro_ready, 1)

            for step in ORDER:
                if step[0] == "mm":
                    mm(step)
                elif step[0] == "mm_small":
                    mm_small(step)
                elif step[0] == "cum":
                    cum()
                elif step[0] == "scores":
                    scores(step)
                elif step[0] == "pt":
                    pt(step)
                elif step[0] == "pv":
                    pv(step)
                elif step[0] == "turn":
                    turn(step)
                elif step[0] == "ret_s":
                    ret_s(step)
                elif step[0] == "ret_o":
                    ret_o(step)

        def wait_acc(eng, c):
            ch = CH[c]
            if ch["kind"] == "small":
                eng.wait_ge(small_ready, 1 if ch["name"] == "f" else 2)
            else:
                eng.wait_ge(w_used, ch["u0"] + ch["n"])

        def t_dest(n):
            tj = TJ[n]
            d, p = tj["dst"], place(n)
            if d[0] == "X":
                _, tt, q = d
                v = slice(tt * P, (tt + 1) * P)
                return (X_hi[:, 4 * q:4 * q + 4, v], X_lo[:, 4 * q:4 * q + 4, v], p.rearrange("p (k s) -> p k s", k=4))
            nt = tj["tiles"]
            src = p[:, 0:nt * S].rearrange("p (k s) -> p k s", k=nt)
            at = slice(d[-1], d[-1] + nt)
            if d[0] == "S":
                return S_hi[:, at, :], S_lo[:, at, :], src
            if d[0] == "qpe":
                return qpeT[:, at, :], None, src
            if d[0] == "kpe":
                return kpeT[:, at, :], None, src
            return (qT if d[1] == "q" else kT)[d[2]][:, at, :], None, src

        @block.scalar
        def _(act):
            def split(u):
                n = unit_size(u)
                act.wait_ge(landed[u % RAW], 16 * (u // RAW + 1))
                if u >= RING:
                    act.wait_ge(w_used, u - RING + 1)
                nc.scalar.activation(w_hi[:, u % RING, 0:n], raw[:, u % RAW, 0:n], ACT.Copy).then_inc(hi_done, 1)

            def turn(n):
                hi, _, src = t_dest(n)
                act.wait_ge(t_ready, RANK[n] + 1)
                nc.scalar.activation(hi, src, ACT.Copy).then_inc(t_hi, 1)

            def evac(c):
                ch = CH[c]
                e, b0 = ch["evac"], ch["bank"]
                kind = e[0]
                if kind in ("rope", "rope_kpe", "norm"):
                    return
                if kind != "conv":
                    wait_acc(act, c)
                    after_waits(act, ch)
                if kind == "copy_feat":
                    _, which, s, half = e
                    dst = (qT if which == "q" else kT)[s][:, 2 * half:2 * half + 2, :]
                    nc.scalar.activation(dst, acc[:, b0, :].rearrange("p (a s) -> p a s", a=2), ACT.Copy)\
                        .then_inc(evac_act, 1)
                elif kind == "copy_tok":
                    nc.scalar.activation(vv[e[1]][:, :, :], acc[:, b0:b0 + 2, :], ACT.Copy).then_inc(evac_act, 1)
                elif kind == "mla_kv":
                    nc.scalar.activation(kT[0][:, :, :], acc[:, b0:b0 + 2, :].rearrange("p b (a s) -> p (b a) s", a=2), ACT.Copy)
                    nc.scalar.activation(vv[0][:, :, :], acc[:, b0 + 2:b0 + 4, :], ACT.Copy).then_inc(evac_act, 1)
                elif kind == "mla_q":
                    nc.scalar.activation(qT[0][:, :, :], acc[:, b0:b0 + 2, :].rearrange("p b (a s) -> p (b a) s", a=2), ACT.Copy)\
                        .then_inc(qn_copied, 1)
                elif kind == "gate":
                    nc.scalar.activation(gate[:, e[1], :, :], acc[:, b0:b0 + 2, :], ACT.Tanh, scale=0.5).then_inc(th_done, 1)
                elif kind == "rms":
                    for tt in range(NT):
                        for x in range(2):
                            last = nc.scalar.activation(rtmp[:, tt, x * 256:(x + 1) * 256],
                                                        acc[:, b0 + tt, x * 256:(x + 1) * 256], ACT.Square,
                                                        accum_out=ssq[:, 2 * tt + x:2 * tt + x + 1])
                    last.then_inc(sq_done, 1)
                elif kind == "forget":
                    act.wait_ge(z_ready, 1)
                    for i, (a, b, f, kw) in enumerate(((0, 1, ACT.Abs, {}), (1, 1, ACT.Exp, dict(scale=-1.0)),
                                                       (1, 1, ACT.Ln, dict(bias=1.0)))):
                        nc.scalar.activation(lf[:, :, b, :], lf[:, :, a, :], f, **kw).then_inc(ln_ready, 1)
                        act.wait_ge(ln_ready, i + 1)
                elif kind == "conv":
                    j = e[1]
                    wait_acc(act, c)
                    if j == 0:
                        act.wait_ge(conv_in, 16)
                    if j >= 2:
                        act.wait_ge(h_done, j - 1)
                    for i in range(2):
                        last = nc.scalar.activation(conv[j % 2][:, i, :], acc[:, b0, i * S:(i + 1) * S], ACT.Identity,
                                                    scale=cvp[:, 2, i, j:j + 1], bias=cvp[:, 3, i, j:j + 1])
                    last.then_inc(tap_act, 1)

            def soft(j):
                act.wait_ge(max_done, j + 1)
                if j >= 2:
                    act.wait_ge(y_done, j - 1)
                b = j % 2
                nc.scalar.activation(pr[:, b, 0:P], pr[:, b, 0:P], ACT.Exp, bias=neg_max[:, b, 0:1],
                                     accum_out=rsum[:, b, 0:1])
                nc.scalar.activation(pr[:, b, P:3 * P], pr[:, b, P:3 * P], ACT.Exp, bias=neg_max[:, b, 1:2],
                                     accum_out=rsum[:, b, 1:2]).then_inc(exp_done, 1)

            def pt(j):
                act.wait_ge(pt_ready, j + 1)
                if j >= 2:
                    act.wait_ge(o_ready, j - 1)
                if j in (24, 25):
                    act.wait_ge(ro_ready, 4)
                nc.scalar.activation(ptb[:, j % 2, :], job[:, 2, 0:3 * P], ACT.Copy).then_inc(pt_copied, 1)

            def gelu(j):
                act.wait_ge(evac_dve, CH[BY[f"up{j}"]]["count"])
                nc.scalar.activation(gel[j % 2], conv[j % 2][:, 1, :], ACT.Gelu_apprx_tanh).then_inc(gelu_done, 1)

            def h_split(j):
                act.wait_ge(h_done, j + 1)
                nc.scalar.activation(S_hi[:, j, :], hh[j % 2], ACT.Copy).then_inc(h_hi, 1)

            for step in ORDER:
                if step[0] == "split":
                    split(step[1])
                elif step[0] == "turn":
                    turn(step[1])
                elif step[0] == "evac":
                    evac(step[1])
                elif step[0] == "soft":
                    soft(step[1])
                elif step[0] == "pt":
                    pt(step[1])
                elif step[0] == "gelu":
                    gelu(step[1])
                elif step[0] == "h_split":
                    h_split(step[1])
                elif step[0] == "small_split":
                    act.wait_ge(small_in, 16)
                    nc.scalar.activation(wsm_hi[:], wsm, ACT.Copy).then_inc(wsm_hi_done, 1)
                elif step[0] == "tables":
                    act.wait_ge(ang_done, 1)
                    for i, a in enumerate((cos_arg, sin_arg)):
                        nc.scalar.activation(tab64[:, i, :, :], a[:, :, 0:32], ACT.Sin)
                        last = nc.scalar.activation(tab256[:, i, :, :], a[:, :, 32:160], ACT.Sin)
                    last.then_inc(tab_done, 1)
                elif step[0] == "norm_rest":
                    l, tt = step[1], step[2]
                    act.wait_ge(nmr_ready, 2 * l + tt + 1)
                    nc.scalar.activation(res[:, tt, :], res[:, tt, :], ACT.Identity, scale=rstd[:, tt:tt + 1],
                                         bias=nmr[:, tt:tt + 1]).then_inc(x_norm, 1)

        @block.vector
        def _(dve):
            chained = [0]

            def link(ins):
                chained[0] += 1
                ins.then_inc(dve_chain, 1)
                dve.wait_ge(dve_chain, chained[0])

            def split(u):
                n = unit_size(u)
                dve.wait_ge(hi_done, u + 1)
                if u >= RING:
                    dve.wait_ge(w_used, u - RING + 1)
                nc.vector.tensor_tensor(w_lo[:, u % RING, 0:n], raw[:, u % RAW, 0:n],
                                        w_hi[:, u % RING, 0:n].bitcast(F32), ALU.subtract).then_inc(lo_done, 1)

            def turn(n):
                if TJ[n]["split"]:
                    hi, lo, src = t_dest(n)
                    dve.wait_ge(t_hi, RANK[n] + 1)
                    nc.vector.tensor_tensor(lo, src, hi.bitcast(F32), ALU.subtract).then_inc(t_lo, 1)

            def rope(c):
                ch = CH[c]
                kind = ch["evac"][0]
                heads, d = (512 // ch["evac"][3], ch["evac"][3]) if kind == "rope" else (1, 64) if kind == "rope_kpe" else (4, 64)
                b0, half, r = ch["bank"], d // 2, ROT.index(c)
                tab = tab64 if d == 64 else tab256
                if r == 0:
                    dve.wait_ge(tab_done, 1)
                if ROT_READ[c] is not None:
                    dve.wait_ge(t_ready, RANK[ROT_READ[c]] + 1)
                if r >= 1:
                    dve.wait_ge(rot_ready, NT * r)
                if kind == "mla_q":
                    dve.wait_ge(qn_copied, 1 + (ch["name"] == "mlaq1"))
                for tt in range(NT):
                    if kind == "rope_kpe":
                        x = acc[:, b0, tt * 64:(tt + 1) * 64]
                    else:
                        x = acc[:, b0 + tt + (2 if kind == "mla_q" else 0), 0:heads * d]
                    x = x.rearrange("p (h e i) -> p h e i", h=heads, e=2)
                    o = rot[:, tt, 0:heads * d].rearrange("p (h e i) -> p h e i", h=heads, e=2)
                    w = rtmp[:, tt, 0:heads * d].rearrange("p (h e i) -> p h e i", h=heads, e=2)
                    cos, sin = tab[:, 0, tt, :], tab[:, 1, tt, :]
                    nc.vector.tensor_tensor(o, x, cos.unsqueeze(1).unsqueeze(1).to_broadcast([P, heads, 2, half]), ALU.mult)
                    sb_ = sin.unsqueeze(1).to_broadcast([P, heads, half])
                    nc.vector.tensor_tensor(w[:, :, 0, :], x[:, :, 1, :], sb_, ALU.mult)
                    last = nc.vector.tensor_tensor(w[:, :, 1, :], x[:, :, 0, :], sb_, ALU.mult)
                    last.then_inc(rot_prod if tt == 0 else evac_dve, 1)

            def evac(c):
                ch = CH[c]
                e, b0 = ch["evac"], ch["bank"]
                kind = e[0]
                if ch["who"] != "dve":
                    return
                if kind != "conv":
                    wait_acc(dve, c)
                    after_waits(dve, ch)
                if kind in ("rope", "rope_kpe", "mla_q"):
                    rope(c)
                elif kind == "gate":
                    dve.wait_ge(th_done, GATE.index(c) + 1)
                    nc.vector.scalar_tensor_tensor(gate[:, e[1], :, :], gate[:, e[1], :, :], 1.0, acc[:, b0:b0 + 2, :],
                                                   ALU.add, ALU.mult).then_inc(evac_dve, 1)
                elif kind == "norm":
                    l = e[1]
                    for tt in range(NT):
                        last = nc.vector.scalar_tensor_tensor(
                            res[:, tt, :].rearrange("p (b n) -> p b n", b=2), res[:, tt, :].rearrange("p (b n) -> p b n", b=2),
                            ALPHA1 if l < 2 else ALPHA2, acc[:, 2 * tt:2 * tt + 2, :], ALU.mult, ALU.add)
                        if tt == 0:
                            link(last)
                        else:
                            last.then_inc(evac_dve, 1)
                            dve.wait_ge(evac_dve, ch["count"])
                        for x in range(2):
                            last = nc.vector.bn_stats(stats[:, tt, x, :], res[:, tt, x * 512:(x + 1) * 512])
                        link(last)
                        link(nc.vector.bn_aggr(mv[:, tt, :], stats[:, tt, :, :]))
                        nc.vector.tensor_scalar(rstd_in[:, tt:tt + 1], mv[:, tt, 1:2], LN_EPS, None, ALU.add)\
                            .then_inc(pow_in, 1)
                elif kind == "rms":
                    dve.wait_ge(sq_done, 1)
                    dve.wait_ge(rg_in, 16)
                    nc.vector.tensor_scalar(rstd_in[:, 0:4], ssq, 1.0 / 256, RMS_EPS, ALU.mult, ALU.add).then_inc(pow_in, 1)
                    dve.wait_ge(pow_done, POW.index(("rms",)) + 1)
                    for tt in range(NT):
                        for x in range(2):
                            v = slice(x * 256, (x + 1) * 256)
                            last = nc.vector.tensor_scalar(rot[:, tt, v], acc[:, b0 + tt, v],
                                                           rstd[:, 2 * tt + x:2 * tt + x + 1], None, ALU.mult)
                    last.then_inc(evac_dve, 1)
                    dve.wait_ge(evac_dve, ch["count"])
                    for tt in range(NT):
                        nc.vector.tensor_tensor(rot[:, tt, :], rot[:, tt, :], rgain, ALU.mult).then_inc(mn_ready, 1)
                elif kind == "forget":
                    dve.wait_ge(bf_in, 16)
                    dve.wait_ge(half_ready, 1)
                    for tt in range(NT):
                        last = nc.vector.tensor_tensor(lf[:, tt, 0, :], acc[:, b0, tt * 64:tt * 64 + 8], bforget, ALU.add)
                    last.then_inc(z_ready, 1)
                    dve.wait_ge(ln_ready, 3)
                    dve.wait_ge(z_ready, 1)
                    link(nc.vector.scalar_tensor_tensor(lf[:, :, 2, :], lf[:, :, 0, :], 0.0, lf[:, :, 1, :], ALU.min, ALU.subtract))
                    for tt in range(NT):
                        for x, f in ((0, 1.0 / SCALE_64), (1, -1.0 / SCALE_64)):
                            for g in range(2):
                                dst = lfx[:, tt, g, :].rearrange("p (i c) -> p i c", c=32)[:, :, x]
                                last = nc.vector.tensor_scalar(dst, lf[:, tt, 2, 4 * g:4 * g + 4], f, None, ALU.mult)
                    last.then_inc(evac_dve, 1)
                elif kind == "conv":
                    j = e[1]
                    dve.wait_ge(tap_act, j + 1)
                    for lag in (1, 2):
                        for i in range(2):
                            o = conv[j % 2][:, i, lag:S]
                            last = nc.vector.scalar_tensor_tensor(o, acc[:, b0, i * S:i * S + S - lag],
                                                                  cvp[:, 2 - lag, i, j:j + 1], o, ALU.mult, ALU.add)
                        if lag == 1:
                            link(last)
                    last.then_inc(evac_dve, 1)

            def soft(j):
                jb = JOBS[j]
                b = j % 2
                dve.wait_ge(sc_ready, j + 1)
                if j >= 2:
                    dve.wait_ge(pt_ready, j - 1)
                sc = job[:, b, 0:3 * P]
                scale = SCALE_MLA if jb["kind"] == "mla" else SCALE_64
                if jb["kind"] == "band":
                    h = jb["h"]
                    nc.vector.scalar_tensor_tensor(pr[:, b, 0:P], sc[:, 0:P], scale, bias[:, h, P:S], ALU.mult, ALU.add)
                    link(nc.vector.scalar_tensor_tensor(pr[:, b, P:3 * P], sc[:, P:3 * P], scale, bias[:, h, :], ALU.mult, ALU.add))
                else:
                    link(nc.vector.scalar_tensor_tensor(pr[:, b, :], sc, scale, const("causal"), ALU.mult, ALU.add))
                nc.vector.tensor_reduce(neg_max[:, b, 0:1], pr[:, b, 0:P], AX_X, ALU.max, negate=True)
                nc.vector.tensor_reduce(neg_max[:, b, 1:2], pr[:, b, P:3 * P], AX_X, ALU.max, negate=True)\
                    .then_inc(max_done, 1)

            def pv(j):
                jb = JOBS[j]
                b, dv, h = j % 2, jb["dv"], jb["h"]
                per = P // dv
                gated = jb["kind"] in ("mla", "moba")
                dve.wait_ge(exp_done, j + 1)
                if j >= 1:
                    dve.wait_ge(y_done, j)
                if gated:
                    link(nc.vector.tensor_scalar(rdbl, rsum[:, b, :], 2.0, None, ALU.mult))
                link(nc.vector.reciprocal(rinv, rdbl if gated else rsum[:, b, :]))
                dve.wait_ge(o_ready, j + 1)
                slot = Y_SLOT[j]
                first = Y_BEFORE.get(j)
                if first is not None:
                    dve.wait_ge(t_ready, RANK[first] + 1)
                if gated:
                    wait_chunk_evac(dve, [n for n in jb["needs"] if n.startswith("mg")][0])
                for tt in range(NT):
                    o = yb[:, slot, tt, (j % per) * dv:(j % per + 1) * dv]
                    x = job[:, 3, tt * P:tt * P + dv]
                    if gated:
                        last = nc.vector.scalar_tensor_tensor(o, x, rinv[:, tt:tt + 1], gate[:, jb["s"], tt, h * dv:(h + 1) * dv],
                                                              ALU.mult, ALU.mult)
                    else:
                        last = nc.vector.tensor_scalar(o, x, rinv[:, tt:tt + 1], None, ALU.mult)
                last.then_inc(y_done, 1)

            def h_split(j):
                dve.wait_ge(h_hi, j + 1)
                nc.vector.tensor_tensor(S_lo[:, j, :], hh[j % 2], S_hi[:, j, :].bitcast(F32), ALU.subtract).then_inc(h_lo, 1)

            def tables():
                dve.wait_ge(pos_in, 16)
                link(nc.vector.tensor_copy(posf, posi[:]))
                freq = cst[:, CONST["inv64"][0]:CONST["inv256"][1]]
                for tt in range(NT):
                    last = nc.vector.tensor_scalar(ang[:, tt, :], freq, posf[:, tt:tt + 1], None, ALU.mult)
                link(last)
                link(nc.vector.tensor_scalar(turns, ang, 1.0 / TWO_PI, MAGIC, ALU.mult, ALU.add))
                link(nc.vector.tensor_scalar(turns, turns, MAGIC, None, ALU.subtract))
                for cc in (C1, C2, C3):
                    link(nc.vector.scalar_tensor_tensor(ang, turns, -cc, ang, ALU.mult, ALU.add))
                nc.vector.tensor_scalar(sin_arg, ang, PI_SAFE, -PI_SAFE, ALU.min, ALU.max)
                link(nc.vector.tensor_scalar(cos_arg, ang, PI_HALF, None, ALU.add))
                link(nc.vector.tensor_scalar(wrap, cos_arg, PI_SAFE, -TWO_PI, ALU.is_gt, ALU.mult))
                link(nc.vector.tensor_tensor(cos_arg, cos_arg, wrap, ALU.add))
                nc.vector.tensor_scalar(cos_arg, cos_arg, PI_SAFE, -PI_SAFE, ALU.min, ALU.max).then_inc(ang_done, 1)

            def norm_rest(l, tt):
                dve.wait_ge(pow_done, POW.index(("norm", l, tt)) + 1)
                nc.vector.scalar_tensor_tensor(nmr[:, tt:tt + 1], mv[:, tt, 0:1], -1.0, rstd[:, tt:tt + 1],
                                               ALU.mult, ALU.mult).then_inc(nmr_ready, 1)

            def norm_gain(l, tt):
                dve.wait_ge(x_norm, 2 * l + tt + 1)
                dve.wait_ge(ln_g_in, 16 * (l + 1))
                nc.vector.tensor_tensor(res[:, tt, :], res[:, tt, :], gb[:, 0, :], ALU.mult).then_inc(x_gain, 1)

            def ret_s(r):
                dve.wait_ge(rs_ready, r + 1)
                dve.wait_ge(o_ready, 24)
                if r >= 2:
                    dve.wait_ge(ro_ready, r - 1)
                if r == 0:
                    dve.wait_ge(even_in, 16)
                nc.vector.tensor_tensor(ptb[:, r % 2, 0:S], job[:, 0, 0:S], decay[:, r, :], ALU.mult)
                nc.vector.tensor_tensor(ptb[:, r % 2, S:S + P], job[:, 0, S:S + P], decay[:, r, 0:P], ALU.mult)\
                    .then_inc(rp_done, 1)

            def ret_o(r):
                dve.wait_ge(ro_ready, r + 1)
                for tt in range(NT):
                    last = nc.vector.bn_stats(stats[:, tt, 0, :], job[:, 1 + tt, :])
                link(last)
                for tt in range(NT):
                    last = nc.vector.bn_aggr(mv[:, tt, :], stats[:, tt, 0, :])
                link(last)
                nc.vector.tensor_scalar(rstd_in[:, 0:2], mv[:, :, 1], LN_EPS, 4.0, ALU.add, ALU.mult).then_inc(pow_in, 1)
                dve.wait_ge(pow_done, POW.index(("ret", r)) + 1)
                if r >= 1:
                    dve.wait_ge(t_ready, RANK[RET_TURN[r - 1]] + 1)
                for tt in range(NT):
                    last = nc.vector.tensor_scalar(ryb[:, tt, :], job[:, 1 + tt, :], mv[:, tt, 0:1], rstd[:, tt:tt + 1],
                                                   ALU.subtract, ALU.mult)
                link(last)
                wait_chunk_evac(dve, f"rg{r}")
                nc.vector.tensor_tensor(ryb[:, :, :], ryb[:, :, :], gate[:, 1 - r % 2, :, :], ALU.mult).then_inc(ry_done, 1)

            for step in ORDER:
                if step[0] == "split":
                    split(step[1])
                elif step[0] == "turn":
                    turn(step[1])
                elif step[0] == "evac":
                    evac(step[1])
                elif step[0] == "soft":
                    soft(step[1])
                elif step[0] == "pv":
                    pv(step[1])
                elif step[0] == "h_split":
                    h_split(step[1])
                elif step[0] == "small_split":
                    dve.wait_ge(wsm_hi_done, 1)
                    nc.vector.tensor_tensor(wsm_lo[:], wsm, wsm_hi[:].bitcast(F32), ALU.subtract).then_inc(wsm_lo_done, 1)
                elif step[0] == "tables":
                    tables()
                elif step[0] == "norm_rest":
                    norm_rest(step[1], step[2])
                    if step[2] == 1:
                        norm_gain(step[1], 0)
                        norm_gain(step[1], 1)
                elif step[0] == "cum":
                    dve.wait_ge(cum_ready, 1)
                    p0, p1 = const("pick0"), const("pick1")
                    rows = job[:, 0, :].rearrange("p (g s) -> p g s", g=2)
                    nc.vector.tensor_scalar(cumA, rows, p0, p1, ALU.mult, ALU.add).then_inc(cum_done, 1)
                    nc.vector.tensor_scalar(cumB, rows, p1, p0, ALU.mult, ALU.add).then_inc(cum_done, 1)
                    dve.wait_ge(bias_in, 16)
                    band = const("band").unsqueeze(1).to_broadcast([P, 8, P])
                    link(nc.vector.tensor_tensor(bias[:, :, P:S], bias[:, :, P:S], band, ALU.add))
                elif step[0] == "ret_s":
                    ret_s(step[1])
                elif step[0] == "ret_o":
                    ret_o(step[1])

        @block.gpsimd
        def _(pool):
            nc.gpsimd.memset(half_neg, -0.5).then_inc(pool_chain, 1)
            nc.gpsimd.memset(vv[1][:, :, 0:256], 0.0).then_inc(half_ready, 1)
            pool.wait_ge(pool_chain, 1)

            def power(key, a, b):
                i = POW.index(key)
                pool.wait_ge(pow_in, i + 1)
                nc.gpsimd.tensor_tensor(rstd[:, a:b], rstd_in[:, a:b], half_neg[:, 0:b - a], ALU.pow).then_inc(pow_done, 1)

            def rope(c):
                ch = CH[c]
                kind, r = ch["evac"][0], ROT.index(c)
                heads, d = (512 // ch["evac"][3], ch["evac"][3]) if kind == "rope" else (1, 64) if kind == "rope_kpe" else (4, 64)
                for tt in range(NT):
                    if tt == 0:
                        pool.wait_ge(rot_prod, r + 1)
                    else:
                        pool.wait_ge(evac_dve, ch["count"])
                    o = rot[:, tt, 0:heads * d].rearrange("p (h e i) -> p h e i", h=heads, e=2)
                    w = rtmp[:, tt, 0:heads * d].rearrange("p (h e i) -> p h e i", h=heads, e=2)
                    if kind == "rope_kpe":
                        o2 = rot[:, tt, 64:128].rearrange("p (h e i) -> p h e i", h=1, e=2)
                        nc.gpsimd.tensor_tensor(o2[:, :, 0, :], o[:, :, 0, :], w[:, :, 0, :], ALU.subtract)
                        nc.gpsimd.tensor_tensor(o2[:, :, 1, :], o[:, :, 1, :], w[:, :, 1, :], ALU.add)
                    nc.gpsimd.tensor_tensor(o[:, :, 0, :], o[:, :, 0, :], w[:, :, 0, :], ALU.subtract)
                    nc.gpsimd.tensor_tensor(o[:, :, 1, :], o[:, :, 1, :], w[:, :, 1, :], ALU.add).then_inc(rot_ready, 1)

            for step in ORDER:
                if step[0] == "evac":
                    e = CH[step[1]]["evac"]
                    if e[0] == "norm":
                        for tt in range(NT):
                            power(("norm", e[1], tt), tt, tt + 1)
                    elif e[0] == "rms":
                        power(("rms",), 0, 4)
                    elif e[0] in ("rope", "rope_kpe", "mla_q"):
                        rope(step[1])
                elif step[0] == "ret_o":
                    power(("ret", step[1]), 0, 2)
                elif step[0] == "gelu":
                    j = step[1]
                    pool.wait_ge(gelu_done, j + 1)
                    if j >= 2:
                        pool.wait_ge(h_lo, j - 1)
                    nc.gpsimd.tensor_tensor(hh[j % 2], conv[j % 2][:, 0, :], gel[j % 2], ALU.mult).then_inc(h_done, 1)
                elif step[0] == "load" and step[1] == "ln":
                    l = step[2]
                    pool.wait_ge(*((y_done, 16), (x_ready, 2), (ry_done, 4), (y_done, 40))[l])
                    pool.dma_start(gb[:, 0, :], t["ln_gain"][l].partition_broadcast(P)).then_inc(ln_g_in, 16)
                    pool.dma_start(gb[:, 1, :], t["ln_bias"][l].partition_broadcast(P)).then_inc(ln_b_in, 16)
                elif step == ("load", "even"):
                    pool.wait_ge(y_done, 16)
                    pool.dma_start(rgain, t["rms_gain"].partition_broadcast(P)).then_inc(rg_in, 16)
                elif step[0] == "norm_rest":
                    l, tt = step[1], step[2]
                    pool.wait_ge(x_gain, 2 * l + tt + 1)
                    pool.wait_ge(ln_b_in, 16 * (l + 1))
                    nc.gpsimd.tensor_tensor(res[:, tt, :], res[:, tt, :], gb[:, 1, :], ALU.add).then_inc(x_ready, 1)


def lay_out(inputs):
    a = {k: np.asarray(v) for k, v in inputs.items()}
    w = np.zeros((NU, P, UNIT), np.float32)
    for u, (c, i) in enumerate(UNITS):
        ch = CH[c]
        name, rows, cols = ch["pick"]
        key = name if name in ("w_in", "w_out", "w_up", "w_down") else name + "_2"
        m = a[key][0]
        per = {"A": 4, "F": 8, "B": 2, "Q1": 2, "Q2": 2}[ch["kind"]]
        if rows is None:
            rows = list(range(m.shape[0] // P))
        part = rows[i * per:(i + 1) * per]
        m = m if cols is None else m[:, cols]
        block = m.reshape(m.shape[0] // P, P, -1)[part].transpose(1, 0, 2).reshape(P, -1)
        w[u, :, 0:block.shape[1]] = block
    small = np.concatenate([a["w_in"][0][:, FA:FA + 8], a["w_in_even_2"][0][:, MKR:MKR + 64]], 1)
    at = np.minimum(P + np.arange(P)[:, None] - np.arange(S)[None, :], 128) + 128
    cw = np.concatenate([a["conv_w"][0], a["conv_b"]], 0)
    return {
        "w": w,
        "const": constants(),
        "decay": decay_table(),
        "x": a["x"],
        "w_small": small.reshape(KT, P, 72).transpose(1, 0, 2),
        "b_forget": a["b_forget"][0],
        "bias": a["rel_bias"][0][:, at].transpose(1, 0, 2),
        "conv": cw.reshape(4, 2, FT, P).transpose(3, 0, 1, 2),
        "positions_2": a["positions_2"].reshape(NT, P).T,
        "rms_gain": np.concatenate([a["q_norm_even_2"][0], a["kv_norm_even_2"][0]]),
        "ln_gain": np.stack([a["ln1_g"][0], a["ln2_g"][0], a["ln_g_2"][0], a["ln_g_2"][1]]),
        "ln_bias": np.stack([a["ln1_b"][0], a["ln2_b"][0], a["ln_b_2"][0], a["ln_b_2"][1]]),
    }


def kernel(**inputs):
    import concourse.bacc as _bacc
    from concourse.bass_utils import run_bass_kernel_spmd as _run

    nc = _bacc.Bacc("TRN2", target_bir_lowering=False, num_devices=1)
    arrays, t = {}, {}
    for name, a in lay_out(inputs).items():
        a = np.ascontiguousarray(a)
        arrays[f"in_{name}"] = a
        t[name] = nc.dram_tensor(f"in_{name}", a.shape, mybir.dt.from_np(a.dtype), kind="ExternalInput").ap()
    t["out"] = nc.dram_tensor("out_0", (1, S, D), F32, kind="ExternalOutput").ap()
    build(nc, t)
    r = _run(nc, [arrays], core_ids=[0])
    return r.results[0]["out_0"]
```

```python
from contextlib import ExitStack

import numpy as np

import concourse.bass as bass
from concourse import mybir

ALU = mybir.AluOpType
ACT = mybir.ActivationFunctionType
AX_X = mybir.AxisListType.X
F32 = mybir.dt.float32
F32R = mybir.dt.float32r
I32 = mybir.dt.int32

P = 128
S = 256
NT = S // P
D = 1024
KT = D // P
DFF = 2816
FT = DFF // P
PIECE = 1024
RING = 6
RAW = 5
AHEAD = 4
LATE = 4
NEG = -1e30
LN_EPS = 1e-5
RMS_EPS = 1e-6
ALPHA1 = 2.0 ** 0.25
ALPHA2 = 4.0 ** 0.25
HD = 64
SCALE_64 = HD ** -0.5
SCALE_MLA = 192 ** -0.5
MAGIC = 12582912.0
TWO_PI = 6.283185307179586
PI_HALF = 1.5707963267948966
PI_SAFE = 3.1415925
C1 = 6.28125
C2 = float(np.float32(0.0019350051879882812))
C3 = TWO_PI - C1 - C2

QA, KA, VA, FA, QB, KB, VB = 0, 512, 1024, 1536, 1544, 2056, 2568
RQ, RK, RV, RG, MQ, MKV, MKR, MG = 0, 1024, 2048, 4096, 6144, 6400, 6656, 6720


def chunks():
    out = []

    def add(name, kind, n_units, src, tiles, who, evac, pick, **kw):
        out.append(dict(name=name, kind=kind, n=n_units, src=src, tiles=tiles, who=who, evac=evac, pick=pick, **kw))

    k8 = list(range(KT))

    def cols(c0, n):
        return list(range(c0, c0 + n))

    def feat(name, c0, s, half):
        add(f"{name}{half}", "F", 2, "X", k8, "act", ("copy_feat", name[0], s, half),
            ("w_in", None, cols(c0 + 256 * half, 256)))

    feat("kA", KA, 0, 0)
    feat("qA", QA, 0, 0)
    add("f", "F", 1, "X", k8, "dve", ("forget",), ("w_in", None, None))
    add("vA", "A", 4, "X", k8, "act", ("copy_tok", 0), ("w_in", None, cols(VA, 512)))
    feat("kA", KA, 0, 1)
    feat("qA", QA, 0, 1)
    feat("kB", KB, 1, 0)
    feat("qB", QB, 1, 0)
    add("vB", "A", 4, "X", k8, "act", ("copy_tok", 1), ("w_in", None, cols(VB, 512)))
    feat("kB", KB, 1, 1)
    feat("qB", QB, 1, 1)
    add("out1", "B", 8, "S", k8, "dve", ("norm", 0), ("w_out", k8, None))
    for j in range(FT):
        add(f"up{j}", "F", 2, "X", k8, "dve", ("conv", j),
            ("w_up", None, cols(P * j, P) + cols(DFF + P * j, P)))
    add("down", "B", FT, "S", list(range(FT)), "dve", ("norm", 1), ("w_down", list(range(FT)), None))

    even_perm = list(range(0, 256, 2)) + list(range(1, 256, 2))
    add("mqkv", "C", 8, "X", k8, "dve", ("rms",),
        ("w_in_even", None, cols(MQ, 256) + cols(MKR, 32) + cols(MKV, 256) + cols(MKR + 32, 32)))

    def mla(half):
        add(f"mg{half}", "A", 4, "X", k8, "dve", ("gate", 0), ("w_in_even", None, cols(MG + 512 * half, 512)),
            after_job=16 + 4 * half)
        heads = range(4 * half, 4 * half + 4)
        add(f"mlaq{half}", "Q1", 2, "S", [20, 21], "dve", ("mla_q", half),
            ("w_uq_even", [0, 1], [c for h in heads for c in cols(192 * h, 128)]
             + [c for h in heads for c in cols(192 * h + 128, 64)]), after_job=16 + 4 * half)
        add(f"mlakv{half}", "Q2", 2, "S", [22, 23], "act", ("mla_kv", half),
            ("w_ukv_even", [0, 1], [c for h in heads for c in cols(256 * h, 128)]
             + [c for h in heads for c in cols(256 * h + 128, 128)]), after_job=16 + 4 * half)

    def ret_qk(pair):
        for name, c0 in (("k", RK), ("q", RQ)):
            add(f"r{name}{pair}", "A", 4, "X", k8, "dve", ("rope", name, 1 - pair, 256),
                ("w_in_even", None, [c0 + 256 * h + c for h in (2 * pair, 2 * pair + 1) for c in even_perm]),
                after_job=24 * pair)

    def ret_vg(r):
        s = 1 - r % 2
        add(f"rv{r}", "A", 4, "X", k8, "act", ("copy_tok", s), ("w_in_even", None, cols(RV + 512 * r, 512)),
            after_ret=max(r - 1, 0), after_job=24 if r == 1 else 0)
        add(f"rg{r}", "A", 4, "X", k8, "dve", ("gate", s), ("w_in_even", None, cols(RG + 512 * r, 512)),
            after_ret=max(r - 1, 0), after_job=24 if r == 1 else 0)

    mla(0)
    ret_qk(0)
    mla(1)
    for r in (0, 1):
        ret_vg(r)
    ret_qk(1)
    for r in (2, 3):
        ret_vg(r)
    add("out2", "B", 24, "S", list(range(24)), "dve", ("norm", 2), ("w_out_even", list(range(16, 24)) + list(range(16)), None))

    for half in (0, 1):
        s = 1 - half
        for name, c0 in (("k", 1024), ("q", 0)):
            add(f"m{name}{half}", "A", 4, "X", k8, "dve", ("rope", name, s, 64), ("w_in_odd", None, cols(c0 + 512 * half, 512)),
                after_ret=4)
        add(f"mv{half}", "A", 4, "X", k8, "act", ("copy_tok", s), ("w_in_odd", None, cols(2048 + 512 * half, 512)),
            after_ret=4)
        add(f"mgt{half}", "A", 4, "X", k8, "dve", ("gate", s), ("w_in_odd", None, cols(3072 + 512 * half, 512)),
            after_ret=4)
    add("out3", "B", 8, "S", k8, "dve", ("norm", 3), ("w_out_odd", k8, None))

    width = dict(F=1, A=2, B=4, C=4, Q1=4, Q2=4)
    at, held, n_act, n_dve, u = 0, [None] * 4, 0, 0, 0
    for c, ch in enumerate(out):
        w = width[ch["kind"]]
        at = (at + w - 1) // w * w % 4
        ch["bank"], ch["before"] = at, sorted({held[b] for b in range(at, at + w)} - {None})
        for b in range(at, at + w):
            held[b] = c
        at = (at + w) % 4
        ch["u0"] = u
        u += ch["n"]
        if ch["who"] == "act":
            n_act += 1
        else:
            n_dve += 1
        ch["count"] = n_act if ch["who"] == "act" else n_dve
    return out


CH = chunks()
BY = {ch["name"]: i for i, ch in enumerate(CH)}
PIECES = [(c, i) for c, ch in enumerate(CH) for i in range(ch["n"])]
NU = len(PIECES)


def piece_size(u):
    c, i = PIECES[u]
    return 576 if CH[c]["kind"] == "C" else 512 if (CH[c]["kind"], i) == ("Q1", 1) else PIECE


JOBS = []
for h in range(8):
    JOBS.append(dict(kind="fox", s=0, h=h, needs=["vA", "f", f"kA{h // 4}", f"qA{h // 4}"]))
for h in range(8):
    JOBS.append(dict(kind="band", s=1, h=h, needs=["vB", f"kB{h // 4}", f"qB{h // 4}"]))
for h in range(8):
    JOBS.append(dict(kind="mla", s=0, h=h % 4, needs=[f"mlaq{h // 4}", f"mlakv{h // 4}", f"mg{h // 4}"]))
for h in range(16):
    JOBS.append(dict(kind="moba", s=1 - h // 8, h=h % 8, needs=[f"m{x}{h // 8}" for x in ("k", "q", "v", "gt")]))
for j, job in enumerate(JOBS):
    job["dv"] = 128 if job["kind"] == "mla" else 64

TJ = []


def new_t(src, dst, split, bank, needs, tiles=1):
    TJ.append(dict(src=src, dst=dst, split=split, bank=bank, needs=needs, tiles=tiles))
    return len(TJ) - 1


def plan():
    order, given, pending, deferred = [], set(), [], []
    state = dict(split=0, wait=0)

    def emit(step, *gives):
        order.append(step)
        given.update(gives)

    def background():
        if pending and pending[0][0] <= given:
            _, steps, gives = pending.pop(0)
            for st in steps:
                emit(st)
            given.update(gives)

    def require(names):
        while not names <= given:
            if deferred and not pending[0][0] <= given:
                flush_turns()
            need, steps, gives = pending.pop(0)
            assert need <= given, (names - given, need - given)
            for st in steps:
                emit(st)
            given.update(gives)

    def split_to(u):
        while state["split"] < min(u, NU):
            emit(("split", state["split"]))
            state["split"] += 1

    def flush_turns():
        while deferred:
            name = deferred.pop()
            rope_turns(name)
            given.add(name)
            state["wait"] = 0

    def evacuate(c):
        name, kind = CH[c]["name"], CH[c]["evac"][0]
        if kind in ("rope", "mla_q", "rms"):
            flush_turns()
        emit(("evac", c))
        if kind in ("rope", "mla_q"):
            deferred.append(name)
            state["wait"] = 4
        else:
            given.add(name)

    def run(name, rate, needs=lambda i: set(), before_last=()):
        c = BY[name]
        ch = CH[c]
        n = ch["n"]
        late = LATE if ch["kind"] == "B" else 0
        halves = [(i, part) for i in range(n - late) for part in (0, 1)]
        halves += [(i, part) for part in (0, 1) for i in range(n - late, n)]
        for x, (i, part) in enumerate(halves):
            u = ch["u0"] + i
            require(needs(i))
            if x == len(halves) - 1:
                for st in before_last:
                    emit(st)
            emit(("mm", u, part))
            if late and part == 0 and i == n - 1:
                emit(("norm_first", ch["evac"][1]))
            if late and i >= n - late and part == 0:
                split_to(ch["u0"] + n - late + AHEAD)
            elif part == 0 or late:
                split_to(u + AHEAD + 1)
            if deferred:
                state["wait"] -= 1
                if state["wait"] == 0:
                    flush_turns()
            if x == len(halves) - 1:
                evacuate(c)
            for _ in range(rate):
                background()

    def rope_turns(name):
        kind = CH[BY[name]]["evac"]
        if kind[0] == "rope":
            tiles, dst = 4, ("attn", kind[1], kind[2])
        else:
            tiles, dst = 2, ("qpe",)
        for i in range(0, tiles, 2):
            emit(("turn", new_t(("rot", i), dst + (i,), False, 3, BY[name], 2)))

    def attention(jobs):
        n = len(jobs)
        for i in range(n + 3):
            steps, need, gives = [], set(), set()
            if i >= 3:
                j = jobs[i - 3]
                job = JOBS[j]
                per = P // job["dv"]
                if (j + 1) % per == 0:
                    tile = (j % 16 if job["kind"] in ("fox", "band") else j - 16 if job["kind"] == "mla" else j - 24) // per
                    steps.append(("turn", new_t(("y", j), ("S", tile), True, 3, j)))
                    gives.add(f"{'L1' if j < 16 else 'L2' if j < 24 else 'L3'}y{tile}")
            if i < n:
                need = set(JOBS[jobs[i]]["needs"])
                steps += [("scores", jobs[i]), ("soft", jobs[i])]
            pending.append((need, steps, gives))
            steps = []
            if 1 <= i <= n:
                steps += [("pt", jobs[i - 1])]
            if 2 <= i <= n + 1:
                steps += [("pv", jobs[i - 2])]
            if steps:
                pending.append((set(), steps, set()))

    def retention(r):
        s = set([f"rk{r // 2}", f"rq{r // 2}"])
        pending.append((s, [("ret_s", r)], set()))
        pending.append((s | {f"rv{r}", f"rg{r}"}, [("ret_o", r)], set()))
        for i in (0, 2):
            t = new_t(("ry", r, i), ("S", 8 + 4 * r + i), True, 3, r, 2)
            pending.append((set(), [("turn", t)], {f"L2y{8 + 4 * r + i}", f"L2y{9 + 4 * r + i}"}))

    def turn_x(base):
        for t in range(NT):
            if base:
                emit(("norm_rest", base - 1, t))
            for q in range(2):
                emit(("turn", new_t(("x", t, q), ("X", t, q), True, 2 * t + q, base)))

    emit(("load", "start"))
    turn_x(0)
    split_to(AHEAD)

    for name in ("kA0", "qA0", "f"):
        run(name, 0)
    run("vA", 0)
    attention(range(0, 8))
    for name in ("kA1", "qA1", "kB0", "qB0"):
        run(name, 1)
    run("vB", 1)
    attention(range(8, 16))
    for name in ("kB1", "qB1"):
        run(name, 1)
    run("out1", 1, lambda i: {f"L1y{i}"}, [("load", "ln", 0)])
    turn_x(1)
    for j in range(FT + 2):
        if j < FT:
            run(f"up{j}", 0)
        if 1 <= j <= FT:
            emit(("gelu", j - 1))
        if j >= 2:
            emit(("h_split", j - 2))
    emit(("tables",))
    run("down", 0, before_last=[("load", "ln", 1)])
    turn_x(2)

    emit(("load", "even"))
    run("mqkv", 0)
    run("mg0", 0)
    emit(("turn", new_t(("kpe", 0), ("kpe", 0), False, 3, 0)))
    for i in (0, 2):
        emit(("turn", new_t(("mn", i), ("S", 20 + i), True, 3, 0, 2)))
    for name in ("mlaq0", "mlakv0"):
        run(name, 0)
    attention(range(16, 20))
    for name in ("rk0", "rq0"):
        run(name, 1)
    require({"L2y3"})
    run("mg1", 0)
    for name in ("mlaq1", "mlakv1"):
        run(name, 0)
    attention(range(20, 24))
    retention(0)
    run("rv0", 1)
    run("rg0", 1)
    retention(1)
    require({"L2y7"})
    for name in ("rv1", "rg1"):
        run(name, 1)
    for name in ("rk1", "rq1"):
        run(name, 1)
    retention(2)
    require({"L2y15"})
    for name in ("rv2", "rg2"):
        run(name, 1)
    retention(3)
    run("rv3", 1)
    require({"L2y19"})
    run("rg3", 1)
    run("out2", 1, lambda i: {f"L2y{i}"}, [("load", "ln", 2)])
    turn_x(3)

    for name in ("mk0", "mq0", "mv0", "mgt0"):
        run(name, 0)
    attention(range(24, 32))
    for name in ("mk1", "mq1", "mv1", "mgt1"):
        run(name, 1)
    attention(range(32, 40))
    run("out3", 1, lambda i: {f"L3y{i}"}, [("load", "ln", 3)])
    emit(("norm_rest", 3, 0))
    emit(("norm_rest", 3, 1))
    emit(("store",))
    assert not pending, pending
    return order


ORDER = plan()
assert [s[1] for s in ORDER if s[0] == "evac"] == list(range(len(CH)))
RANK = {n: i for i, n in enumerate(s[1] for s in ORDER if s[0] == "turn")}
SPLITS = [s[1] for s in ORDER if s[0] == "turn" and TJ[s[1]]["split"]]
SPLIT_RANK = {n: i for i, n in enumerate(SPLITS)}
BANKS = dict(scores=lambda n: [n % 2], pt=lambda n: [2], pv=lambda n: [3], turn=lambda n: [TJ[n]["bank"]],
             ret_s=lambda n: [0], ret_o=lambda n: [1, 2])
BANK_BEFORE = {}
_last = {}
for _s in ORDER:
    if _s[0] in BANKS:
        _banks = BANKS[_s[0]](_s[-1])
        BANK_BEFORE[_s] = sorted({_last[b] for b in _banks if b in _last})
        _last.update({b: _s for b in _banks})
FILLED = {}
_seen = {}
for _s in ORDER:
    if _s[0] == "turn":
        d = TJ[_s[1]]["dst"]
        if d[0] == "S":
            for _i in range(TJ[_s[1]]["tiles"]):
                _seen[("S", d[1] + _i)] = _s[1]
        elif d[0] == "X":
            _seen[d] = _s[1]
        else:
            _seen[d[:3] if d[0] == "attn" else d[:1]] = _s[1]
    elif _s[0] in ("mm", "scores", "ret_s"):
        FILLED[_s] = dict(_seen)
Y_TURN = {TJ[n]["src"][1]: n for n in RANK if TJ[n]["src"][0] == "y"}
_tiles = sorted(Y_TURN)
Y_SLOT = {j: i % 2 for i, j in enumerate(_tiles)}
Y_BEFORE = {}
for _i, _j in enumerate(_tiles):
    for _k in range(_j - P // JOBS[_j]["dv"] + 1, _j + 1):
        Y_SLOT[_k] = _i % 2
        if _i >= 2:
            Y_BEFORE[_k] = Y_TURN[_tiles[_i - 2]]
ROT_READ, _r = {}, None
for _s in ORDER:
    if _s[0] == "turn" and TJ[_s[1]]["src"][0] in ("rot", "mn", "kpe"):
        _r = _s[1]
    elif _s[0] == "evac":
        ROT_READ[_s[1]] = _r
RET_TURN = {r: max((n for n in RANK if TJ[n]["src"][:2] == ("ry", r)), key=RANK.get) for r in range(4)}

CONST = {}
_at = 0
for _name, _n in (("ident", P), ("causal", 3 * P), ("band", P), ("cumA", 4), ("cumB", 4),
                  ("inv64", 32), ("inv256", 128)):
    CONST[_name] = (_at, _at + _n)
    _at += _n
NCONST = _at


def constants():
    c = np.zeros((P, NCONST), np.float32)

    def put(name, a):
        c[:, CONST[name][0]:CONST[name][1]] = a

    q, k = np.arange(P)[:, None], np.arange(P)[None, :]
    tri = np.where(k <= q, 0.0, NEG).astype(np.float32)
    put("ident", np.eye(P, dtype=np.float32))
    put("causal", np.concatenate([tri, np.zeros((P, P), np.float32), tri], 1))
    put("band", np.where(k // 64 <= q // 64, 0.0, NEG).astype(np.float32))
    r = np.arange(P)[:, None] % 32
    g = np.arange(2)[None, :]
    big = np.float32(1.0 / SCALE_64)
    put("cumA", np.concatenate([(r == 2 * g) * big, (r == 2 * g + 1) * np.float32(1)], 1))
    put("cumB", np.concatenate([(r == 2 * g + 1) * -big, (r == 2 * g) * np.float32(1)], 1))
    put("inv64", (1.0 / (np.float32(10000.0) ** (np.arange(0, 64, 2, dtype=np.float32) / np.float32(64)))).astype(np.float32)[None, :])
    put("inv256", (1.0 / (np.float32(10000.0) ** np.linspace(0, 1, 128, dtype=np.float32))).astype(np.float32)[None, :])
    return c


def decay_table():
    g = 1.0 - 2.0 ** (-5.0 - np.arange(4, dtype=np.float64))
    d = np.arange(S)[None, :] - np.arange(P)[:, None]
    t = np.where(d[None] >= 0, g[:, None, None] ** np.maximum(d, 0)[None], 0.0) / 16.0
    return np.ascontiguousarray(t.transpose(1, 0, 2)).astype(np.float32)


def build(nc, t):
    with ExitStack() as ctx:
        def sb(name, shape, dt=F32):
            return ctx.enter_context(nc.sbuf_tensor(name, shape, dt))

        def sem(name):
            return ctx.enter_context(nc.semaphore(name))

        raw = sb("raw", [P, RAW, PIECE])
        w_hi = sb("w_hi", [P, RING, PIECE], F32R)
        w_lo = sb("w_lo", [P, RING, PIECE], F32R)
        X_hi = sb("X_hi", [P, KT, S], F32R)
        X_lo = sb("X_lo", [P, KT, S], F32R)
        S_hi = sb("S_hi", [P, 24, S], F32R)
        S_lo = sb("S_lo", [P, 24, S], F32R)
        res = sb("res", [P, NT, D])
        decay = sb("decay", [P, 4, S])
        ryb = sb("ryb", [P, NT, 512])
        cst = sb("cst", [P, NCONST])
        qT = [sb(f"qT{s}", [P, 4, S]) for s in (0, 1)]
        kT = [sb(f"kT{s}", [P, 4, S]) for s in (0, 1)]
        vv = [sb(f"v{s}", [P, NT, 512]) for s in (0, 1)]
        gate = sb("gate", [P, 2, NT, 512])
        qpeT = sb("qpeT", [P, 2, S])
        kpeT = sb("kpeT", [P, 1, S])
        rot = sb("rot", [P, NT, 512])
        rtmp = sb("rtmp", [P, NT, 512])
        pr = sb("pr", [P, 2, 3 * P])
        ptb = sb("ptb", [P, 2, 3 * P])
        yb = sb("yb", [P, 2, NT, P])
        small = sb("small", [P, 96])
        tab64 = sb("tab64", [P, 2, NT, 32])
        tab256 = sb("tab256", [P, 2, NT, 128])
        cvp = sb("cvp", [P, 4, 2, FT])
        posi = sb("posi", [P, NT], I32)
        cumA = rot[:, 0, :].rearrange("p (g s) -> p g s", g=2)
        cumB = rot[:, 1, :].rearrange("p (g s) -> p g s", g=2)

        acc = ctx.enter_context(nc.psum_tensor("acc", [P, 4, 512], F32))
        job = ctx.enter_context(nc.psum_tensor("job", [P, 4, 512], F32))

        fox = rtmp[:, :, :].rearrange("p t (a s) -> p (t a) s", a=2)
        bias = gate[:, :, :, :].rearrange("p s t n -> p (s t n)").rearrange("p (h k) -> p h k", h=8)
        conv = [vv[b][:, 0, :].rearrange("p (i s) -> p i s", i=2) for b in (0, 1)]
        gel = [vv[b][:, 1, 0:256] for b in (0, 1)]
        hh = [vv[b][:, 1, 256:512] for b in (0, 1)]
        gb = gate[:, :, :, :].rearrange("p s t n -> p s (t n)")
        rgain = pr[:, :, :].rearrange("p b n -> p (b n)")[:, 0:512]
        ang = qT[0][:, 0:2, 0:160]
        turns = qT[0][:, 2:4, 0:160]
        wrap = qT[1][:, 0:2, 0:160]
        sin_arg = kT[0][:, 0:2, 0:160]
        cos_arg = kT[0][:, 2:4, 0:160]
        posf = small[:, 90:92]
        bforget = small[:, 80:81]
        neg_max = small[:, 0:4].rearrange("p (b t) -> p b t", b=2)
        rsum = small[:, 64:70].rearrange("p (b t) -> p b t", b=3)
        rinv = small[:, 8:10]
        rdbl = small[:, 10:12]
        stats = small[:, 12:36].rearrange("p (t q s) -> p t q s", t=2, q=2)
        mv = small[:, 36:40].rearrange("p (t a) -> p t a", t=2)
        rstd_in = small[:, 40:44]
        rstd = small[:, 44:48]
        half_neg = small[:, 48:52]
        ssq = small[:, 56:60]

        def const(name):
            a, b = CONST[name]
            return cst[:, a:b]

        ident = const("ident")

        landed = [sem(f"landed{i}") for i in range(RAW)]
        hi_done, lo_done, w_used = sem("hi_done"), sem("lo_done"), sem("w_used")
        evac_act, evac_dve = sem("evac_act"), sem("evac_dve")
        t_ready, t_hi, t_lo = sem("t_ready"), sem("t_hi"), sem("t_lo")
        sc_ready, max_done, exp_done = sem("sc_ready"), sem("max_done"), sem("exp_done")
        pt_ready, pt_copied, o_ready, y_done = sem("pt_ready"), sem("pt_copied"), sem("o_ready"), sem("y_done")
        const_in, ident_in, bias_in = sem("const_in"), sem("ident_in"), sem("bias_in")
        x_in = [sem(f"x_in{i}") for i in range(2 * NT)]
        pos_in, bf_in, conv_in = sem("pos_in"), sem("bf_in"), sem("conv_in")
        ln_g_in, ln_b_in, even_in, rg_in = sem("ln_g_in"), sem("ln_b_in"), sem("even_in"), sem("rg_in")
        first_done = sem("first_done")
        ang_done, sin_done, tab_done = sem("ang_done"), sem("sin_done"), sem("tab_done")
        z_ready, ln_ready = sem("z_ready"), sem("ln_ready")
        tap_act, tap_dve, gelu_done, h_done, h_hi, h_lo = (sem("tap_act"), sem("tap_dve"), sem("gelu_done"),
                                                           sem("h_done"), sem("h_hi"), sem("h_lo"))
        pow_done, x_ready = sem("pow_done"), sem("x_ready")
        pow_in = sem("pow_in")
        mn_ready = sem("mn_ready")
        sq_done = sem("sq_done")
        half_ready = sem("half_ready")
        th_done = sem("th_done")
        rot_prod, rot_ready = sem("rot_prod"), sem("rot_ready")
        rs_ready, rp_done, ro_ready, ry_done = sem("rs_ready"), sem("rp_done"), sem("ro_ready"), sem("ry_done")
        stored = sem("stored")
        qn_copied, kpe_prod = sem("qn_copied"), sem("kpe_prod")
        dve_chain, act_chain, pool_chain = sem("dve_chain"), sem("act_chain"), sem("pool_chain")

        block = ctx.enter_context(nc.Block())

        ROT = [c for c, ch in enumerate(CH) if ch["evac"][0] in ("rope", "rms", "mla_q")]
        ROPES = [c for c in ROT if CH[c]["evac"][0] != "rms"]
        GATE = [c for c, ch in enumerate(CH) if ch["evac"][0] == "gate"]
        POW = []
        for s_ in ORDER:
            if s_[0] == "norm_first":
                POW.append(("norm", s_[1], 0))
            elif s_[0] == "evac" and CH[s_[1]]["evac"][0] == "norm":
                POW.append(("norm", CH[s_[1]]["evac"][1], 1))
            elif s_[0] == "evac" and CH[s_[1]]["evac"][0] == "rms":
                POW.append(("rms",))
            elif s_[0] == "ret_o":
                POW.append(("ret", s_[1]))

        def chunk_waits(eng, c):
            for b in CH[c]["before"]:
                eng.wait_ge(evac_act if CH[b]["who"] == "act" else evac_dve, CH[b]["count"])

        def wait_chunk_evac(eng, name):
            ch = CH[BY[name]]
            eng.wait_ge(evac_act if ch["who"] == "act" else evac_dve, ch["count"])

        def after_waits(eng, ch):
            if ch.get("after_job"):
                eng.wait_ge(y_done, ch["after_job"])
            if ch.get("after_ret"):
                eng.wait_ge(ry_done, ch["after_ret"])

        def place(n):
            return job[:, TJ[n]["bank"], :]

        def bank_free(eng, step):
            for before in BANK_BEFORE[step]:
                kind, n = before[0], before[-1]
                if kind == "scores":
                    eng.wait_ge(max_done, n + 1)
                elif kind == "pt":
                    eng.wait_ge(pt_copied, n + 1)
                elif kind == "pv":
                    eng.wait_ge(y_done, n + 1)
                elif kind == "ret_s":
                    eng.wait_ge(rp_done, n + 1)
                elif kind == "ret_o":
                    eng.wait_ge(ry_done, n + 1)
                elif TJ[n]["split"]:
                    eng.wait_ge(t_lo, SPLIT_RANK[n] + 1)
                else:
                    eng.wait_ge(t_hi, RANK[n] + 1)

        @block.sync
        def _(sp):
            def load_piece(u):
                n = piece_size(u)
                if u >= RAW:
                    sp.wait_ge(lo_done, u - RAW + 1)
                sp.dma_start(raw[:, u % RAW, 0:n], t["w"][u, :, 0:n]).then_inc(landed[u % RAW], 16)

            for step in ORDER:
                if step == ("load", "start"):
                    sp.dma_start(ident, t["const"][:, 0:P]).then_inc(ident_in, 16)
                    for i in range(2 * NT):
                        tt, q = divmod(i, 2)
                        sp.dma_start(res[:, tt, q * 512:(q + 1) * 512],
                                     t["x"][0, tt * P:(tt + 1) * P, q * 512:(q + 1) * 512]).then_inc(x_in[i], 16)
                    for u in range(RAW):
                        load_piece(u)
                        if u == 2:
                            sp.dma_start(cst[:, P:], t["const"][:, P:]).then_inc(const_in, 16)
                            sp.dma_start(bforget, t["b_forget"]).then_inc(bf_in, 16)
                    sp.dma_start(bias[:, :, :], t["bias"]).then_inc(bias_in, 16)
                    sp.dma_start(posi[:], t["positions_2"]).then_inc(pos_in, 16)
                    sp.dma_start(cvp[:], t["conv"]).then_inc(conv_in, 16)
                    sp.dma_start(decay[:], t["decay"]).then_inc(even_in, 16)
                elif step[0] == "split":
                    if step[1] + RAW < NU:
                        load_piece(step[1] + RAW)
                elif step == ("store",):
                    for i in range(2 * NT):
                        tt, q = divmod(i, 2)
                        sp.wait_ge(x_ready, 2 * NT * 3 + i + 1)
                        sp.dma_start(t["out"][0, tt * P:(tt + 1) * P, q * 512:(q + 1) * 512],
                                     res[:, tt, q * 512:(q + 1) * 512]).then_inc(stored, 16)
            sp.wait_ge(stored, 16 * 2 * NT)

        @block.tensor
        def _(pe):
            def three(out, a_hi, a_lo, b_hi, b_lo, start, stop):
                nc.tensor.matmul(out, a_hi, b_hi, start=start, stop=False)
                nc.tensor.matmul(out, a_hi, b_lo, start=False, stop=False)
                return nc.tensor.matmul(out, a_lo, b_hi, start=False, stop=stop)

            def wait_operand(step, ch, keys):
                seen = FILLED[step]
                if ch["name"] == "down":
                    pe.wait_ge(h_lo, max(k[1] for k in keys) + 1)
                else:
                    pe.wait_ge(t_lo, max(SPLIT_RANK[seen[k]] for k in keys) + 1)

            def mm(step):
                u, part = step[1], step[2]
                c, i = PIECES[u]
                ch = CH[c]
                hi, lo = (X_hi, X_lo) if ch["src"] == "X" else (S_hi, S_lo)
                wh, wl = w_hi[:, u % RING, :], w_lo[:, u % RING, :]
                kind, b0, tiles = ch["kind"], ch["bank"], ch["tiles"]
                if i == 0 and part == 0:
                    chunk_waits(pe, c)
                if part == 0:
                    pe.wait_ge(lo_done, u + 1)
                last = None
                if kind == "F":
                    wait_operand(step, ch, [("X", tt, part) for tt in range(NT)])
                    for k in range(4 * part, 4 * part + 4):
                        w = slice(k * P, (k + 1) * P)
                        last = three(acc[:, b0, i * S:(i + 1) * S], wh[:, w], wl[:, w], hi[:, k, :], lo[:, k, :],
                                     k == 0, k == KT - 1)
                elif kind == "A":
                    x = 2 * i + part
                    k = tiles[x]
                    wait_operand(step, ch, [("X", tt, k // 4) for tt in range(NT)])
                    w = slice(part * 512, (part + 1) * 512)
                    for tt in range(NT):
                        last = three(acc[:, b0 + tt, :], hi[:, k, tt * P:(tt + 1) * P], lo[:, k, tt * P:(tt + 1) * P],
                                     wh[:, w], wl[:, w], x == 0, x == len(tiles) - 1)
                elif kind in ("B", "C"):
                    k, tt = tiles[i], part
                    wait_operand(step, ch, [("X", tt, k // 4)] if ch["src"] == "X" else [("S", k)])
                    n = 512 if kind == "B" else 288
                    for nn in range(2):
                        w = slice(nn * n, (nn + 1) * n)
                        last = three(acc[:, b0 + tt * 2 + nn, 0:n], hi[:, k, tt * P:(tt + 1) * P],
                                     lo[:, k, tt * P:(tt + 1) * P], wh[:, w], wl[:, w], i == 0, i == len(tiles) - 1)
                    if kind == "B" and part == 0 and i == ch["n"] - 1:
                        last.then_inc(first_done, 1)
                elif i == 0:
                    wait_operand(step, ch, [("S", k) for k in tiles])
                    for f in (2 * part, 2 * part + 1):
                        for x, k in enumerate(tiles):
                            w = slice(x * 512 + f * P, x * 512 + f * P + P)
                            last = three(acc[:, b0 + f // 2, (f % 2) * S:(f % 2 + 1) * S], wh[:, w], wl[:, w],
                                         hi[:, k, :], lo[:, k, :], x == 0, x == 1)
                else:
                    n = 256 if kind == "Q1" else 512
                    for x, k in enumerate(tiles):
                        w = slice(x * n, x * n + n)
                        last = three(acc[:, b0 + 2 + part, 0:n], hi[:, k, part * P:(part + 1) * P],
                                     lo[:, k, part * P:(part + 1) * P], wh[:, w], wl[:, w], x == 0, x == 1)
                if part == 1:
                    last.then_inc(w_used, 1)

            def scores(step):
                j = step[1]
                jb = JOBS[j]
                s, h = jb["s"], jb["h"]
                for name in jb["needs"]:
                    if CH[BY[name]]["evac"][0] not in ("gate", "rope", "forget"):
                        wait_chunk_evac(pe, name)
                bank_free(pe, step)
                out = job[:, j % 2, :]
                blocks = [(out[:, 0:P], 0, P), (out[:, P:3 * P], 1, S)]
                seen = FILLED[step]
                if jb["kind"] in ("mla", "moba"):
                    keys = [("qpe",), ("kpe",)] if jb["kind"] == "mla" else [("attn", "q", s), ("attn", "k", s)]
                    pe.wait_ge(t_hi, max(RANK[seen[k]] for k in keys) + 1)
                for dst, tt, nk in blocks:
                    q = slice(tt * P, (tt + 1) * P)
                    if jb["kind"] == "mla":
                        lo_p = 64 * (h % 2)
                        nc.tensor.matmul(dst, qT[s][:, h, q], kT[s][:, h, 0:nk], start=True, stop=False)
                        last = nc.tensor.matmul(dst, qpeT[lo_p:lo_p + 64, h // 2, q], kpeT[lo_p:lo_p + 64, 0, 0:nk],
                                                start=False, stop=True)
                    else:
                        lo_p = 64 * (h % 2)
                        fox = jb["kind"] == "fox"
                        last = nc.tensor.matmul(dst, qT[s][lo_p:lo_p + 64, h // 2, q], kT[s][lo_p:lo_p + 64, h // 2, 0:nk],
                                                start=True, stop=not fox)
                        if fox:
                            wait_chunk_evac(pe, "f")
                            r = 32 * (h % 4)
                            last = nc.tensor.matmul(dst, cumA[r:r + 4, h // 4, q], cumB[r:r + 4, h // 4, 0:nk],
                                                    start=False, stop=True)
                last.then_inc(sc_ready, 1)

            def pt(step):
                j = step[1]
                pe.wait_ge(exp_done, j + 1)
                bank_free(pe, step)
                for b in range(3):
                    last = nc.tensor.transpose(job[:, 2, b * P:(b + 1) * P], pr[:, j % 2, b * P:(b + 1) * P], ident)
                last.then_inc(pt_ready, 1)

            def pv(step):
                j = step[1]
                jb = JOBS[j]
                s, h, dv = jb["s"], jb["h"], jb["dv"]
                pe.wait_ge(pt_copied, j + 1)
                bank_free(pe, step)
                b = ptb[:, j % 2, :]
                v = slice(h * dv, (h + 1) * dv)
                nc.tensor.matmul(job[:, 3, 0:dv], b[:, 0:P], vv[s][:, 0, v], start=True, stop=True)
                nc.tensor.matmul(job[:, 3, P:P + dv], b[:, P:2 * P], vv[s][:, 0, v], start=True, stop=False)
                nc.tensor.matmul(job[:, 3, P:P + dv], b[:, 2 * P:3 * P], vv[s][:, 1, v], start=False, stop=True)\
                    .then_inc(o_ready, 1)

            def turn(step):
                n = step[1]
                tj = TJ[n]
                kind = tj["src"][0]
                bank_free(pe, step)
                out = place(n)
                if kind == "x":
                    _, tt, q = tj["src"]
                    if tj["needs"] == 0:
                        pe.wait_ge(x_in[2 * tt + q], 16)
                        pe.wait_ge(ident_in, 16)
                    else:
                        pe.wait_ge(x_ready, 2 * NT * (tj["needs"] - 1) + 2 * tt + q + 1)
                    for i in range(4):
                        k = 4 * q + i
                        last = nc.tensor.transpose(out[:, i * P:(i + 1) * P], res[:, tt, k * P:(k + 1) * P], ident)
                else:
                    for tt in range(NT):
                        if kind == "rot":
                            pe.wait_ge(rot_ready, NT * ROT.index(tj["needs"]) + tt + 1)
                            src = rot[:, tt, tj["src"][1] * P:]
                        elif kind == "kpe":
                            pe.wait_ge(rot_ready, NT * ROT.index(BY["mqkv"]) + tt + 1)
                            src = ryb[:, tt, 0:P]
                        elif kind == "mn":
                            pe.wait_ge(mn_ready, tt + 1)
                            src = rot[:, tt, tj["src"][1] * P:]
                        elif kind == "y":
                            pe.wait_ge(y_done, tj["src"][1] + 1)
                            src = yb[:, Y_SLOT[tj["src"][1]], tt, :]
                        else:
                            pe.wait_ge(ry_done, tj["src"][1] + 1)
                            src = ryb[:, tt, tj["src"][2] * P:]
                        for i in range(tj["tiles"]):
                            last = nc.tensor.transpose(out[:, i * S + tt * P:i * S + (tt + 1) * P],
                                                       src[:, i * P:(i + 1) * P], ident)
                last.then_inc(t_ready, 1)

            def ret_s(step):
                r = step[1]
                s = 1 - r // 2
                seen = FILLED[step]
                pe.wait_ge(t_hi, max(RANK[seen[("attn", "q", s)]], RANK[seen[("attn", "k", s)]]) + 1)
                bank_free(pe, step)
                b = 2 * (r % 2)
                for e in range(2):
                    nc.tensor.matmul(job[:, 0, 0:S], kT[s][:, b + e, 0:P], qT[s][:, b + e, :], start=e == 0, stop=e == 1)
                for e in range(2):
                    last = nc.tensor.matmul(job[:, 0, S:S + P], kT[s][:, b + e, P:S], qT[s][:, b + e, P:S],
                                            start=e == 0, stop=e == 1)
                last.then_inc(rs_ready, 1)

            def ret_o(step):
                r = step[1]
                s = 1 - r % 2
                wait_chunk_evac(pe, f"rv{r}")
                pe.wait_ge(rp_done, r + 1)
                bank_free(pe, step)
                b = ptb[:, r % 2, :]
                nc.tensor.matmul(job[:, 1, :], b[:, 0:P], vv[s][:, 0, :], start=True, stop=True)
                nc.tensor.matmul(job[:, 2, :], b[:, P:2 * P], vv[s][:, 0, :], start=True, stop=False)
                nc.tensor.matmul(job[:, 2, :], b[:, 2 * P:3 * P], vv[s][:, 1, :], start=False, stop=True)\
                    .then_inc(ro_ready, 1)

            for step in ORDER:
                if step[0] == "mm":
                    mm(step)
                elif step[0] == "scores":
                    scores(step)
                elif step[0] == "pt":
                    pt(step)
                elif step[0] == "pv":
                    pv(step)
                elif step[0] == "turn":
                    turn(step)
                elif step[0] == "ret_s":
                    ret_s(step)
                elif step[0] == "ret_o":
                    ret_o(step)

        def wait_acc(eng, c):
            eng.wait_ge(w_used, CH[c]["u0"] + CH[c]["n"])

        def t_dest(n):
            tj = TJ[n]
            d, p = tj["dst"], place(n)
            if d[0] == "X":
                _, tt, q = d
                v = slice(tt * P, (tt + 1) * P)
                return (X_hi[:, 4 * q:4 * q + 4, v], X_lo[:, 4 * q:4 * q + 4, v], p.rearrange("p (k s) -> p k s", k=4))
            nt = tj["tiles"]
            src = p[:, 0:nt * S].rearrange("p (k s) -> p k s", k=nt)
            at = slice(d[-1], d[-1] + nt)
            if d[0] == "S":
                return S_hi[:, at, :], S_lo[:, at, :], src
            if d[0] == "qpe":
                return qpeT[:, at, :], None, src
            if d[0] == "kpe":
                return kpeT[:, at, :], None, src
            return (qT if d[1] == "q" else kT)[d[2]][:, at, :], None, src

        @block.scalar
        def _(act):
            def split(u):
                n = piece_size(u)
                act.wait_ge(landed[u % RAW], 16 * (u // RAW + 1))
                if u >= RING:
                    act.wait_ge(w_used, u - RING + 1)
                nc.scalar.activation(w_hi[:, u % RING, 0:n], raw[:, u % RAW, 0:n], ACT.Copy).then_inc(hi_done, 1)

            def turn(n):
                hi, _, src = t_dest(n)
                act.wait_ge(t_ready, RANK[n] + 1)
                nc.scalar.activation(hi, src, ACT.Copy).then_inc(t_hi, 1)

            def evac(c):
                ch = CH[c]
                e, b0 = ch["evac"], ch["bank"]
                kind = e[0]
                if kind in ("rope", "norm"):
                    return
                if kind != "conv":
                    wait_acc(act, c)
                    after_waits(act, ch)
                if kind == "copy_feat":
                    _, which, s, half = e
                    dst = (qT if which == "q" else kT)[s][:, 2 * half:2 * half + 2, :]
                    nc.scalar.activation(dst, acc[:, b0, :].rearrange("p (a s) -> p a s", a=2), ACT.Copy)\
                        .then_inc(evac_act, 1)
                elif kind == "copy_tok":
                    nc.scalar.activation(vv[e[1]][:, :, :], acc[:, b0:b0 + 2, :], ACT.Copy).then_inc(evac_act, 1)
                elif kind == "mla_kv":
                    nc.scalar.activation(kT[0][:, :, :], acc[:, b0:b0 + 2, :].rearrange("p b (a s) -> p (b a) s", a=2), ACT.Copy)
                    nc.scalar.activation(vv[0][:, :, :], acc[:, b0 + 2:b0 + 4, :], ACT.Copy).then_inc(evac_act, 1)
                elif kind == "mla_q":
                    nc.scalar.activation(qT[0][:, :, :], acc[:, b0:b0 + 2, :].rearrange("p b (a s) -> p (b a) s", a=2), ACT.Copy)\
                        .then_inc(qn_copied, 1)
                elif kind == "gate":
                    nc.scalar.activation(gate[:, e[1], :, :], acc[:, b0:b0 + 2, :], ACT.Tanh, scale=0.5).then_inc(th_done, 1)
                elif kind == "rms":
                    act.wait_ge(kpe_prod, NT)
                    for tt in range(NT):
                        for x in range(2):
                            last = nc.scalar.activation(rtmp[:, tt, x * 256:(x + 1) * 256],
                                                        acc[:, b0 + 2 * tt + x, 0:256], ACT.Square,
                                                        accum_out=ssq[:, 2 * tt + x:2 * tt + x + 1])
                    last.then_inc(sq_done, 1)
                elif kind == "forget":
                    act.wait_ge(z_ready, 1)
                    for i, (a, f, kw) in enumerate(((0, ACT.Abs, {}), (1, ACT.Exp, dict(scale=-1.0)),
                                                    (1, ACT.Ln, dict(bias=1.0)))):
                        nc.scalar.activation(fox[:, 1, :], fox[:, a, :], f, **kw).then_inc(ln_ready, 1)
                        act.wait_ge(ln_ready, i + 1)
                elif kind == "conv":
                    j = e[1]
                    wait_acc(act, c)
                    if j == 0:
                        act.wait_ge(conv_in, 16)
                    if j >= 2:
                        act.wait_ge(h_done, j - 1)
                    for i in range(2):
                        last = nc.scalar.activation(conv[j % 2][:, i, :], acc[:, b0, i * S:(i + 1) * S], ACT.Identity,
                                                    scale=cvp[:, 2, i, j:j + 1], bias=cvp[:, 3, i, j:j + 1])
                    last.then_inc(tap_act, 1)

            def soft(j):
                act.wait_ge(max_done, j + 1)
                if j >= 3:
                    act.wait_ge(y_done, j - 2)
                b = j % 2
                nc.scalar.activation(pr[:, b, 0:P], pr[:, b, 0:P], ACT.Exp, bias=neg_max[:, b, 0:1],
                                     accum_out=rsum[:, j % 3, 0:1])
                nc.scalar.activation(pr[:, b, P:3 * P], pr[:, b, P:3 * P], ACT.Exp, bias=neg_max[:, b, 1:2],
                                     accum_out=rsum[:, j % 3, 1:2]).then_inc(exp_done, 1)

            def pt(j):
                act.wait_ge(pt_ready, j + 1)
                if j >= 2:
                    act.wait_ge(o_ready, j - 1)
                if j in (24, 25):
                    act.wait_ge(ro_ready, 4)
                nc.scalar.activation(ptb[:, j % 2, :], job[:, 2, 0:3 * P], ACT.Copy).then_inc(pt_copied, 1)

            def gelu(j):
                act.wait_ge(evac_dve, CH[BY[f"up{j}"]]["count"])
                nc.scalar.activation(gel[j % 2], conv[j % 2][:, 1, :], ACT.Gelu_apprx_tanh).then_inc(gelu_done, 1)

            def h_split(j):
                act.wait_ge(h_done, j + 1)
                nc.scalar.activation(S_hi[:, j, :], hh[j % 2], ACT.Copy).then_inc(h_hi, 1)

            for step in ORDER:
                if step[0] == "split":
                    split(step[1])
                elif step[0] == "turn":
                    turn(step[1])
                elif step[0] == "evac":
                    evac(step[1])
                elif step[0] == "soft":
                    soft(step[1])
                elif step[0] == "pt":
                    pt(step[1])
                elif step[0] == "gelu":
                    gelu(step[1])
                elif step[0] == "h_split":
                    h_split(step[1])
                elif step[0] == "tables":
                    act.wait_ge(ang_done, 1)
                    for i, a in enumerate((cos_arg, sin_arg)):
                        nc.scalar.activation(tab64[:, i, :, :], a[:, :, 0:32], ACT.Sin)
                        last = nc.scalar.activation(tab256[:, i, :, :], a[:, :, 32:160], ACT.Sin)
                    last.then_inc(tab_done, 1)

        @block.vector
        def _(dve):
            chained = [0]

            def link(ins):
                chained[0] += 1
                ins.then_inc(dve_chain, 1)
                dve.wait_ge(dve_chain, chained[0])

            def split(u):
                n = piece_size(u)
                dve.wait_ge(hi_done, u + 1)
                if u >= RING:
                    dve.wait_ge(w_used, u - RING + 1)
                nc.vector.tensor_tensor(w_lo[:, u % RING, 0:n], raw[:, u % RAW, 0:n],
                                        w_hi[:, u % RING, 0:n].bitcast(F32), ALU.subtract).then_inc(lo_done, 1)

            def turn(n):
                if TJ[n]["split"]:
                    hi, lo, src = t_dest(n)
                    dve.wait_ge(t_hi, RANK[n] + 1)
                    nc.vector.tensor_tensor(lo, src, hi.bitcast(F32), ALU.subtract).then_inc(t_lo, 1)

            def rope(c):
                ch = CH[c]
                kind = ch["evac"][0]
                heads, d = (512 // ch["evac"][3], ch["evac"][3]) if kind == "rope" else (1, 64) if kind == "rms" else (4, 64)
                b0, half, r = ch["bank"], d // 2, ROT.index(c)
                tab = tab64 if d == 64 else tab256
                if r == 0:
                    dve.wait_ge(tab_done, 1)
                if ROT_READ[c] is not None and kind != "rms":
                    dve.wait_ge(t_ready, RANK[ROT_READ[c]] + 1)
                if r >= 1:
                    dve.wait_ge(rot_ready, NT * r)
                if kind == "mla_q":
                    dve.wait_ge(qn_copied, 1 + (ch["name"] == "mlaq1"))
                for tt in range(NT):
                    if kind == "rms":
                        x = acc[:, b0 + 2 * tt:b0 + 2 * tt + 2, 256:288].unsqueeze(1)
                        o = ryb[:, tt, 0:64].rearrange("p (h e i) -> p h e i", h=1, e=2)
                        w = ryb[:, tt, P:P + 64].rearrange("p (h e i) -> p h e i", h=1, e=2)
                    else:
                        x = acc[:, b0 + tt + (2 if kind == "mla_q" else 0), 0:heads * d].rearrange("p (h e i) -> p h e i", h=heads, e=2)
                        o = rot[:, tt, 0:heads * d].rearrange("p (h e i) -> p h e i", h=heads, e=2)
                        w = rtmp[:, tt, 0:heads * d].rearrange("p (h e i) -> p h e i", h=heads, e=2)
                    cos, sin = tab[:, 0, tt, :], tab[:, 1, tt, :]
                    nc.vector.tensor_tensor(o, x, cos.unsqueeze(1).unsqueeze(1).to_broadcast([P, heads, 2, half]), ALU.mult)
                    sb_ = sin.unsqueeze(1).to_broadcast([P, heads, half])
                    nc.vector.tensor_tensor(w[:, :, 0, :], x[:, :, 1, :], sb_, ALU.mult)
                    last = nc.vector.tensor_tensor(w[:, :, 1, :], x[:, :, 0, :], sb_, ALU.mult)
                    last.then_inc(kpe_prod if kind == "rms" else rot_prod if tt == 0 else evac_dve, 1)

            def evac(c):
                ch = CH[c]
                e, b0 = ch["evac"], ch["bank"]
                kind = e[0]
                if ch["who"] != "dve":
                    return
                if kind != "conv":
                    wait_acc(dve, c)
                    after_waits(dve, ch)
                if kind in ("rope", "mla_q"):
                    rope(c)
                elif kind == "gate":
                    dve.wait_ge(th_done, GATE.index(c) + 1)
                    nc.vector.scalar_tensor_tensor(gate[:, e[1], :, :], gate[:, e[1], :, :], 1.0, acc[:, b0:b0 + 2, :],
                                                   ALU.add, ALU.mult).then_inc(evac_dve, 1)
                elif kind == "norm":
                    norm(c, 1)
                elif kind == "rms":
                    rope(c)
                    dve.wait_ge(sq_done, 1)
                    dve.wait_ge(rg_in, 16)
                    nc.vector.tensor_scalar(rstd_in[:, 0:4], ssq, 1.0 / 256, RMS_EPS, ALU.mult, ALU.add).then_inc(pow_in, 1)
                    dve.wait_ge(pow_done, POW.index(("rms",)) + 1)
                    for tt in range(NT):
                        for x in range(2):
                            v = slice(x * 256, (x + 1) * 256)
                            last = nc.vector.tensor_scalar(rot[:, tt, v], acc[:, b0 + 2 * tt + x, 0:256],
                                                           rstd[:, 2 * tt + x:2 * tt + x + 1], None, ALU.mult)
                    last.then_inc(evac_dve, 1)
                    dve.wait_ge(evac_dve, ch["count"])
                    for tt in range(NT):
                        nc.vector.tensor_tensor(rot[:, tt, :], rot[:, tt, :], rgain, ALU.mult).then_inc(mn_ready, 1)
                elif kind == "forget":
                    dve.wait_ge(bf_in, 16)
                    nc.vector.tensor_scalar(fox[:, 0, :], acc[:, b0, 0:S], bforget, None, ALU.add).then_inc(z_ready, 1)
                    dve.wait_ge(z_ready, 1)
                    dve.wait_ge(ln_ready, 3)
                    link(nc.vector.scalar_tensor_tensor(fox[:, 2, :], fox[:, 0, :], 0.0, fox[:, 1, :], ALU.min, ALU.subtract))
                    dve.wait_ge(half_ready, 1)
                    link(nc.vector.tensor_tensor_scan(fox[:, 0, :], fox[:, 3, :], fox[:, 2, :], 0.0, ALU.mult, ALU.add))
                    dve.wait_ge(const_in, 16)
                    for g in range(2):
                        for o, name in ((cumA, "cumA"), (cumB, "cumB")):
                            k = const(name)
                            last = nc.vector.tensor_scalar(o[:, g, :], fox[:, 0, :], k[:, g:g + 1], k[:, 2 + g:3 + g],
                                                           ALU.mult, ALU.add)
                    last.then_inc(evac_dve, 1)
                elif kind == "conv":
                    j = e[1]
                    dve.wait_ge(tap_act, j + 1)
                    for lag in (1, 2):
                        for i in range(2):
                            o = conv[j % 2][:, i, lag:S]
                            last = nc.vector.scalar_tensor_tensor(o, acc[:, b0, i * S:i * S + S - lag],
                                                                  cvp[:, 2 - lag, i, j:j + 1], o, ALU.mult, ALU.add)
                        if lag == 1:
                            link(last)
                    last.then_inc(evac_dve, 1)

            def soft(j):
                jb = JOBS[j]
                b = j % 2
                dve.wait_ge(sc_ready, j + 1)
                if j >= 2:
                    dve.wait_ge(pt_ready, j - 1)
                sc = job[:, b, 0:3 * P]
                scale = SCALE_MLA if jb["kind"] == "mla" else SCALE_64
                if j == 0:
                    dve.wait_ge(const_in, 16)
                if j == 8:
                    dve.wait_ge(bias_in, 16)
                    band = const("band").unsqueeze(1).to_broadcast([P, 8, P])
                    link(nc.vector.tensor_tensor(bias[:, :, P:S], bias[:, :, P:S], band, ALU.add))
                if jb["kind"] == "band":
                    h = jb["h"]
                    nc.vector.scalar_tensor_tensor(pr[:, b, 0:P], sc[:, 0:P], scale, bias[:, h, P:S], ALU.mult, ALU.add)
                    link(nc.vector.scalar_tensor_tensor(pr[:, b, P:3 * P], sc[:, P:3 * P], scale, bias[:, h, :], ALU.mult, ALU.add))
                else:
                    link(nc.vector.scalar_tensor_tensor(pr[:, b, :], sc, scale, const("causal"), ALU.mult, ALU.add))
                nc.vector.tensor_reduce(neg_max[:, b, 0:1], pr[:, b, 0:P], AX_X, ALU.max, negate=True)
                nc.vector.tensor_reduce(neg_max[:, b, 1:2], pr[:, b, P:3 * P], AX_X, ALU.max, negate=True)\
                    .then_inc(max_done, 1)

            def pv(j):
                jb = JOBS[j]
                b, dv, h = j % 3, jb["dv"], jb["h"]
                per = P // dv
                gated = jb["kind"] in ("mla", "moba")
                dve.wait_ge(exp_done, j + 1)
                if j >= 1:
                    dve.wait_ge(y_done, j)
                if gated:
                    link(nc.vector.tensor_scalar(rdbl, rsum[:, b, :], 2.0, None, ALU.mult))
                link(nc.vector.reciprocal(rinv, rdbl if gated else rsum[:, b, :]))
                dve.wait_ge(o_ready, j + 1)
                slot = Y_SLOT[j]
                first = Y_BEFORE.get(j)
                if first is not None:
                    dve.wait_ge(t_ready, RANK[first] + 1)
                if gated:
                    wait_chunk_evac(dve, [n for n in jb["needs"] if n.startswith("mg")][0])
                for tt in range(NT):
                    o = yb[:, slot, tt, (j % per) * dv:(j % per + 1) * dv]
                    x = job[:, 3, tt * P:tt * P + dv]
                    if gated:
                        last = nc.vector.scalar_tensor_tensor(o, x, rinv[:, tt:tt + 1], gate[:, jb["s"], tt, h * dv:(h + 1) * dv],
                                                              ALU.mult, ALU.mult)
                    else:
                        last = nc.vector.tensor_scalar(o, x, rinv[:, tt:tt + 1], None, ALU.mult)
                last.then_inc(y_done, 1)

            def h_split(j):
                dve.wait_ge(h_hi, j + 1)
                nc.vector.tensor_tensor(S_lo[:, j, :], hh[j % 2], S_hi[:, j, :].bitcast(F32), ALU.subtract).then_inc(h_lo, 1)

            def tables():
                dve.wait_ge(pos_in, 16)
                link(nc.vector.tensor_copy(posf, posi[:]))
                freq = cst[:, CONST["inv64"][0]:CONST["inv256"][1]]
                for tt in range(NT):
                    last = nc.vector.tensor_scalar(ang[:, tt, :], freq, posf[:, tt:tt + 1], None, ALU.mult)
                link(last)
                link(nc.vector.tensor_scalar(turns, ang, 1.0 / TWO_PI, MAGIC, ALU.mult, ALU.add))
                link(nc.vector.tensor_scalar(turns, turns, MAGIC, None, ALU.subtract))
                for cc in (C1, C2, C3):
                    link(nc.vector.scalar_tensor_tensor(ang, turns, -cc, ang, ALU.mult, ALU.add))
                nc.vector.tensor_scalar(sin_arg, ang, PI_SAFE, -PI_SAFE, ALU.min, ALU.max)
                link(nc.vector.tensor_scalar(cos_arg, ang, PI_HALF, None, ALU.add))
                link(nc.vector.tensor_scalar(wrap, cos_arg, PI_SAFE, -TWO_PI, ALU.is_gt, ALU.mult))
                link(nc.vector.tensor_tensor(cos_arg, cos_arg, wrap, ALU.add))
                nc.vector.tensor_scalar(cos_arg, cos_arg, PI_SAFE, -PI_SAFE, ALU.min, ALU.max).then_inc(ang_done, 1)

            def norm(c, tt):
                ch = CH[c]
                l, b = ch["evac"][1], ch["bank"] + 2 * tt
                if tt == 0:
                    dve.wait_ge(first_done, l + 1)
                last = nc.vector.scalar_tensor_tensor(
                    res[:, tt, :].rearrange("p (b n) -> p b n", b=2), res[:, tt, :].rearrange("p (b n) -> p b n", b=2),
                    ALPHA1 if l < 2 else ALPHA2, acc[:, b:b + 2, :], ALU.mult, ALU.add)
                if tt == 0:
                    link(last)
                else:
                    last.then_inc(evac_dve, 1)
                    dve.wait_ge(evac_dve, ch["count"])
                for x in range(2):
                    last = nc.vector.bn_stats(stats[:, tt, x, :], res[:, tt, x * 512:(x + 1) * 512])
                link(last)
                link(nc.vector.bn_aggr(mv[:, tt, :], stats[:, tt, :, :]))
                nc.vector.tensor_scalar(rstd_in[:, tt:tt + 1], mv[:, tt, 1:2], LN_EPS, None, ALU.add).then_inc(pow_in, 1)

            def norm_rest(l, tt):
                dve.wait_ge(ln_g_in, 16 * (l + 1))
                link(nc.vector.scalar_tensor_tensor(res[:, tt, :], res[:, tt, :], mv[:, tt, 0:1], gb[:, 0, :],
                                                    ALU.subtract, ALU.mult))
                dve.wait_ge(ln_b_in, 16 * (l + 1))
                dve.wait_ge(pow_done, POW.index(("norm", l, tt)) + 1)
                for q in range(2):
                    v = slice(q * 512, (q + 1) * 512)
                    nc.vector.scalar_tensor_tensor(res[:, tt, v], res[:, tt, v], rstd[:, tt:tt + 1], gb[:, 1, v],
                                                   ALU.mult, ALU.add).then_inc(x_ready, 1)

            def ret_s(r):
                dve.wait_ge(rs_ready, r + 1)
                dve.wait_ge(o_ready, 24)
                if r >= 2:
                    dve.wait_ge(ro_ready, r - 1)
                if r == 0:
                    dve.wait_ge(even_in, 16)
                nc.vector.tensor_tensor(ptb[:, r % 2, 0:S], job[:, 0, 0:S], decay[:, r, :], ALU.mult)
                nc.vector.tensor_tensor(ptb[:, r % 2, S:S + P], job[:, 0, S:S + P], decay[:, r, 0:P], ALU.mult)\
                    .then_inc(rp_done, 1)

            def ret_o(r):
                dve.wait_ge(ro_ready, r + 1)
                for tt in range(NT):
                    last = nc.vector.bn_stats(stats[:, tt, 0, :], job[:, 1 + tt, :])
                link(last)
                for tt in range(NT):
                    last = nc.vector.bn_aggr(mv[:, tt, :], stats[:, tt, 0, :])
                link(last)
                nc.vector.tensor_scalar(rstd_in[:, 0:2], mv[:, :, 1], LN_EPS, 4.0, ALU.add, ALU.mult).then_inc(pow_in, 1)
                dve.wait_ge(pow_done, POW.index(("ret", r)) + 1)
                if r >= 1:
                    dve.wait_ge(t_ready, RANK[RET_TURN[r - 1]] + 1)
                for tt in range(NT):
                    last = nc.vector.tensor_scalar(ryb[:, tt, :], job[:, 1 + tt, :], mv[:, tt, 0:1], rstd[:, tt:tt + 1],
                                                   ALU.subtract, ALU.mult)
                link(last)
                wait_chunk_evac(dve, f"rg{r}")
                nc.vector.tensor_tensor(ryb[:, :, :], ryb[:, :, :], gate[:, 1 - r % 2, :, :], ALU.mult).then_inc(ry_done, 1)

            for step in ORDER:
                if step[0] == "split":
                    split(step[1])
                elif step[0] == "turn":
                    turn(step[1])
                elif step[0] == "evac":
                    evac(step[1])
                elif step[0] == "soft":
                    soft(step[1])
                elif step[0] == "pv":
                    pv(step[1])
                elif step[0] == "h_split":
                    h_split(step[1])
                elif step[0] == "tables":
                    tables()
                elif step[0] == "norm_first":
                    norm(BY[("out1", "down", "out2", "out3")[step[1]]], 0)
                elif step[0] == "norm_rest":
                    norm_rest(step[1], step[2])
                elif step[0] == "ret_s":
                    ret_s(step[1])
                elif step[0] == "ret_o":
                    ret_o(step[1])

        @block.gpsimd
        def _(pool):
            nc.gpsimd.memset(half_neg, -0.5).then_inc(pool_chain, 1)
            nc.gpsimd.memset(fox[:, 3, :], 1.0).then_inc(half_ready, 1)
            pool.wait_ge(pool_chain, 1)

            def power(key, a, b):
                i = POW.index(key)
                pool.wait_ge(pow_in, i + 1)
                nc.gpsimd.tensor_tensor(rstd[:, a:b], rstd_in[:, a:b], half_neg[:, 0:b - a], ALU.pow).then_inc(pow_done, 1)

            def rope(c):
                ch = CH[c]
                kind, r = ch["evac"][0], ROT.index(c)
                heads, d = (512 // ch["evac"][3], ch["evac"][3]) if kind == "rope" else (1, 64) if kind == "rms" else (4, 64)
                for tt in range(NT):
                    if kind == "rms":
                        pool.wait_ge(kpe_prod, tt + 1)
                    elif tt == 0:
                        pool.wait_ge(rot_prod, ROPES.index(c) + 1)
                    else:
                        pool.wait_ge(evac_dve, ch["count"])
                    if kind == "rms":
                        o = ryb[:, tt, 0:64].rearrange("p (h e i) -> p h e i", h=1, e=2)
                        w = ryb[:, tt, P:P + 64].rearrange("p (h e i) -> p h e i", h=1, e=2)
                        o2 = ryb[:, tt, 64:P].rearrange("p (h e i) -> p h e i", h=1, e=2)
                        nc.gpsimd.tensor_tensor(o2[:, :, 0, :], o[:, :, 0, :], w[:, :, 0, :], ALU.subtract)
                        nc.gpsimd.tensor_tensor(o2[:, :, 1, :], o[:, :, 1, :], w[:, :, 1, :], ALU.add)
                    else:
                        o = rot[:, tt, 0:heads * d].rearrange("p (h e i) -> p h e i", h=heads, e=2)
                        w = rtmp[:, tt, 0:heads * d].rearrange("p (h e i) -> p h e i", h=heads, e=2)
                    nc.gpsimd.tensor_tensor(o[:, :, 0, :], o[:, :, 0, :], w[:, :, 0, :], ALU.subtract)
                    nc.gpsimd.tensor_tensor(o[:, :, 1, :], o[:, :, 1, :], w[:, :, 1, :], ALU.add).then_inc(rot_ready, 1)

            for step in ORDER:
                if step[0] == "evac":
                    e = CH[step[1]]["evac"]
                    if e[0] == "norm":
                        power(("norm", e[1], 1), 1, 2)
                    elif e[0] == "rms":
                        rope(step[1])
                        power(("rms",), 0, 4)
                    elif e[0] in ("rope", "mla_q"):
                        rope(step[1])
                elif step[0] == "norm_first":
                    power(("norm", step[1], 0), 0, 1)
                elif step[0] == "ret_o":
                    power(("ret", step[1]), 0, 2)
                elif step[0] == "gelu":
                    j = step[1]
                    pool.wait_ge(gelu_done, j + 1)
                    if j >= 2:
                        pool.wait_ge(h_lo, j - 1)
                    nc.gpsimd.tensor_tensor(hh[j % 2], conv[j % 2][:, 0, :], gel[j % 2], ALU.mult).then_inc(h_done, 1)
                elif step[0] == "load" and step[1] == "ln":
                    l = step[2]
                    pool.wait_ge(*((y_done, 16), (x_ready, 2 * NT), (ry_done, 4), (y_done, 40))[l])
                    pool.dma_start(gb[:, 0, :], t["ln_gain"][l].partition_broadcast(P)).then_inc(ln_g_in, 16)
                    pool.dma_start(gb[:, 1, :], t["ln_bias"][l].partition_broadcast(P)).then_inc(ln_b_in, 16)
                elif step == ("load", "even"):
                    pool.wait_ge(y_done, 16)
                    pool.dma_start(rgain, t["rms_gain"].partition_broadcast(P)).then_inc(rg_in, 16)


def lay_out(inputs):
    a = {k: np.asarray(v) for k, v in inputs.items()}
    w = np.zeros((NU, P, PIECE), np.float32)
    forget = np.zeros((D, P), np.float32)
    b_forget = np.zeros((P, 1), np.float32)
    for h in range(8):
        for r in (0, 1):
            at = 32 * (h % 4) + 2 * (h // 4) + r
            forget[:, at] = a["w_in"][0][:, FA + h]
            b_forget[at, 0] = a["b_forget"][0][h]
    for u, (c, i) in enumerate(PIECES):
        ch = CH[c]
        name, rows, cols = ch["pick"]
        key = name if name in ("w_in", "w_out", "w_up", "w_down") else name + "_2"
        m = forget if ch["name"] == "f" else a[key][0]
        m = m if cols is None else m[:, cols]
        m = m.reshape(m.shape[0] // P, P, -1)
        if rows is not None:
            m = m[rows]
        kind = ch["kind"]
        if kind == "F":
            block = m[:, :, i * P:(i + 1) * P]
        elif kind == "A":
            block = m[2 * i:2 * i + 2]
        elif kind in ("B", "C"):
            block = m[i:i + 1]
        else:
            block = m[:, :, 0:512] if i == 0 else m[:, :, 512:]
        block = block.transpose(1, 0, 2).reshape(P, -1)
        assert block.shape[1] == piece_size(u)
        w[u, :, 0:block.shape[1]] = block
    at = np.minimum(P + np.arange(P)[:, None] - np.arange(S)[None, :], 128) + 128
    cw = np.concatenate([a["conv_w"][0], a["conv_b"]], 0)
    return {
        "w": w,
        "const": constants(),
        "decay": decay_table(),
        "x": a["x"],
        "b_forget": b_forget,
        "bias": a["rel_bias"][0][:, at].transpose(1, 0, 2),
        "conv": cw.reshape(4, 2, FT, P).transpose(3, 0, 1, 2),
        "positions_2": a["positions_2"].reshape(NT, P).T,
        "rms_gain": np.concatenate([a["q_norm_even_2"][0], a["kv_norm_even_2"][0]]),
        "ln_gain": np.stack([a["ln1_g"][0], a["ln2_g"][0], a["ln_g_2"][0], a["ln_g_2"][1]]),
        "ln_bias": np.stack([a["ln1_b"][0], a["ln2_b"][0], a["ln_b_2"][0], a["ln_b_2"][1]]),
    }


def kernel(**inputs):
    import concourse.bacc as _bacc
    from concourse.bass_utils import run_bass_kernel_spmd as _run

    nc = _bacc.Bacc("TRN2", target_bir_lowering=False, num_devices=1)
    arrays, t = {}, {}
    for name, a in lay_out(inputs).items():
        a = np.ascontiguousarray(a)
        arrays[f"in_{name}"] = a
        t[name] = nc.dram_tensor(f"in_{name}", a.shape, mybir.dt.from_np(a.dtype), kind="ExternalInput").ap()
    t["out"] = nc.dram_tensor("out_0", (1, S, D), F32, kind="ExternalOutput").ap()
    build(nc, t)
    r = _run(nc, [arrays], core_ids=[0])
    return r.results[0]["out_0"]
```

```python
from contextlib import ExitStack

import numpy as np

import concourse.bass as bass
from concourse import mybir

ALU = mybir.AluOpType
ACT = mybir.ActivationFunctionType
AX_X = mybir.AxisListType.X
F32 = mybir.dt.float32
F32R = mybir.dt.float32r
I32 = mybir.dt.int32

P = 128
S = 256
NT = S // P
D = 1024
KT = D // P
DFF = 2816
FT = DFF // P
PIECE = 1024
RING = 6
RAW = 5
AHEAD = 4
LATE = 4
TURN_WAIT = 4
NEG = -1e30
LN_EPS = 1e-5
RMS_EPS = 1e-6
ALPHA1 = 2.0 ** 0.25
ALPHA2 = 4.0 ** 0.25
HD = 64
SCALE_64 = HD ** -0.5
SCALE_MLA = 192 ** -0.5
MAGIC = 12582912.0
TWO_PI = 6.283185307179586
PI_HALF = 1.5707963267948966
PI_SAFE = 3.1415925
C1 = 6.28125
C2 = float(np.float32(0.0019350051879882812))
C3 = TWO_PI - C1 - C2

QA, KA, VA, FA, QB, KB, VB = 0, 512, 1024, 1536, 1544, 2056, 2568
RQ, RK, RV, RG, MQ, MKV, MKR, MG = 0, 1024, 2048, 4096, 6144, 6400, 6656, 6720


def chunks():
    out = []

    def add(name, kind, n_units, src, tiles, who, evac, pick, **kw):
        out.append(dict(name=name, kind=kind, n=n_units, src=src, tiles=tiles, who=who, evac=evac, pick=pick, **kw))

    k8 = list(range(KT))

    def cols(c0, n):
        return list(range(c0, c0 + n))

    def feat(name, c0, s, half):
        add(f"{name}{half}", "F", 2, "X", k8, "act", ("copy_feat", name[0], s, half),
            ("w_in", None, cols(c0 + 256 * half, 256)))

    feat("kA", KA, 0, 0)
    feat("qA", QA, 0, 0)
    add("f", "F", 1, "X", k8, "dve", ("forget",), ("w_in", None, None))
    add("vA", "A", 4, "X", k8, "act", ("copy_tok", 0), ("w_in", None, cols(VA, 512)))
    feat("kA", KA, 0, 1)
    feat("qA", QA, 0, 1)
    feat("kB", KB, 1, 0)
    feat("qB", QB, 1, 0)
    add("vB", "A", 4, "X", k8, "act", ("copy_tok", 1), ("w_in", None, cols(VB, 512)))
    feat("kB", KB, 1, 1)
    feat("qB", QB, 1, 1)
    add("out1", "B", 8, "S", k8, "dve", ("norm", 0), ("w_out", k8, None))
    for j in range(FT):
        add(f"up{j}", "F", 2, "X", k8, "dve", ("conv", j),
            ("w_up", None, cols(P * j, P) + cols(DFF + P * j, P)))
    add("down", "B", FT, "S", list(range(FT)), "dve", ("norm", 1), ("w_down", list(range(FT)), None))

    even_perm = list(range(0, 256, 2)) + list(range(1, 256, 2))
    add("mqkv", "C", 8, "X", k8, "dve", ("rms",),
        ("w_in_even", None, cols(MQ, 256) + cols(MKR, 32) + cols(MKV, 256) + cols(MKR + 32, 32)))

    def mla(half):
        add(f"mg{half}", "A", 4, "X", k8, "dve", ("gate", 0), ("w_in_even", None, cols(MG + 512 * half, 512)),
            after_job=16 + 4 * half)
        heads = range(4 * half, 4 * half + 4)
        add(f"mlaq{half}", "Q1", 2, "S", [20, 21], "dve", ("mla_q", half),
            ("w_uq_even", [0, 1], [c for h in heads for c in cols(192 * h, 128)]
             + [c for h in heads for c in cols(192 * h + 128, 64)]), after_job=16 + 4 * half)
        add(f"mlakv{half}", "Q2", 2, "S", [22, 23], "act", ("mla_kv", half),
            ("w_ukv_even", [0, 1], [c for h in heads for c in cols(256 * h, 128)]
             + [c for h in heads for c in cols(256 * h + 128, 128)]), after_job=16 + 4 * half)

    def ret_qk(pair):
        for name, c0 in (("k", RK), ("q", RQ)):
            add(f"r{name}{pair}", "A", 4, "X", k8, "dve", ("rope", name, 1 - pair, 256),
                ("w_in_even", None, [c0 + 256 * h + c for h in (2 * pair, 2 * pair + 1) for c in even_perm]),
                after_job=24 * pair)

    def ret_vg(r):
        s = 1 - r % 2
        add(f"rv{r}", "A", 4, "X", k8, "act", ("copy_tok", s), ("w_in_even", None, cols(RV + 512 * r, 512)),
            after_ret=max(r - 1, 0), after_job=24 if r == 1 else 0)
        add(f"rg{r}", "A", 4, "X", k8, "dve", ("gate", s), ("w_in_even", None, cols(RG + 512 * r, 512)),
            after_ret=max(r - 1, 0), after_job=24 if r == 1 else 0)

    mla(0)
    ret_qk(0)
    mla(1)
    for r in (0, 1):
        ret_vg(r)
    ret_qk(1)
    for r in (2, 3):
        ret_vg(r)
    add("out2", "B", 24, "S", list(range(24)), "dve", ("norm", 2), ("w_out_even", list(range(16, 24)) + list(range(16)), None))

    for half in (0, 1):
        s = 1 - half
        for name, c0 in (("k", 1024), ("q", 0)):
            add(f"m{name}{half}", "A", 4, "X", k8, "dve", ("rope", name, s, 64), ("w_in_odd", None, cols(c0 + 512 * half, 512)),
                after_ret=4, by_token=(name, half) == ("k", 0))
        add(f"mv{half}", "A", 4, "X", k8, "act", ("copy_tok", s), ("w_in_odd", None, cols(2048 + 512 * half, 512)),
            after_ret=4)
        add(f"mgt{half}", "A", 4, "X", k8, "dve", ("gate", s), ("w_in_odd", None, cols(3072 + 512 * half, 512)),
            after_ret=4)
    add("out3", "B", 8, "S", k8, "dve", ("norm", 3), ("w_out_odd", k8, None))

    width = dict(F=1, A=2, B=4, C=4, Q1=4, Q2=4)
    at, held, n_act, n_dve, u = 0, [None] * 4, 0, 0, 0
    for c, ch in enumerate(out):
        w = width[ch["kind"]]
        at = (at + w - 1) // w * w % 4
        ch["bank"], ch["before"] = at, {b: held[b] for b in range(at, at + w) if held[b] is not None}
        for b in range(at, at + w):
            held[b] = c
        at = (at + w) % 4
        ch["u0"] = u
        u += ch["n"]
        if ch["who"] == "act":
            n_act += 1
        else:
            n_dve += 1
        ch["count"] = n_act if ch["who"] == "act" else n_dve
    return out


CH = chunks()
BY = {ch["name"]: i for i, ch in enumerate(CH)}
PIECES = [(c, i) for c, ch in enumerate(CH) for i in range(ch["n"])]
NU = len(PIECES)


def piece_size(u):
    c, i = PIECES[u]
    return 576 if CH[c]["kind"] == "C" else 512 if (CH[c]["kind"], i) == ("Q1", 1) else PIECE


JOBS = []
for h in range(8):
    JOBS.append(dict(kind="fox", s=0, h=h, needs=["vA", "f", f"kA{h // 4}", f"qA{h // 4}"]))
for h in range(8):
    JOBS.append(dict(kind="band", s=1, h=h, needs=["vB", f"kB{h // 4}", f"qB{h // 4}"]))
for h in range(8):
    JOBS.append(dict(kind="mla", s=0, h=h % 4, needs=[f"mlaq{h // 4}", f"mlakv{h // 4}", f"mg{h // 4}"]))
for h in range(16):
    JOBS.append(dict(kind="moba", s=1 - h // 8, h=h % 8, needs=[f"m{x}{h // 8}" for x in ("k", "q", "v", "gt")]))
for j, job in enumerate(JOBS):
    job["dv"] = 128 if job["kind"] == "mla" else 64

TJ = []


def new_t(src, dst, split, bank, needs, tiles=1):
    TJ.append(dict(src=src, dst=dst, split=split, bank=bank, needs=needs, tiles=tiles))
    return len(TJ) - 1


def plan():
    order, given, pending, deferred = [], set(), [], []
    state = dict(hi=0, lo=0, wait=0)

    def emit(step, *gives):
        order.append(step)
        given.update(gives)

    def background():
        if pending and pending[0][0] <= given:
            _, steps, gives = pending.pop(0)
            for st in steps:
                emit(st)
            given.update(gives)

    def require(names):
        while not names <= given:
            if deferred and not pending[0][0] <= given:
                flush_turns()
            need, steps, gives = pending.pop(0)
            assert need <= given, (names - given, need - given)
            for st in steps:
                emit(st)
            given.update(gives)

    def split_to(u, parts=("hi", "lo")):
        for part in parts:
            while state[part] < min(u, NU):
                emit((f"split_{part}", state[part]))
                state[part] += 1

    def flush_turns():
        while deferred:
            rope_turns()

    def evacuate(c):
        name, kind = CH[c]["name"], CH[c]["evac"][0]
        if kind in ("rope", "mla_q", "rms"):
            flush_turns()
        emit(("evac", c))
        if kind in ("rope", "mla_q"):
            deferred.append((name, 0))
            state["wait"] = TURN_WAIT
        else:
            given.add(name)

    def run(name, rate, needs=lambda i: set(), early=0, between=(), tail=()):
        c = BY[name]
        ch = CH[c]
        n = ch["n"]
        late = LATE if ch["kind"] == "B" else 0
        halves = [(i, part) for part in (0, 1) for i in range(early)]
        halves += [(i, part) for i in range(early, n - late) for part in (0, 1)]
        halves += [(i, 0) for i in range(n - late, n) if late] + [(i, 1, nn) for nn in (0, 1) for i in range(n - late, n) if late]
        split_to(ch["u0"] + early)
        for x, half in enumerate(halves):
            i, part = half[:2]
            u = ch["u0"] + i
            require(needs(i))
            if early and half == (0, 1):
                for st in between:
                    emit(st)
            emit(("mm", ch["u0"] + i) + half[1:])
            if late and i == n - 1 and part == 0:
                emit(("norm_first", ch["evac"][1]))
            if late and half == (n - 1, 1, 0):
                for q in range(2):
                    emit(("norm_rest", ch["evac"][1], 0, q))
                emit(("norm_half", ch["evac"][1]))
            if late and i >= n - late:
                split_to(ch["u0"] + n - late + RING)
            elif i < early:
                if part == 1:
                    split_to(u + AHEAD + 1)
            elif part == 0 or late:
                split_to(u + AHEAD + 1, ("hi",))
                split_to(u + AHEAD, ("lo",))
            else:
                split_to(u + AHEAD + 1)
            if deferred:
                state["wait"] -= 1
                if state["wait"] <= 0:
                    rope_turns()
            if x == len(halves) - 1:
                for st in tail:
                    emit(st)
                evacuate(c)
            for _ in range(rate):
                background()

    def rope_turns():
        name, i = deferred.pop()
        kind = CH[BY[name]]["evac"]
        dst = ("attn", kind[1], kind[2]) if kind[0] == "rope" else ("qpe",)
        emit(("turn", new_t(("rot", i), dst + (i,), False, 3, BY[name], 2)))
        if kind[0] == "rope" and i == 0:
            deferred.append((name, 2))
        else:
            given.add(name)

    def attention(jobs):
        n = len(jobs)
        for i in range(n + 3):
            steps, need, gives = [], set(), set()
            if i < n:
                need = set(JOBS[jobs[i]]["needs"])
                steps.append(("scores", jobs[i]))
            if i >= 3:
                j = jobs[i - 3]
                job = JOBS[j]
                per = P // job["dv"]
                if (j + 1) % per == 0:
                    tile = (j % 16 if job["kind"] in ("fox", "band") else j - 16 if job["kind"] == "mla" else j - 24) // per
                    steps.append(("turn", new_t(("y", j), ("S", tile), True, (jobs[0] + i + 1) % 2, j)))
                    gives.add(f"{'L1' if j < 16 else 'L2' if j < 24 else 'L3'}y{tile}")
            if i < n:
                steps.append(("soft", jobs[i]))
            pending.append((need, steps, gives))
            steps = []
            if 1 <= i <= n:
                steps += [("pt", jobs[i - 1])]
            if 2 <= i <= n + 1:
                steps += [("pv", jobs[i - 2])]
            if steps:
                pending.append((set(), steps, set()))

    def retention(r):
        s = set([f"rk{r // 2}", f"rq{r // 2}"])
        pending.append((s, [("ret_s", r)], set()))
        pending.append((s | {f"rv{r}", f"rg{r}"}, [("ret_o", r)], set()))
        pending.extend((set(), [], set()) for _ in range(3))
        for i in (0, 2):
            t = new_t(("ry", r, i), ("S", 8 + 4 * r + i), True, 3 if i == 0 else 0, r, 2)
            pending.append((set(), [("turn", t)], {f"L2y{8 + 4 * r + i}", f"L2y{9 + 4 * r + i}"}))

    def turn_x(base, t):
        return [("turn", new_t(("x", t, q), ("X", t, q), True, 2 * t + q, base)) for q in range(2)]

    def norm_second(l, u):
        split_to(u)
        emit(("norm_rest", l, 1, 0))
        emit(("norm_rest", l, 1, 1))
        return turn_x(l + 1, 1)

    emit(("load", "start"))
    for st in turn_x(0, 0) + turn_x(0, 1):
        emit(st)
    split_to(AHEAD)

    for name in ("kA0", "qA0", "f"):
        run(name, 0)
    run("vA", 0)
    attention(range(0, 8))
    for name in ("kA1", "qA1", "kB0", "qB0"):
        run(name, 1)
    run("vB", 1)
    attention(range(8, 16))
    for name in ("kB1", "qB1"):
        run(name, 1)
    emit(("load", "ln", 0))
    run("out1", 1, lambda i: {f"L1y{i}"}, tail=turn_x(1, 0))
    for st in norm_second(0, 0):
        emit(st)
    for j in range(FT + 2):
        if j < FT:
            run(f"up{j}", 0)
        if 1 <= j <= FT:
            emit(("gelu", j - 1))
        if j >= 2:
            emit(("h_split", j - 2))
    emit(("tables",))
    emit(("load", "ln", 1))
    emit(("load", "even"))
    run("down", 0, tail=turn_x(2, 0))

    rest = norm_second(1, CH[BY["mqkv"]]["u0"] + 4)
    run("mqkv", 0, early=4, between=rest)
    run("mg0", 0)
    emit(("turn", new_t(("kpe", 0), ("kpe", 0), False, 3, 0)))
    for i in (0, 2):
        emit(("turn", new_t(("mn", i), ("S", 20 + i), True, 3, 0, 2)))
    for name in ("mlaq0", "mlakv0"):
        run(name, 0)
    attention(range(16, 20))
    for name in ("rk0", "rq0"):
        run(name, 1)
    require({"L2y3"})
    run("mg1", 0)
    for name in ("mlaq1", "mlakv1"):
        run(name, 0)
    attention(range(20, 24))
    retention(0)
    run("rv0", 1)
    run("rg0", 1)
    retention(1)
    require({"L2y7"})
    for name in ("rv1", "rg1"):
        run(name, 1)
    for name in ("rk1", "rq1"):
        run(name, 1)
    retention(2)
    require({"L2y11"})
    for name in ("rv2", "rg2"):
        run(name, 1)
    retention(3)
    require({"L2y15"})
    run("rv3", 1)
    run("rg3", 1)
    emit(("load", "ln", 2))
    run("out2", 1, lambda i: {f"L2y{i}"}, tail=turn_x(3, 0))

    rest = norm_second(2, CH[BY["mk0"]]["u0"] + 3)
    run("mk0", 0, early=3, between=rest)
    for name in ("mq0", "mv0", "mgt0"):
        run(name, 0)
    attention(range(24, 32))
    for name in ("mk1", "mq1", "mv1", "mgt1"):
        run(name, 1)
    attention(range(32, 40))
    emit(("load", "ln", 3))
    run("out3", 1, lambda i: {f"L3y{i}"})
    for q in range(2):
        emit(("norm_rest", 3, 1, q))
    emit(("store",))
    assert not pending, pending
    return order


ORDER = plan()
assert [s[1] for s in ORDER if s[0] == "evac"] == list(range(len(CH)))
RANK = {n: i for i, n in enumerate(s[1] for s in ORDER if s[0] == "turn")}
SPLITS = [s[1] for s in ORDER if s[0] == "turn" and TJ[s[1]]["split"]]
SPLIT_RANK = {n: i for i, n in enumerate(SPLITS)}
BANKS = dict(scores=lambda n: [n % 2], pt=lambda n: [2], pv=lambda n: [3], turn=lambda n: [TJ[n]["bank"]],
             ret_s=lambda n: [0], ret_o=lambda n: [1, 2])
BANK_BEFORE = {}
_last = {}
for _s in ORDER:
    if _s[0] in BANKS:
        _banks = BANKS[_s[0]](_s[-1])
        BANK_BEFORE[_s] = sorted({_last[b] for b in _banks if b in _last})
        _last.update({b: _s for b in _banks})
FILLED = {}
_seen = {}
for _s in ORDER:
    if _s[0] == "turn":
        d = TJ[_s[1]]["dst"]
        if d[0] == "S":
            for _i in range(TJ[_s[1]]["tiles"]):
                _seen[("S", d[1] + _i)] = _s[1]
        elif d[0] == "X":
            _seen[d] = _s[1]
        else:
            _seen[d[:3] if d[0] == "attn" else d[:1]] = _s[1]
    elif _s[0] in ("mm", "scores", "ret_s"):
        FILLED[_s] = dict(_seen)
Y_TURN = {TJ[n]["src"][1]: n for n in RANK if TJ[n]["src"][0] == "y"}
_tiles = sorted(Y_TURN)
Y_SLOT = {j: i % 2 for i, j in enumerate(_tiles)}
Y_BEFORE = {}
for _i, _j in enumerate(_tiles):
    for _k in range(_j - P // JOBS[_j]["dv"] + 1, _j + 1):
        Y_SLOT[_k] = _i % 2
        if _i >= 2:
            Y_BEFORE[_k] = Y_TURN[_tiles[_i - 2]]
ROT_READ, _r = {}, None
for _s in ORDER:
    if _s[0] == "turn" and TJ[_s[1]]["src"][0] in ("rot", "mn", "kpe"):
        _r = _s[1]
    elif _s[0] == "evac":
        ROT_READ[_s[1]] = _r
RET_TURN = {r: max((n for n in RANK if TJ[n]["src"][:2] == ("ry", r)), key=RANK.get) for r in range(4)}

CONST = {}
_at = 0
for _name, _n in (("ident", P), ("causal", 3 * P), ("band", P), ("cumA", 4), ("cumB", 4),
                  ("inv64", 32), ("inv256", 128)):
    CONST[_name] = (_at, _at + _n)
    _at += _n
NCONST = _at


def constants():
    c = np.zeros((P, NCONST), np.float32)

    def put(name, a):
        c[:, CONST[name][0]:CONST[name][1]] = a

    q, k = np.arange(P)[:, None], np.arange(P)[None, :]
    tri = np.where(k <= q, 0.0, NEG).astype(np.float32)
    put("ident", np.eye(P, dtype=np.float32))
    put("causal", np.concatenate([tri, np.zeros((P, P), np.float32), tri], 1))
    put("band", np.where(k // 64 <= q // 64, 0.0, NEG).astype(np.float32))
    r = np.arange(P)[:, None] % 32
    g = np.arange(2)[None, :]
    big = np.float32(1.0 / SCALE_64)
    put("cumA", np.concatenate([(r == 2 * g) * big, (r == 2 * g + 1) * np.float32(1)], 1))
    put("cumB", np.concatenate([(r == 2 * g + 1) * -big, (r == 2 * g) * np.float32(1)], 1))
    put("inv64", (1.0 / (np.float32(10000.0) ** (np.arange(0, 64, 2, dtype=np.float32) / np.float32(64)))).astype(np.float32)[None, :])
    put("inv256", (1.0 / (np.float32(10000.0) ** np.linspace(0, 1, 128, dtype=np.float32))).astype(np.float32)[None, :])
    return c


def decay_table():
    g = 1.0 - 2.0 ** (-5.0 - np.arange(4, dtype=np.float64))
    d = np.arange(S)[None, :] - np.arange(P)[:, None]
    t = np.where(d[None] >= 0, g[:, None, None] ** np.maximum(d, 0)[None], 0.0) / 16.0
    return np.ascontiguousarray(t.transpose(1, 0, 2)).astype(np.float32)


def build(nc, t):
    with ExitStack() as ctx:
        def sb(name, shape, dt=F32):
            return ctx.enter_context(nc.sbuf_tensor(name, shape, dt))

        def sem(name):
            return ctx.enter_context(nc.semaphore(name))

        raw = sb("raw", [P, RAW, PIECE])
        w_hi = sb("w_hi", [P, RING, PIECE], F32R)
        w_lo = sb("w_lo", [P, RING, PIECE], F32R)
        X_hi = sb("X_hi", [P, KT, S], F32R)
        X_lo = sb("X_lo", [P, KT, S], F32R)
        S_hi = sb("S_hi", [P, 24, S], F32R)
        S_lo = sb("S_lo", [P, 24, S], F32R)
        res = sb("res", [P, NT, D])
        decay = sb("decay", [P, 4, S])
        ryb = sb("ryb", [P, NT, 512])
        cst = sb("cst", [P, NCONST])
        qT = [sb(f"qT{s}", [P, 4, S]) for s in (0, 1)]
        kT = [sb(f"kT{s}", [P, 4, S]) for s in (0, 1)]
        vv = [sb(f"v{s}", [P, NT, 512]) for s in (0, 1)]
        gate = sb("gate", [P, 2, NT, 512])
        qpeT = sb("qpeT", [P, 2, S])
        kpeT = sb("kpeT", [P, 1, S])
        rot = sb("rot", [P, NT, 512])
        rtmp = sb("rtmp", [P, NT, 512])
        pr = sb("pr", [P, 2, 3 * P])
        ptb = sb("ptb", [P, 2, 3 * P])
        yb = sb("yb", [P, 2, NT, P])
        small = sb("small", [P, 96])
        tab64 = sb("tab64", [P, 2, NT, 32])
        tab256 = sb("tab256", [P, 2, NT, 128])
        cvp = sb("cvp", [P, 4, 2, FT])
        posi = sb("posi", [P, NT], I32)
        cumA = rot[:, 0, :].rearrange("p (g s) -> p g s", g=2)
        cumB = rot[:, 1, :].rearrange("p (g s) -> p g s", g=2)

        acc = ctx.enter_context(nc.psum_tensor("acc", [P, 4, 512], F32))
        job = ctx.enter_context(nc.psum_tensor("job", [P, 4, 512], F32))

        fox = rtmp[:, :, :].rearrange("p t (a s) -> p (t a) s", a=2)
        bias = gate[:, :, :, :].rearrange("p s t n -> p (s t n)").rearrange("p (h k) -> p h k", h=8)
        conv = [vv[b][:, 0, :].rearrange("p (i s) -> p i s", i=2) for b in (0, 1)]
        gel = [vv[b][:, 1, 0:256] for b in (0, 1)]
        hh = [vv[b][:, 1, 256:512] for b in (0, 1)]
        gb = gate[:, :, :, :].rearrange("p s t n -> p s (t n)")
        rgain = pr[:, :, :].rearrange("p b n -> p (b n)")[:, 0:512]
        ang = qT[0][:, 0:2, 0:160]
        turns = qT[0][:, 2:4, 0:160]
        wrap = qT[1][:, 0:2, 0:160]
        sin_arg = kT[0][:, 0:2, 0:160]
        cos_arg = kT[0][:, 2:4, 0:160]
        posf = small[:, 90:92]
        bforget = small[:, 80:81]
        neg_max = small[:, 0:4].rearrange("p (b t) -> p b t", b=2)
        rsum = small[:, 64:70].rearrange("p (b t) -> p b t", b=3)
        rinv = small[:, 8:10]
        rdbl = small[:, 10:12]
        stats = small[:, 12:36].rearrange("p (t q s) -> p t q s", t=2, q=2)
        mv = small[:, 36:40].rearrange("p (t a) -> p t a", t=2)
        rstd_in = small[:, 40:44]
        rstd = small[:, 44:48]
        half_neg = small[:, 48:52]
        ssq = small[:, 56:60]

        def const(name):
            a, b = CONST[name]
            return cst[:, a:b]

        ident = const("ident")

        landed = [sem(f"landed{i}") for i in range(RAW)]
        hi_done, lo_done, w_used = sem("hi_done"), sem("lo_done"), sem("w_used")
        evac_act, evac_dve = sem("evac_act"), sem("evac_dve")
        t_ready, t_hi, t_lo = sem("t_ready"), sem("t_hi"), sem("t_lo")
        sc_ready, max_done, exp_done = sem("sc_ready"), sem("max_done"), sem("exp_done")
        pt_ready, pt_copied, o_ready, y_done = sem("pt_ready"), sem("pt_copied"), sem("o_ready"), sem("y_done")
        const_in, ident_in, bias_in = sem("const_in"), sem("ident_in"), sem("bias_in")
        x_in = [sem(f"x_in{i}") for i in range(2 * NT)]
        pos_in, bf_in, conv_in = sem("pos_in"), sem("bf_in"), sem("conv_in")
        ln_g_in, ln_b_in, even_in, rg_in = sem("ln_g_in"), sem("ln_b_in"), sem("even_in"), sem("rg_in")
        first_done, half_done = sem("first_done"), sem("half_done")
        ang_done, sin_done, tab_done = sem("ang_done"), sem("sin_done"), sem("tab_done")
        z_ready, ln_ready = sem("z_ready"), sem("ln_ready")
        tap_act, tap_dve, gelu_done, h_done, h_hi, h_lo = (sem("tap_act"), sem("tap_dve"), sem("gelu_done"),
                                                           sem("h_done"), sem("h_hi"), sem("h_lo"))
        pow_done, x_ready = sem("pow_done"), sem("x_ready")
        pow_in = sem("pow_in")
        mn_ready = sem("mn_ready")
        sq_done = sem("sq_done")
        half_ready = sem("half_ready")
        th_done = sem("th_done")
        rot_prod, rot_ready = sem("rot_prod"), sem("rot_ready")
        rs_ready, rp_done, ro_ready, ry_done = sem("rs_ready"), sem("rp_done"), sem("ro_ready"), sem("ry_done")
        stored = sem("stored")
        qn_copied, kn_copied, raw_copied = sem("qn_copied"), sem("kn_copied"), sem("raw_copied")
        kpe_prod = sem("kpe_prod")
        dve_chain, act_chain, pool_chain = sem("dve_chain"), sem("act_chain"), sem("pool_chain")

        block = ctx.enter_context(nc.Block())

        ROT = [c for c, ch in enumerate(CH) if ch["evac"][0] in ("rope", "rms", "mla_q")]
        ROPES = [c for c in ROT if CH[c]["evac"][0] != "rms"]
        GATE = [c for c, ch in enumerate(CH) if ch["evac"][0] == "gate"]
        POW = []
        for s_ in ORDER:
            if s_[0] == "norm_first":
                POW.append(("norm", s_[1], 0))
            elif s_[0] == "evac" and CH[s_[1]]["evac"][0] == "norm":
                POW.append(("norm", CH[s_[1]]["evac"][1], 1))
            elif s_[0] == "evac" and CH[s_[1]]["evac"][0] == "rms":
                POW.append(("rms",))
            elif s_[0] == "ret_o":
                POW.append(("ret", s_[1]))

        def chunk_waits(eng, c, banks):
            waits = {}
            for b in banks:
                if b not in CH[c]["before"]:
                    continue
                old = CH[CH[c]["before"][b]]
                kind = old["evac"][0]
                if b < 2 and kind == "norm":
                    waits[pow_in] = POW.index(("norm", old["evac"][1], 0)) + 1
                elif b < 2 and kind == "mla_q":
                    waits[qn_copied] = 1 + old["evac"][1]
                elif b < 2 and kind == "mla_kv":
                    waits[kn_copied] = 1 + old["evac"][1]
                elif b < 2 and kind == "rms":
                    waits[raw_copied] = 1
                else:
                    who = evac_act if old["who"] == "act" else evac_dve
                    waits[who] = max(waits.get(who, 0), old["count"])
            for who, n in waits.items():
                eng.wait_ge(who, n)

        def wait_chunk_evac(eng, name):
            ch = CH[BY[name]]
            eng.wait_ge(evac_act if ch["who"] == "act" else evac_dve, ch["count"])

        def after_waits(eng, ch):
            if ch.get("after_job"):
                eng.wait_ge(y_done, ch["after_job"])
            if ch.get("after_ret"):
                eng.wait_ge(ry_done, ch["after_ret"])

        def place(n):
            return job[:, TJ[n]["bank"], :]

        def bank_free(eng, step):
            for before in BANK_BEFORE[step]:
                kind, n = before[0], before[-1]
                if kind == "scores":
                    eng.wait_ge(max_done, n + 1)
                elif kind == "pt":
                    eng.wait_ge(pt_copied, n + 1)
                elif kind == "pv":
                    eng.wait_ge(y_done, n + 1)
                elif kind == "ret_s":
                    eng.wait_ge(rp_done, n + 1)
                elif kind == "ret_o":
                    eng.wait_ge(ry_done, n + 1)
                elif TJ[n]["split"]:
                    eng.wait_ge(t_lo, SPLIT_RANK[n] + 1)
                else:
                    eng.wait_ge(t_hi, RANK[n] + 1)

        @block.sync
        def _(sp):
            def load_piece(u):
                n = piece_size(u)
                if u >= RAW:
                    sp.wait_ge(lo_done, u - RAW + 1)
                sp.dma_start(raw[:, u % RAW, 0:n], t["w"][u, :, 0:n]).then_inc(landed[u % RAW], 16)

            for step in ORDER:
                if step == ("load", "start"):
                    sp.dma_start(ident, t["const"][:, 0:P]).then_inc(ident_in, 16)
                    for i in range(2 * NT):
                        tt, q = divmod(i, 2)
                        sp.dma_start(res[:, tt, q * 512:(q + 1) * 512],
                                     t["x"][0, tt * P:(tt + 1) * P, q * 512:(q + 1) * 512]).then_inc(x_in[i], 16)
                    for u in range(RAW):
                        load_piece(u)
                        if u == 2:
                            sp.dma_start(cst[:, P:], t["const"][:, P:]).then_inc(const_in, 16)
                            sp.dma_start(bforget, t["b_forget"]).then_inc(bf_in, 16)
                    sp.dma_start(bias[:, :, :], t["bias"]).then_inc(bias_in, 16)
                    sp.dma_start(posi[:], t["positions_2"]).then_inc(pos_in, 16)
                    sp.dma_start(cvp[:], t["conv"]).then_inc(conv_in, 16)
                    sp.dma_start(decay[:], t["decay"]).then_inc(even_in, 16)
                elif step[0] == "split_lo":
                    if step[1] + RAW < NU:
                        load_piece(step[1] + RAW)
                elif step == ("store",):
                    for i in range(2 * NT):
                        tt, q = divmod(i, 2)
                        sp.wait_ge(x_ready, 2 * NT * 3 + i + 1)
                        sp.dma_start(t["out"][0, tt * P:(tt + 1) * P, q * 512:(q + 1) * 512],
                                     res[:, tt, q * 512:(q + 1) * 512]).then_inc(stored, 16)
            sp.wait_ge(stored, 16 * 2 * NT)

        @block.tensor
        def _(pe):
            def three(out, a_hi, a_lo, b_hi, b_lo, start, stop):
                nc.tensor.matmul(out, a_hi, b_hi, start=start, stop=False)
                nc.tensor.matmul(out, a_hi, b_lo, start=False, stop=False)
                return nc.tensor.matmul(out, a_lo, b_hi, start=False, stop=stop)

            def wait_operand(step, ch, keys):
                seen = FILLED[step]
                if ch["name"] == "down":
                    pe.wait_ge(h_lo, max(k[1] for k in keys) + 1)
                else:
                    pe.wait_ge(t_lo, max(SPLIT_RANK[seen[k]] for k in keys) + 1)

            def mm(step):
                u, part, whole = step[1], step[2], len(step) == 3
                c, i = PIECES[u]
                ch = CH[c]
                hi, lo = (X_hi, X_lo) if ch["src"] == "X" else (S_hi, S_lo)
                wh, wl = w_hi[:, u % RING, :], w_lo[:, u % RING, :]
                kind, b0, tiles = ch["kind"], ch["bank"], ch["tiles"]
                if kind in ("Q1", "Q2"):
                    if part == 0:
                        chunk_waits(pe, c, (2 * i, 2 * i + 1))
                elif i == 0 and kind in ("B", "C"):
                    chunk_waits(pe, c, (2 * part, 2 * part + 1))
                elif i == 0 and ch.get("by_token"):
                    chunk_waits(pe, c, (b0 + part,))
                elif i == 0 and part == 0:
                    chunk_waits(pe, c, range(b0, b0 + (2 if kind == "A" else 1)))
                if part == 0:
                    pe.wait_ge(lo_done, u + 1)
                last = None
                if kind == "F":
                    wait_operand(step, ch, [("X", tt, part) for tt in range(NT)])
                    for k in range(4 * part, 4 * part + 4):
                        w = slice(k * P, (k + 1) * P)
                        last = three(acc[:, b0, i * S:(i + 1) * S], wh[:, w], wl[:, w], hi[:, k, :], lo[:, k, :],
                                     k == 0, k == KT - 1)
                elif ch.get("by_token"):
                    tt = part
                    wait_operand(step, ch, [("X", tt, 2 * i // 4)])
                    for e in range(2):
                        x = 2 * i + e
                        w = slice(e * 512, (e + 1) * 512)
                        last = three(acc[:, b0 + tt, :], hi[:, x, tt * P:(tt + 1) * P], lo[:, x, tt * P:(tt + 1) * P],
                                     wh[:, w], wl[:, w], x == 0, x == len(tiles) - 1)
                elif kind == "A":
                    x = 2 * i + part
                    k = tiles[x]
                    wait_operand(step, ch, [("X", tt, k // 4) for tt in range(NT)])
                    w = slice(part * 512, (part + 1) * 512)
                    for tt in range(NT):
                        last = three(acc[:, b0 + tt, :], hi[:, k, tt * P:(tt + 1) * P], lo[:, k, tt * P:(tt + 1) * P],
                                     wh[:, w], wl[:, w], x == 0, x == len(tiles) - 1)
                elif kind in ("B", "C"):
                    k, tt = tiles[i], part
                    wait_operand(step, ch, [("X", tt, k // 4)] if ch["src"] == "X" else [("S", k)])
                    n = 512 if kind == "B" else 288
                    for nn in range(2) if whole else [step[3]]:
                        w = slice(nn * n, (nn + 1) * n)
                        last = three(acc[:, b0 + tt * 2 + nn, 0:n], hi[:, k, tt * P:(tt + 1) * P],
                                     lo[:, k, tt * P:(tt + 1) * P], wh[:, w], wl[:, w], i == 0, i == len(tiles) - 1)
                    if kind == "B" and part == 0 and i == ch["n"] - 1:
                        last.then_inc(first_done, 1)
                    if not whole and step[3] == 0 and i == ch["n"] - 1:
                        last.then_inc(half_done, 1)
                elif i == 0:
                    wait_operand(step, ch, [("S", k) for k in tiles])
                    for f in (2 * part, 2 * part + 1):
                        for x, k in enumerate(tiles):
                            w = slice(x * 512 + f * P, x * 512 + f * P + P)
                            last = three(acc[:, b0 + f // 2, (f % 2) * S:(f % 2 + 1) * S], wh[:, w], wl[:, w],
                                         hi[:, k, :], lo[:, k, :], x == 0, x == 1)
                else:
                    n = 256 if kind == "Q1" else 512
                    for x, k in enumerate(tiles):
                        w = slice(x * n, x * n + n)
                        last = three(acc[:, b0 + 2 + part, 0:n], hi[:, k, part * P:(part + 1) * P],
                                     lo[:, k, part * P:(part + 1) * P], wh[:, w], wl[:, w], x == 0, x == 1)
                if part == 1 and (whole or step[3] == 1):
                    last.then_inc(w_used, 1)

            def scores(step):
                j = step[1]
                jb = JOBS[j]
                s, h = jb["s"], jb["h"]
                for name in jb["needs"]:
                    if CH[BY[name]]["evac"][0] not in ("gate", "rope", "forget"):
                        wait_chunk_evac(pe, name)
                bank_free(pe, step)
                out = job[:, j % 2, :]
                blocks = [(out[:, 0:P], 0, P), (out[:, P:3 * P], 1, S)]
                seen = FILLED[step]
                if jb["kind"] in ("mla", "moba"):
                    keys = [("qpe",), ("kpe",)] if jb["kind"] == "mla" else [("attn", "q", s), ("attn", "k", s)]
                    pe.wait_ge(t_hi, max(RANK[seen[k]] for k in keys) + 1)
                for dst, tt, nk in blocks:
                    q = slice(tt * P, (tt + 1) * P)
                    if jb["kind"] == "mla":
                        lo_p = 64 * (h % 2)
                        nc.tensor.matmul(dst, qT[s][:, h, q], kT[s][:, h, 0:nk], start=True, stop=False)
                        last = nc.tensor.matmul(dst, qpeT[lo_p:lo_p + 64, h // 2, q], kpeT[lo_p:lo_p + 64, 0, 0:nk],
                                                start=False, stop=True)
                    else:
                        lo_p = 64 * (h % 2)
                        fox = jb["kind"] == "fox"
                        last = nc.tensor.matmul(dst, qT[s][lo_p:lo_p + 64, h // 2, q], kT[s][lo_p:lo_p + 64, h // 2, 0:nk],
                                                start=True, stop=not fox)
                        if fox:
                            wait_chunk_evac(pe, "f")
                            r = 32 * (h % 4)
                            last = nc.tensor.matmul(dst, cumA[r:r + 4, h // 4, q], cumB[r:r + 4, h // 4, 0:nk],
                                                    start=False, stop=True)
                last.then_inc(sc_ready, 1)

            def pt(step):
                j = step[1]
                pe.wait_ge(exp_done, j + 1)
                bank_free(pe, step)
                for b in range(3):
                    last = nc.tensor.transpose(job[:, 2, b * P:(b + 1) * P], pr[:, j % 2, b * P:(b + 1) * P], ident)
                last.then_inc(pt_ready, 1)

            def pv(step):
                j = step[1]
                jb = JOBS[j]
                s, h, dv = jb["s"], jb["h"], jb["dv"]
                pe.wait_ge(pt_copied, j + 1)
                bank_free(pe, step)
                b = ptb[:, j % 2, :]
                v = slice(h * dv, (h + 1) * dv)
                nc.tensor.matmul(job[:, 3, 0:dv], b[:, 0:P], vv[s][:, 0, v], start=True, stop=True)
                nc.tensor.matmul(job[:, 3, P:P + dv], b[:, P:2 * P], vv[s][:, 0, v], start=True, stop=False)
                nc.tensor.matmul(job[:, 3, P:P + dv], b[:, 2 * P:3 * P], vv[s][:, 1, v], start=False, stop=True)\
                    .then_inc(o_ready, 1)

            def turn(step):
                n = step[1]
                tj = TJ[n]
                kind = tj["src"][0]
                bank_free(pe, step)
                out = place(n)
                if kind == "x":
                    _, tt, q = tj["src"]
                    if tj["needs"] == 0:
                        pe.wait_ge(x_in[2 * tt + q], 16)
                        pe.wait_ge(ident_in, 16)
                    else:
                        pe.wait_ge(x_ready, 2 * NT * (tj["needs"] - 1) + 2 * tt + q + 1)
                    for i in range(4):
                        k = 4 * q + i
                        last = nc.tensor.transpose(out[:, i * P:(i + 1) * P], res[:, tt, k * P:(k + 1) * P], ident)
                else:
                    for tt in range(NT):
                        if kind == "rot":
                            pe.wait_ge(rot_ready, NT * ROT.index(tj["needs"]) + tt + 1)
                            src = rot[:, tt, tj["src"][1] * P:]
                        elif kind == "kpe":
                            pe.wait_ge(rot_ready, NT * ROT.index(BY["mqkv"]) + tt + 1)
                            src = ryb[:, tt, 0:P]
                        elif kind == "mn":
                            pe.wait_ge(mn_ready, tt + 1)
                            src = rot[:, tt, tj["src"][1] * P:]
                        elif kind == "y":
                            pe.wait_ge(y_done, tj["src"][1] + 1)
                            src = yb[:, Y_SLOT[tj["src"][1]], tt, :]
                        else:
                            pe.wait_ge(ry_done, tj["src"][1] + 1)
                            src = ryb[:, tt, tj["src"][2] * P:]
                        for i in range(tj["tiles"]):
                            last = nc.tensor.transpose(out[:, i * S + tt * P:i * S + (tt + 1) * P],
                                                       src[:, i * P:(i + 1) * P], ident)
                last.then_inc(t_ready, 1)

            def ret_s(step):
                r = step[1]
                s = 1 - r // 2
                seen = FILLED[step]
                pe.wait_ge(t_hi, max(RANK[seen[("attn", "q", s)]], RANK[seen[("attn", "k", s)]]) + 1)
                bank_free(pe, step)
                b = 2 * (r % 2)
                for e in range(2):
                    nc.tensor.matmul(job[:, 0, 0:S], kT[s][:, b + e, 0:P], qT[s][:, b + e, :], start=e == 0, stop=e == 1)
                for e in range(2):
                    last = nc.tensor.matmul(job[:, 0, S:S + P], kT[s][:, b + e, P:S], qT[s][:, b + e, P:S],
                                            start=e == 0, stop=e == 1)
                last.then_inc(rs_ready, 1)

            def ret_o(step):
                r = step[1]
                s = 1 - r % 2
                wait_chunk_evac(pe, f"rv{r}")
                pe.wait_ge(rp_done, r + 1)
                bank_free(pe, step)
                b = ptb[:, r % 2, :]
                nc.tensor.matmul(job[:, 1, :], b[:, 0:P], vv[s][:, 0, :], start=True, stop=True)
                nc.tensor.matmul(job[:, 2, :], b[:, P:2 * P], vv[s][:, 0, :], start=True, stop=False)
                nc.tensor.matmul(job[:, 2, :], b[:, 2 * P:3 * P], vv[s][:, 1, :], start=False, stop=True)\
                    .then_inc(ro_ready, 1)

            for step in ORDER:
                if step[0] == "mm":
                    mm(step)
                elif step[0] == "scores":
                    scores(step)
                elif step[0] == "pt":
                    pt(step)
                elif step[0] == "pv":
                    pv(step)
                elif step[0] == "turn":
                    turn(step)
                elif step[0] == "ret_s":
                    ret_s(step)
                elif step[0] == "ret_o":
                    ret_o(step)

        def wait_acc(eng, c):
            eng.wait_ge(w_used, CH[c]["u0"] + CH[c]["n"])

        def t_dest(n):
            tj = TJ[n]
            d, p = tj["dst"], place(n)
            if d[0] == "X":
                _, tt, q = d
                v = slice(tt * P, (tt + 1) * P)
                return (X_hi[:, 4 * q:4 * q + 4, v], X_lo[:, 4 * q:4 * q + 4, v], p.rearrange("p (k s) -> p k s", k=4))
            nt = tj["tiles"]
            src = p[:, 0:nt * S].rearrange("p (k s) -> p k s", k=nt)
            at = slice(d[-1], d[-1] + nt)
            if d[0] == "S":
                return S_hi[:, at, :], S_lo[:, at, :], src
            if d[0] == "qpe":
                return qpeT[:, at, :], None, src
            if d[0] == "kpe":
                return kpeT[:, at, :], None, src
            return (qT if d[1] == "q" else kT)[d[2]][:, at, :], None, src

        @block.scalar
        def _(act):
            def split(u):
                n = piece_size(u)
                act.wait_ge(landed[u % RAW], 16 * (u // RAW + 1))
                if u >= RING:
                    act.wait_ge(w_used, u - RING + 1)
                nc.scalar.activation(w_hi[:, u % RING, 0:n], raw[:, u % RAW, 0:n], ACT.Copy).then_inc(hi_done, 1)

            def turn(n):
                hi, _, src = t_dest(n)
                act.wait_ge(t_ready, RANK[n] + 1)
                nc.scalar.activation(hi, src, ACT.Copy).then_inc(t_hi, 1)

            def evac(c):
                ch = CH[c]
                e, b0 = ch["evac"], ch["bank"]
                kind = e[0]
                if kind in ("rope", "norm"):
                    return
                if kind in ("mla_q", "mla_kv"):
                    act.wait_ge(w_used, ch["u0"] + 1)
                elif kind != "conv":
                    wait_acc(act, c)
                if kind != "conv":
                    after_waits(act, ch)
                if kind == "copy_feat":
                    _, which, s, half = e
                    dst = (qT if which == "q" else kT)[s][:, 2 * half:2 * half + 2, :]
                    nc.scalar.activation(dst, acc[:, b0, :].rearrange("p (a s) -> p a s", a=2), ACT.Copy)\
                        .then_inc(evac_act, 1)
                elif kind == "copy_tok":
                    nc.scalar.activation(vv[e[1]][:, :, :], acc[:, b0:b0 + 2, :], ACT.Copy).then_inc(evac_act, 1)
                elif kind == "mla_kv":
                    nc.scalar.activation(kT[0][:, :, :], acc[:, b0:b0 + 2, :].rearrange("p b (a s) -> p (b a) s", a=2), ACT.Copy)\
                        .then_inc(kn_copied, 1)
                    wait_acc(act, c)
                    nc.scalar.activation(vv[0][:, :, :], acc[:, b0 + 2:b0 + 4, :], ACT.Copy).then_inc(evac_act, 1)
                elif kind == "mla_q":
                    nc.scalar.activation(qT[0][:, :, :], acc[:, b0:b0 + 2, :].rearrange("p b (a s) -> p (b a) s", a=2), ACT.Copy)\
                        .then_inc(qn_copied, 1)
                elif kind == "gate":
                    nc.scalar.activation(gate[:, e[1], :, :], acc[:, b0:b0 + 2, :], ACT.Tanh, scale=0.5).then_inc(th_done, 1)
                elif kind == "rms":
                    nc.scalar.activation(rot[:, 0, :].rearrange("p (x n) -> p x n", x=2), acc[:, b0:b0 + 2, 0:256], ACT.Copy)
                    nc.scalar.activation(ryb[:, 0, 256:320].rearrange("p (x n) -> p x n", x=2), acc[:, b0:b0 + 2, 256:288], ACT.Copy)\
                        .then_inc(raw_copied, 1)
                    act.wait_ge(raw_copied, 1)
                    act.wait_ge(evac_dve, ch["count"])
                    for tt in range(NT):
                        for x in range(2):
                            last = nc.scalar.activation(rtmp[:, tt, x * 256:(x + 1) * 256],
                                                        rot[:, tt, x * 256:(x + 1) * 256], ACT.Square,
                                                        accum_out=ssq[:, 2 * tt + x:2 * tt + x + 1])
                    last.then_inc(sq_done, 1)
                elif kind == "forget":
                    act.wait_ge(z_ready, 1)
                    for i, (a, f, kw) in enumerate(((0, ACT.Abs, {}), (1, ACT.Exp, dict(scale=-1.0)),
                                                    (1, ACT.Ln, dict(bias=1.0)))):
                        nc.scalar.activation(fox[:, 1, :], fox[:, a, :], f, **kw).then_inc(ln_ready, 1)
                        act.wait_ge(ln_ready, i + 1)
                elif kind == "conv":
                    j = e[1]
                    wait_acc(act, c)
                    if j == 0:
                        act.wait_ge(conv_in, 16)
                    if j >= 2:
                        act.wait_ge(h_done, j - 1)
                    for i in range(2):
                        last = nc.scalar.activation(conv[j % 2][:, i, :], acc[:, b0, i * S:(i + 1) * S], ACT.Identity,
                                                    scale=cvp[:, 2, i, j:j + 1], bias=cvp[:, 3, i, j:j + 1])
                    last.then_inc(tap_act, 1)

            def soft(j):
                act.wait_ge(max_done, j + 1)
                if j >= 3:
                    act.wait_ge(y_done, j - 2)
                b = j % 2
                nc.scalar.activation(pr[:, b, 0:P], pr[:, b, 0:P], ACT.Exp, bias=neg_max[:, b, 0:1],
                                     accum_out=rsum[:, j % 3, 0:1])
                nc.scalar.activation(pr[:, b, P:3 * P], pr[:, b, P:3 * P], ACT.Exp, bias=neg_max[:, b, 1:2],
                                     accum_out=rsum[:, j % 3, 1:2]).then_inc(exp_done, 1)

            def pt(j):
                act.wait_ge(pt_ready, j + 1)
                if j >= 2:
                    act.wait_ge(o_ready, j - 1)
                if j in (24, 25):
                    act.wait_ge(ro_ready, 4)
                nc.scalar.activation(ptb[:, j % 2, :], job[:, 2, 0:3 * P], ACT.Copy).then_inc(pt_copied, 1)

            def gelu(j):
                act.wait_ge(evac_dve, CH[BY[f"up{j}"]]["count"])
                nc.scalar.activation(gel[j % 2], conv[j % 2][:, 1, :], ACT.Gelu_apprx_tanh).then_inc(gelu_done, 1)

            def h_split(j):
                act.wait_ge(h_done, j + 1)
                nc.scalar.activation(S_hi[:, j, :], hh[j % 2], ACT.Copy).then_inc(h_hi, 1)

            for step in ORDER:
                if step[0] == "split_hi":
                    split(step[1])
                elif step[0] == "turn":
                    turn(step[1])
                elif step[0] == "evac":
                    evac(step[1])
                elif step[0] == "soft":
                    soft(step[1])
                elif step[0] == "pt":
                    pt(step[1])
                elif step[0] == "gelu":
                    gelu(step[1])
                elif step[0] == "h_split":
                    h_split(step[1])
                elif step[0] == "tables":
                    act.wait_ge(ang_done, 1)
                    for i, a in enumerate((cos_arg, sin_arg)):
                        nc.scalar.activation(tab64[:, i, :, :], a[:, :, 0:32], ACT.Sin)
                        last = nc.scalar.activation(tab256[:, i, :, :], a[:, :, 32:160], ACT.Sin)
                    last.then_inc(tab_done, 1)

        @block.vector
        def _(dve):
            chained = [0]

            def link(ins):
                chained[0] += 1
                ins.then_inc(dve_chain, 1)
                dve.wait_ge(dve_chain, chained[0])

            def split(u):
                n = piece_size(u)
                dve.wait_ge(hi_done, u + 1)
                if u >= RING:
                    dve.wait_ge(w_used, u - RING + 1)
                nc.vector.tensor_tensor(w_lo[:, u % RING, 0:n], raw[:, u % RAW, 0:n],
                                        w_hi[:, u % RING, 0:n].bitcast(F32), ALU.subtract).then_inc(lo_done, 1)

            def turn(n):
                if TJ[n]["split"]:
                    hi, lo, src = t_dest(n)
                    dve.wait_ge(t_hi, RANK[n] + 1)
                    nc.vector.tensor_tensor(lo, src, hi.bitcast(F32), ALU.subtract).then_inc(t_lo, 1)

            def rope(c):
                ch = CH[c]
                kind = ch["evac"][0]
                heads, d = (512 // ch["evac"][3], ch["evac"][3]) if kind == "rope" else (1, 64) if kind == "rms" else (4, 64)
                b0, half, r = ch["bank"], d // 2, ROT.index(c)
                tab = tab64 if d == 64 else tab256
                if r == 0:
                    dve.wait_ge(tab_done, 1)
                if ROT_READ[c] is not None and kind != "rms":
                    dve.wait_ge(t_ready, RANK[ROT_READ[c]] + 1)
                if r >= 1:
                    dve.wait_ge(rot_ready, NT * r)
                if kind == "mla_q":
                    dve.wait_ge(qn_copied, 1 + (ch["name"] == "mlaq1"))
                for tt in range(NT):
                    if kind == "rms":
                        x = ryb[:, tt, 256:320].rearrange("p (h e i) -> p h e i", h=1, e=2)
                        o = ryb[:, tt, 0:64].rearrange("p (h e i) -> p h e i", h=1, e=2)
                        w = ryb[:, tt, P:P + 64].rearrange("p (h e i) -> p h e i", h=1, e=2)
                    else:
                        x = acc[:, b0 + tt + (2 if kind == "mla_q" else 0), 0:heads * d].rearrange("p (h e i) -> p h e i", h=heads, e=2)
                        o = rot[:, tt, 0:heads * d].rearrange("p (h e i) -> p h e i", h=heads, e=2)
                        w = rtmp[:, tt, 0:heads * d].rearrange("p (h e i) -> p h e i", h=heads, e=2)
                    cos, sin = tab[:, 0, tt, :], tab[:, 1, tt, :]
                    nc.vector.tensor_tensor(o, x, cos.unsqueeze(1).unsqueeze(1).to_broadcast([P, heads, 2, half]), ALU.mult)
                    sb_ = sin.unsqueeze(1).to_broadcast([P, heads, half])
                    nc.vector.tensor_tensor(w[:, :, 0, :], x[:, :, 1, :], sb_, ALU.mult)
                    last = nc.vector.tensor_tensor(w[:, :, 1, :], x[:, :, 0, :], sb_, ALU.mult)
                    last.then_inc(kpe_prod if kind == "rms" else rot_prod if tt == 0 else evac_dve, 1)

            def evac(c):
                ch = CH[c]
                e, b0 = ch["evac"], ch["bank"]
                kind = e[0]
                if ch["who"] != "dve":
                    return
                if kind != "conv":
                    wait_acc(dve, c)
                    after_waits(dve, ch)
                if kind in ("rope", "mla_q"):
                    rope(c)
                elif kind == "gate":
                    dve.wait_ge(th_done, GATE.index(c) + 1)
                    nc.vector.scalar_tensor_tensor(gate[:, e[1], :, :], gate[:, e[1], :, :], 1.0, acc[:, b0:b0 + 2, :],
                                                   ALU.add, ALU.mult).then_inc(evac_dve, 1)
                elif kind == "norm":
                    norm_last(c)
                elif kind == "rms":
                    nc.vector.tensor_copy(rot[:, 1, :].rearrange("p (x n) -> p x n", x=2), acc[:, b0 + 2:b0 + 4, 0:256])
                    nc.vector.tensor_copy(ryb[:, 1, 256:320].rearrange("p (x n) -> p x n", x=2), acc[:, b0 + 2:b0 + 4, 256:288])\
                        .then_inc(evac_dve, 1)
                    dve.wait_ge(evac_dve, ch["count"])
                    dve.wait_ge(raw_copied, 1)
                    rope(c)
                    dve.wait_ge(sq_done, 1)
                    dve.wait_ge(rg_in, 16)
                    nc.vector.tensor_scalar(rstd_in[:, 0:4], ssq, 1.0 / 256, RMS_EPS, ALU.mult, ALU.add).then_inc(pow_in, 1)
                    dve.wait_ge(pow_done, POW.index(("rms",)) + 1)
                    for tt in range(NT):
                        for x in range(2):
                            v = slice(x * 256, (x + 1) * 256)
                            last = nc.vector.scalar_tensor_tensor(rot[:, tt, v], rot[:, tt, v],
                                                                  rstd[:, 2 * tt + x:2 * tt + x + 1], rgain[:, v],
                                                                  ALU.mult, ALU.mult)
                        last.then_inc(mn_ready, 1)
                elif kind == "forget":
                    dve.wait_ge(bf_in, 16)
                    nc.vector.tensor_scalar(fox[:, 0, :], acc[:, b0, 0:S], bforget, None, ALU.add).then_inc(z_ready, 1)
                    dve.wait_ge(z_ready, 1)
                    dve.wait_ge(ln_ready, 3)
                    link(nc.vector.scalar_tensor_tensor(fox[:, 2, :], fox[:, 0, :], 0.0, fox[:, 1, :], ALU.min, ALU.subtract))
                    dve.wait_ge(half_ready, 1)
                    link(nc.vector.tensor_tensor_scan(fox[:, 0, :], fox[:, 3, :], fox[:, 2, :], 0.0, ALU.mult, ALU.add))
                    dve.wait_ge(const_in, 16)
                    for g in range(2):
                        for o, name in ((cumA, "cumA"), (cumB, "cumB")):
                            k = const(name)
                            last = nc.vector.tensor_scalar(o[:, g, :], fox[:, 0, :], k[:, g:g + 1], k[:, 2 + g:3 + g],
                                                           ALU.mult, ALU.add)
                    last.then_inc(evac_dve, 1)
                elif kind == "conv":
                    j = e[1]
                    dve.wait_ge(tap_act, j + 1)
                    for lag in (1, 2):
                        for i in range(2):
                            o = conv[j % 2][:, i, lag:S]
                            last = nc.vector.scalar_tensor_tensor(o, acc[:, b0, i * S:i * S + S - lag],
                                                                  cvp[:, 2 - lag, i, j:j + 1], o, ALU.mult, ALU.add)
                        if lag == 1:
                            link(last)
                    last.then_inc(evac_dve, 1)

            def soft(j):
                jb = JOBS[j]
                b = j % 2
                dve.wait_ge(sc_ready, j + 1)
                if j >= 2:
                    dve.wait_ge(pt_ready, j - 1)
                sc = job[:, b, 0:3 * P]
                scale = SCALE_MLA if jb["kind"] == "mla" else SCALE_64
                if j == 0:
                    dve.wait_ge(const_in, 16)
                if j == 8:
                    dve.wait_ge(bias_in, 16)
                    band = const("band").unsqueeze(1).to_broadcast([P, 8, P])
                    link(nc.vector.tensor_tensor(bias[:, :, P:S], bias[:, :, P:S], band, ALU.add))
                if jb["kind"] == "band":
                    h = jb["h"]
                    nc.vector.scalar_tensor_tensor(pr[:, b, 0:P], sc[:, 0:P], scale, bias[:, h, P:S], ALU.mult, ALU.add)
                    link(nc.vector.scalar_tensor_tensor(pr[:, b, P:3 * P], sc[:, P:3 * P], scale, bias[:, h, :], ALU.mult, ALU.add))
                else:
                    link(nc.vector.scalar_tensor_tensor(pr[:, b, :], sc, scale, const("causal"), ALU.mult, ALU.add))
                nc.vector.tensor_reduce(neg_max[:, b, 0:1], pr[:, b, 0:P], AX_X, ALU.max, negate=True)
                nc.vector.tensor_reduce(neg_max[:, b, 1:2], pr[:, b, P:3 * P], AX_X, ALU.max, negate=True)\
                    .then_inc(max_done, 1)

            def pv(j):
                jb = JOBS[j]
                b, dv, h = j % 3, jb["dv"], jb["h"]
                per = P // dv
                gated = jb["kind"] in ("mla", "moba")
                dve.wait_ge(exp_done, j + 1)
                if j >= 1:
                    dve.wait_ge(y_done, j)
                if gated:
                    link(nc.vector.tensor_scalar(rdbl, rsum[:, b, :], 2.0, None, ALU.mult))
                link(nc.vector.reciprocal(rinv, rdbl if gated else rsum[:, b, :]))
                dve.wait_ge(o_ready, j + 1)
                slot = Y_SLOT[j]
                first = Y_BEFORE.get(j)
                if first is not None:
                    dve.wait_ge(t_ready, RANK[first] + 1)
                if gated:
                    wait_chunk_evac(dve, [n for n in jb["needs"] if n.startswith("mg")][0])
                for tt in range(NT):
                    o = yb[:, slot, tt, (j % per) * dv:(j % per + 1) * dv]
                    x = job[:, 3, tt * P:tt * P + dv]
                    if gated:
                        last = nc.vector.scalar_tensor_tensor(o, x, rinv[:, tt:tt + 1], gate[:, jb["s"], tt, h * dv:(h + 1) * dv],
                                                              ALU.mult, ALU.mult)
                    else:
                        last = nc.vector.tensor_scalar(o, x, rinv[:, tt:tt + 1], None, ALU.mult)
                last.then_inc(y_done, 1)

            def h_split(j):
                dve.wait_ge(h_hi, j + 1)
                nc.vector.tensor_tensor(S_lo[:, j, :], hh[j % 2], S_hi[:, j, :].bitcast(F32), ALU.subtract).then_inc(h_lo, 1)

            def tables():
                dve.wait_ge(pos_in, 16)
                link(nc.vector.tensor_copy(posf, posi[:]))
                freq = cst[:, CONST["inv64"][0]:CONST["inv256"][1]]
                for tt in range(NT):
                    last = nc.vector.tensor_scalar(ang[:, tt, :], freq, posf[:, tt:tt + 1], None, ALU.mult)
                link(last)
                link(nc.vector.tensor_scalar(turns, ang, 1.0 / TWO_PI, MAGIC, ALU.mult, ALU.add))
                link(nc.vector.tensor_scalar(turns, turns, MAGIC, None, ALU.subtract))
                for cc in (C1, C2, C3):
                    link(nc.vector.scalar_tensor_tensor(ang, turns, -cc, ang, ALU.mult, ALU.add))
                nc.vector.tensor_scalar(sin_arg, ang, PI_SAFE, -PI_SAFE, ALU.min, ALU.max)
                link(nc.vector.tensor_scalar(cos_arg, ang, PI_HALF, None, ALU.add))
                link(nc.vector.tensor_scalar(wrap, cos_arg, PI_SAFE, -TWO_PI, ALU.is_gt, ALU.mult))
                link(nc.vector.tensor_tensor(cos_arg, cos_arg, wrap, ALU.add))
                nc.vector.tensor_scalar(cos_arg, cos_arg, PI_SAFE, -PI_SAFE, ALU.min, ALU.max).then_inc(ang_done, 1)

            def norm_sum(c, tt, q):
                ch = CH[c]
                last = nc.vector.scalar_tensor_tensor(
                    res[:, tt, q * 512:(q + 1) * 512], res[:, tt, q * 512:(q + 1) * 512],
                    ALPHA1 if ch["evac"][1] < 2 else ALPHA2, acc[:, ch["bank"] + 2 * tt + q, :], ALU.mult, ALU.add)
                if (tt, q) == (1, 1):
                    last.then_inc(evac_dve, 1)
                    dve.wait_ge(evac_dve, ch["count"])
                else:
                    link(last)
                return nc.vector.bn_stats(stats[:, tt, q, :], res[:, tt, q * 512:(q + 1) * 512])

            def norm_variance(tt):
                link(nc.vector.bn_aggr(mv[:, tt, :], stats[:, tt, :, :]))
                nc.vector.tensor_scalar(rstd_in[:, tt:tt + 1], mv[:, tt, 1:2], LN_EPS, None, ALU.add).then_inc(pow_in, 1)

            def norm_first(c):
                dve.wait_ge(first_done, CH[c]["evac"][1] + 1)
                norm_sum(c, 0, 0)
                link(norm_sum(c, 0, 1))
                norm_variance(0)

            def norm_half(c):
                dve.wait_ge(half_done, CH[c]["evac"][1] + 1)
                link(norm_sum(c, 1, 0))

            def norm_last(c):
                link(norm_sum(c, 1, 1))
                norm_variance(1)

            def norm_rest(l, tt, q):
                v = slice(q * 512, (q + 1) * 512)
                dve.wait_ge(ln_g_in, 16 * (l + 1))
                link(nc.vector.scalar_tensor_tensor(res[:, tt, v], res[:, tt, v], mv[:, tt, 0:1], gb[:, 1, v],
                                                    ALU.subtract, ALU.mult))
                dve.wait_ge(ln_b_in, 16 * (l + 1))
                dve.wait_ge(pow_done, POW.index(("norm", l, tt)) + 1)
                nc.vector.scalar_tensor_tensor(res[:, tt, v], res[:, tt, v], rstd[:, tt:tt + 1], gb[:, 0, v],
                                               ALU.mult, ALU.add).then_inc(x_ready, 1)

            def ret_s(r):
                dve.wait_ge(rs_ready, r + 1)
                dve.wait_ge(o_ready, 24)
                if r >= 2:
                    dve.wait_ge(ro_ready, r - 1)
                if r == 0:
                    dve.wait_ge(even_in, 16)
                nc.vector.tensor_tensor(ptb[:, r % 2, 0:S], job[:, 0, 0:S], decay[:, r, :], ALU.mult)
                nc.vector.tensor_tensor(ptb[:, r % 2, S:S + P], job[:, 0, S:S + P], decay[:, r, 0:P], ALU.mult)\
                    .then_inc(rp_done, 1)

            def ret_o(r):
                dve.wait_ge(ro_ready, r + 1)
                for tt in range(NT):
                    last = nc.vector.bn_stats(stats[:, tt, 0, :], job[:, 1 + tt, :])
                link(last)
                for tt in range(NT):
                    last = nc.vector.bn_aggr(mv[:, tt, :], stats[:, tt, 0, :])
                link(last)
                nc.vector.tensor_scalar(rstd_in[:, 0:2], mv[:, :, 1], LN_EPS, 4.0, ALU.add, ALU.mult).then_inc(pow_in, 1)
                dve.wait_ge(pow_done, POW.index(("ret", r)) + 1)
                if r >= 1:
                    dve.wait_ge(t_ready, RANK[RET_TURN[r - 1]] + 1)
                for tt in range(NT):
                    last = nc.vector.tensor_scalar(ryb[:, tt, :], job[:, 1 + tt, :], mv[:, tt, 0:1], rstd[:, tt:tt + 1],
                                                   ALU.subtract, ALU.mult)
                link(last)
                wait_chunk_evac(dve, f"rg{r}")
                nc.vector.tensor_tensor(ryb[:, :, :], ryb[:, :, :], gate[:, 1 - r % 2, :, :], ALU.mult).then_inc(ry_done, 1)

            for step in ORDER:
                if step[0] == "split_lo":
                    split(step[1])
                elif step[0] == "turn":
                    turn(step[1])
                elif step[0] == "evac":
                    evac(step[1])
                elif step[0] == "soft":
                    soft(step[1])
                elif step[0] == "pv":
                    pv(step[1])
                elif step[0] == "h_split":
                    h_split(step[1])
                elif step[0] == "tables":
                    tables()
                elif step[0] == "norm_first":
                    norm_first(BY[("out1", "down", "out2", "out3")[step[1]]])
                elif step[0] == "norm_half":
                    norm_half(BY[("out1", "down", "out2", "out3")[step[1]]])
                elif step[0] == "norm_rest":
                    norm_rest(*step[1:])
                elif step[0] == "ret_s":
                    ret_s(step[1])
                elif step[0] == "ret_o":
                    ret_o(step[1])

        @block.gpsimd
        def _(pool):
            nc.gpsimd.memset(half_neg, -0.5).then_inc(pool_chain, 1)
            nc.gpsimd.memset(fox[:, 3, :], 1.0).then_inc(half_ready, 1)
            pool.wait_ge(pool_chain, 1)

            def power(key, a, b):
                i = POW.index(key)
                pool.wait_ge(pow_in, i + 1)
                nc.gpsimd.tensor_tensor(rstd[:, a:b], rstd_in[:, a:b], half_neg[:, 0:b - a], ALU.pow).then_inc(pow_done, 1)

            def rope(c):
                ch = CH[c]
                kind, r = ch["evac"][0], ROT.index(c)
                heads, d = (512 // ch["evac"][3], ch["evac"][3]) if kind == "rope" else (1, 64) if kind == "rms" else (4, 64)
                for tt in range(NT):
                    if kind == "rms":
                        pool.wait_ge(kpe_prod, tt + 1)
                    elif tt == 0:
                        pool.wait_ge(rot_prod, ROPES.index(c) + 1)
                    else:
                        pool.wait_ge(evac_dve, ch["count"])
                    if kind == "rms":
                        o = ryb[:, tt, 0:64].rearrange("p (h e i) -> p h e i", h=1, e=2)
                        w = ryb[:, tt, P:P + 64].rearrange("p (h e i) -> p h e i", h=1, e=2)
                        o2 = ryb[:, tt, 64:P].rearrange("p (h e i) -> p h e i", h=1, e=2)
                        nc.gpsimd.tensor_tensor(o2[:, :, 0, :], o[:, :, 0, :], w[:, :, 0, :], ALU.subtract)
                        nc.gpsimd.tensor_tensor(o2[:, :, 1, :], o[:, :, 1, :], w[:, :, 1, :], ALU.add)
                    else:
                        o = rot[:, tt, 0:heads * d].rearrange("p (h e i) -> p h e i", h=heads, e=2)
                        w = rtmp[:, tt, 0:heads * d].rearrange("p (h e i) -> p h e i", h=heads, e=2)
                    nc.gpsimd.tensor_tensor(o[:, :, 0, :], o[:, :, 0, :], w[:, :, 0, :], ALU.subtract)
                    nc.gpsimd.tensor_tensor(o[:, :, 1, :], o[:, :, 1, :], w[:, :, 1, :], ALU.add).then_inc(rot_ready, 1)

            for step in ORDER:
                if step[0] == "evac":
                    e = CH[step[1]]["evac"]
                    if e[0] == "norm":
                        power(("norm", e[1], 1), 1, 2)
                    elif e[0] == "rms":
                        rope(step[1])
                        power(("rms",), 0, 4)
                    elif e[0] in ("rope", "mla_q"):
                        rope(step[1])
                elif step[0] == "norm_first":
                    power(("norm", step[1], 0), 0, 1)
                elif step[0] == "ret_o":
                    power(("ret", step[1]), 0, 2)
                elif step[0] == "gelu":
                    j = step[1]
                    pool.wait_ge(gelu_done, j + 1)
                    if j >= 2:
                        pool.wait_ge(h_lo, j - 1)
                    nc.gpsimd.tensor_tensor(hh[j % 2], conv[j % 2][:, 0, :], gel[j % 2], ALU.mult).then_inc(h_done, 1)
                elif step[0] == "load" and step[1] == "ln":
                    l = step[2]
                    pool.wait_ge(*((max_done, 16), (x_ready, 2 * NT), (ry_done, 3), (y_done, 32))[l])
                    pool.dma_start(gb[:, 1, :], t["ln_gain"][l].partition_broadcast(P)).then_inc(ln_g_in, 16)
                    pool.wait_ge(*((max_done, 16), (x_ready, 2 * NT), (ry_done, 4), (y_done, 40))[l])
                    pool.dma_start(gb[:, 0, :], t["ln_bias"][l].partition_broadcast(P)).then_inc(ln_b_in, 16)
                elif step == ("load", "even"):
                    pool.wait_ge(y_done, 16)
                    pool.dma_start(rgain, t["rms_gain"].partition_broadcast(P)).then_inc(rg_in, 16)


def lay_out(inputs):
    a = {k: np.asarray(v) for k, v in inputs.items()}
    w = np.zeros((NU, P, PIECE), np.float32)
    forget = np.zeros((D, P), np.float32)
    b_forget = np.zeros((P, 1), np.float32)
    for h in range(8):
        for r in (0, 1):
            at = 32 * (h % 4) + 2 * (h // 4) + r
            forget[:, at] = a["w_in"][0][:, FA + h]
            b_forget[at, 0] = a["b_forget"][0][h]
    for u, (c, i) in enumerate(PIECES):
        ch = CH[c]
        name, rows, cols = ch["pick"]
        key = name if name in ("w_in", "w_out", "w_up", "w_down") else name + "_2"
        m = forget if ch["name"] == "f" else a[key][0]
        m = m if cols is None else m[:, cols]
        m = m.reshape(m.shape[0] // P, P, -1)
        if rows is not None:
            m = m[rows]
        kind = ch["kind"]
        if kind == "F":
            block = m[:, :, i * P:(i + 1) * P]
        elif kind == "A":
            block = m[2 * i:2 * i + 2]
        elif kind in ("B", "C"):
            block = m[i:i + 1]
        else:
            block = m[:, :, 0:512] if i == 0 else m[:, :, 512:]
        block = block.transpose(1, 0, 2).reshape(P, -1)
        assert block.shape[1] == piece_size(u)
        w[u, :, 0:block.shape[1]] = block
    at = np.minimum(P + np.arange(P)[:, None] - np.arange(S)[None, :], 128) + 128
    cw = np.concatenate([a["conv_w"][0], a["conv_b"]], 0)
    return {
        "w": w,
        "const": constants(),
        "decay": decay_table(),
        "x": a["x"],
        "b_forget": b_forget,
        "bias": a["rel_bias"][0][:, at].transpose(1, 0, 2),
        "conv": cw.reshape(4, 2, FT, P).transpose(3, 0, 1, 2),
        "positions_2": a["positions_2"].reshape(NT, P).T,
        "rms_gain": np.concatenate([a["q_norm_even_2"][0], a["kv_norm_even_2"][0]]),
        "ln_gain": np.stack([a["ln1_g"][0], a["ln2_g"][0], a["ln_g_2"][0], a["ln_g_2"][1]]),
        "ln_bias": np.stack([a["ln1_b"][0], a["ln2_b"][0], a["ln_b_2"][0], a["ln_b_2"][1]]),
    }


def kernel(**inputs):
    import concourse.bacc as _bacc
    from concourse.bass_utils import run_bass_kernel_spmd as _run

    nc = _bacc.Bacc("TRN2", target_bir_lowering=False, num_devices=1)
    arrays, t = {}, {}
    for name, a in lay_out(inputs).items():
        a = np.ascontiguousarray(a)
        arrays[f"in_{name}"] = a
        t[name] = nc.dram_tensor(f"in_{name}", a.shape, mybir.dt.from_np(a.dtype), kind="ExternalInput").ap()
    t["out"] = nc.dram_tensor("out_0", (1, S, D), F32, kind="ExternalOutput").ap()
    build(nc, t)
    r = _run(nc, [arrays], core_ids=[0])
    return r.results[0]["out_0"]
```
